# Optimizing a Trainium2 kernel written in Bass

```python
import jax
import jax.numpy as jnp
from jax import lax
import numpy as np
import jax, jax.numpy as jnp

D_MODEL = 1024
BATCH = 1
SEQ = 512
DEPTH = 2

CTX_LEN = 256
GRID_W = 64
BLOCK = 128
WINDOW = 128
ROPE_BASE = 10000.0
EPS = 1e-6
NEG_INF = -1e30

H_A = 8
HKV_A = 2
G_A = H_A // HKV_A
HD_A = 64
SCALE_A = HD_A ** -0.5

H_B = 8
Q_LORA = 384
KV_LORA = 256
NOPE_B = 64
ROPE_B = 32
V_B = 64
SCALE_B = (NOPE_B + ROPE_B) ** -0.5

W_C = 512
CONV_K = 3

W_BRANCH = 512

IN_SIZES = (H_A * HD_A, HKV_A * HD_A, HKV_A * HD_A, W_BRANCH,
            Q_LORA, KV_LORA, ROPE_B, W_BRANCH,
            W_C, W_C, W_C, W_BRANCH,
            D_MODEL, D_MODEL, D_MODEL)
D_IN = sum(IN_SIZES)


def rms_norm(x, g):
    xf = x.astype(jnp.float32)
    y = xf * lax.rsqrt(jnp.mean(xf * xf, axis=-1, keepdims=True) + EPS)
    return (y * g.astype(jnp.float32)).astype(x.dtype)

def axial_rope_angles(rows, rot_dim):
    row = jnp.repeat(jnp.arange(rows, dtype=jnp.float32), GRID_W)
    col = jnp.tile(jnp.arange(GRID_W, dtype=jnp.float32), rows)
    axis_dim = rot_dim // 2
    inv = ROPE_BASE ** (-jnp.arange(0, axis_dim, 2, dtype=jnp.float32) / axis_dim)
    ang = jnp.concatenate([row[:, None] * inv, col[:, None] * inv], axis=-1)
    return jnp.cos(ang), jnp.sin(ang)

def apply_rope(x, cos, sin):
    xf = x.astype(jnp.float32)
    x1, x2 = jnp.split(xf, 2, axis=-1)
    c = cos[None, :, None, :]
    s = sin[None, :, None, :]
    return jnp.concatenate([x1 * c - x2 * s, x2 * c + x1 * s], axis=-1).astype(x.dtype)

def in_proj(h, w_in):
    splits = np.cumsum(IN_SIZES)[:-1].tolist()
    return jnp.split(h @ w_in, splits, axis=-1)

def window_attn_latent(q, k, v, k_ctx, v_ctx, sink):
    B, S = q.shape[:2]
    nb = S // BLOCK
    qb = q.reshape(B, nb, BLOCK, HKV_A, G_A, HD_A)
    pad = ((0, 0), (BLOCK, BLOCK), (0, 0), (0, 0))
    kp = jnp.pad(k, pad).reshape(B, nb + 2, BLOCK, HKV_A, HD_A)
    vp = jnp.pad(v, pad).reshape(B, nb + 2, BLOCK, HKV_A, HD_A)
    kw = jnp.concatenate([kp[:, :-2], kp[:, 1:-1], kp[:, 2:]], axis=2)
    vw = jnp.concatenate([vp[:, :-2], vp[:, 1:-1], vp[:, 2:]], axis=2)
    s_loc = jnp.einsum('bnqhgd,bnkhd->bnhgqk', qb, kw).astype(jnp.float32) * SCALE_A
    qi = jnp.arange(BLOCK)[:, None] + BLOCK
    kj = jnp.arange(3 * BLOCK)[None, :]
    band = jnp.abs(kj - qi) <= WINDOW
    kabs = jnp.arange(nb)[:, None] * BLOCK + jnp.arange(3 * BLOCK)[None, :] - BLOCK
    valid = (kabs >= 0) & (kabs < S)
    mask = band[None, :, :] & valid[:, None, :]
    s_loc = jnp.where(mask[None, :, None, None], s_loc, NEG_INF)
    s_ctx = jnp.einsum('bnqhgd,blhd->bnhgql', qb, k_ctx).astype(jnp.float32) * SCALE_A
    s_sink = jnp.broadcast_to(sink.astype(jnp.float32).reshape(1, 1, HKV_A, G_A, 1, 1),
                              s_loc.shape[:-1] + (1,))
    p = jax.nn.softmax(jnp.concatenate([s_loc, s_ctx, s_sink], axis=-1), axis=-1)
    p_loc = p[..., :3 * BLOCK].astype(v.dtype)
    p_ctx = p[..., 3 * BLOCK:3 * BLOCK + k_ctx.shape[1]].astype(v.dtype)
    o = (jnp.einsum('bnhgqk,bnkhd->bnqhgd', p_loc, vw)
         + jnp.einsum('bnhgql,blhd->bnqhgd', p_ctx, v_ctx))
    return o.reshape(B, S, H_A * HD_A)

def ctx_gqa_attn(q, k, v, sink):
    B, L = q.shape[:2]
    qg = q.reshape(B, L, HKV_A, G_A, HD_A)
    s = jnp.einsum('blhgd,bmhd->bhglm', qg, k).astype(jnp.float32) * SCALE_A
    sk = jnp.broadcast_to(sink.astype(jnp.float32).reshape(1, HKV_A, G_A, 1, 1), (B, HKV_A, G_A, L, 1))
    p = jax.nn.softmax(jnp.concatenate([s, sk], axis=-1), axis=-1)[..., :L]
    o = jnp.einsum('bhglm,bmhd->blhgd', p.astype(v.dtype), v)
    return o.reshape(B, L, H_A * HD_A)

def mla_project(q_lat, kv_lat, g_qa, w_qb, g_kva, w_kvb):
    B, T = q_lat.shape[:2]
    q = (rms_norm(q_lat, g_qa) @ w_qb).reshape(B, T, H_B, NOPE_B + ROPE_B)
    kv = (rms_norm(kv_lat, g_kva) @ w_kvb).reshape(B, T, H_B, NOPE_B + V_B)
    return q[..., :NOPE_B], q[..., NOPE_B:], kv[..., :NOPE_B], kv[..., NOPE_B:]

def mla_attn_latent(qn, qr, kn, kr, v, kn_c, kr_c, v_c):
    B, S = qn.shape[:2]
    nb = S // BLOCK
    keys_n = jnp.concatenate([kn, kn_c], axis=1)
    keys_r = jnp.concatenate([kr, kr_c], axis=1)
    vals = jnp.concatenate([v, v_c], axis=1)

    def block(qs):
        q_n, q_r = qs
        s = (jnp.einsum('bqhd,bkhd->bhqk', q_n, keys_n)
             + jnp.einsum('bqhd,bkd->bhqk', q_r, keys_r))
        p = jax.nn.softmax(s.astype(jnp.float32) * SCALE_B, axis=-1)
        return jnp.einsum('bhqk,bkhd->bqhd', p.astype(vals.dtype), vals)

    qn_b = qn.reshape(B, nb, BLOCK, H_B, NOPE_B).swapaxes(0, 1)
    qr_b = qr.reshape(B, nb, BLOCK, H_B, ROPE_B).swapaxes(0, 1)
    o = lax.map(block, (qn_b, qr_b))
    return o.swapaxes(0, 1).reshape(B, S, H_B * V_B)

def ctx_mla_attn(qn, qr, kn, kr, v):
    B, L = qn.shape[:2]
    s = jnp.einsum('blhd,bmhd->bhlm', qn, kn) + jnp.einsum('blhd,bmd->bhlm', qr, kr)
    p = jax.nn.softmax(s.astype(jnp.float32) * SCALE_B, axis=-1)
    o = jnp.einsum('bhlm,bmhd->blhd', p.astype(v.dtype), v)
    return o.reshape(B, L, H_B * V_B)

def short_gated_conv(b_gate, c_gate, u, conv_w):
    z = jnp.pad(c_gate * u, ((0, 0), (1, 1), (0, 0)))
    y = conv_w[0] * z[:, :-2] + conv_w[1] * z[:, 1:-1] + conv_w[2] * z[:, 2:]
    return b_gate * y

def merge_branches(ya, yb, yc, za, zb, zc, ga, gb, gc, w_branch, w_o):
    m = (jax.nn.sigmoid(ga) * ((ya * jax.nn.silu(za)) @ w_branch[0])
         + jax.nn.sigmoid(gb) * ((yb * jax.nn.silu(zb)) @ w_branch[1])
         + jax.nn.sigmoid(gc) * ((yc * jax.nn.silu(zc)) @ w_branch[2]))
    return m @ w_o

def mixer_layer(x, ctx, mod_x, mod_c, rope_a, rope_b, g_pre, g_post, w_in, sink,
                g_qa, w_qb, g_kva, w_kvb, conv_w, w_branch, w_o, update_ctx):
    B, S, _ = x.shape
    L = ctx.shape[1]
    shift_x, scale_x, gate_x = [m[:, None, :] for m in jnp.split(mod_x, 3, axis=-1)]
    shift_c, scale_c, gate_c = jnp.split(mod_c, 3, axis=-1)
    hx = rms_norm(x, g_pre) * (1.0 + scale_x) + shift_x
    hc = rms_norm(ctx, g_pre) * (1.0 + scale_c) + shift_c
    (qa_x, ka_x, va_x, za_x, qlb_x, kvlb_x, krb_x, zb_x,
     bc_x, cc_x, uc_x, zc_x, ga_x, gb_x, gc_x) = in_proj(hx, w_in)
    (qa_c, ka_c, va_c, za_c, qlb_c, kvlb_c, krb_c, zb_c,
     bc_c, cc_c, uc_c, zc_c, ga_c, gb_c, gc_c) = in_proj(hc, w_in)

    cos_a, sin_a = rope_a
    qa = apply_rope(qa_x.reshape(B, S, H_A, HD_A), cos_a, sin_a)
    ka = apply_rope(ka_x.reshape(B, S, HKV_A, HD_A), cos_a, sin_a)
    va = va_x.reshape(B, S, HKV_A, HD_A)
    kac = ka_c.reshape(B, L, HKV_A, HD_A)
    vac = va_c.reshape(B, L, HKV_A, HD_A)
    ya_x = window_attn_latent(qa, ka, va, kac, vac, sink)

    cos_b, sin_b = rope_b
    qn_x, qr_x, kn_x, vb_x = mla_project(qlb_x, kvlb_x, g_qa, w_qb, g_kva, w_kvb)
    qr_x = apply_rope(qr_x, cos_b, sin_b)
    kr_x = apply_rope(krb_x[:, :, None, :], cos_b, sin_b)[:, :, 0]
    qn_c, qr_c, kn_c, vb_c = mla_project(qlb_c, kvlb_c, g_qa, w_qb, g_kva, w_kvb)
    yb_x = mla_attn_latent(qn_x, qr_x, kn_x, kr_x, vb_x, kn_c, krb_c, vb_c)

    yc_x = short_gated_conv(bc_x, cc_x, uc_x, conv_w)

    out_x = merge_branches(ya_x, yb_x, yc_x, za_x, zb_x, zc_x, ga_x, gb_x, gc_x, w_branch, w_o)
    x = x + gate_x * rms_norm(out_x, g_post)

    if update_ctx:
        ya_c = ctx_gqa_attn(qa_c.reshape(B, L, H_A, HD_A), kac, vac, sink)
        yb_c = ctx_mla_attn(qn_c, qr_c, kn_c, krb_c, vb_c)
        yc_c = short_gated_conv(bc_c, cc_c, uc_c, conv_w)
        out_c = merge_branches(ya_c, yb_c, yc_c, za_c, zb_c, zc_c, ga_c, gb_c, gc_c, w_branch, w_o)
        ctx = ctx + gate_c * rms_norm(out_c, g_post)
    return x, ctx

def first_inputs(seed: int = 0) -> dict:
    key = jax.random.key(seed)
    ks = jax.random.split(key, 17)
    f32 = jnp.float32

    def nrm(k, shape, scale):
        return jax.random.normal(k, shape, f32) * scale

    return {
        "x": nrm(ks[0], (BATCH, SEQ, D_MODEL), 1.0),
        "c": nrm(ks[1], (BATCH, D_MODEL), 1.0),
        "ctx": nrm(ks[2], (BATCH, CTX_LEN, D_MODEL), 1.0),
        "c_ctx": nrm(ks[3], (D_MODEL,), 1.0),
        "w_mod": nrm(ks[4], (DEPTH, D_MODEL, 3 * D_MODEL), 0.5 * D_MODEL ** -0.5),
        "b_mod": nrm(ks[5], (DEPTH, 3 * D_MODEL), 0.01),
        "g_pre": 1.0 + nrm(ks[6], (DEPTH, D_MODEL), 0.05),
        "g_post": 1.0 + nrm(ks[7], (DEPTH, D_MODEL), 0.05),
        "w_in": nrm(ks[8], (DEPTH, D_MODEL, D_IN), D_MODEL ** -0.5),
        "sink": nrm(ks[9], (DEPTH, H_A), 1.0),
        "g_qa": 1.0 + nrm(ks[10], (DEPTH, Q_LORA), 0.05),
        "w_qb": nrm(ks[11], (DEPTH, Q_LORA, H_B * (NOPE_B + ROPE_B)), Q_LORA ** -0.5),
        "g_kva": 1.0 + nrm(ks[12], (DEPTH, KV_LORA), 0.05),
        "w_kvb": nrm(ks[13], (DEPTH, KV_LORA, H_B * (NOPE_B + V_B)), KV_LORA ** -0.5),
        "conv_w": nrm(ks[14], (DEPTH, CONV_K, W_C), CONV_K ** -0.5),
        "w_branch": nrm(ks[15], (DEPTH, 3, W_BRANCH, D_MODEL), W_BRANCH ** -0.5),
        "w_o": nrm(ks[16], (DEPTH, D_MODEL, D_MODEL), D_MODEL ** -0.5),
    }

def first_block(x, c, ctx, c_ctx, w_mod, b_mod, g_pre, g_post, w_in, sink,
              g_qa, w_qb, g_kva, w_kvb, conv_w, w_branch, w_o):
    rows = x.shape[1] // GRID_W
    rope_a = axial_rope_angles(rows, HD_A)
    rope_b = axial_rope_angles(rows, ROPE_B)
    sc = jax.nn.silu(c)
    scc = jax.nn.silu(c_ctx)
    for i in range(DEPTH):
        mod_x = sc @ w_mod[i] + b_mod[i]
        mod_c = scc @ w_mod[i] + b_mod[i]
        x, ctx = mixer_layer(x, ctx, mod_x, mod_c, rope_a, rope_b, g_pre[i], g_post[i],
                             w_in[i], sink[i], g_qa[i], w_qb[i], g_kva[i], w_kvb[i],
                             conv_w[i], w_branch[i], w_o[i], update_ctx=(i < DEPTH - 1))
    return x


HEAD_DIM = 64
Q_BLOCK = 128
NEG_BIG = -1e30
F_MIN = 1e-6
A_HEADS = 6
A_KV_HEADS = 2
ROPE_THETA = 10000.0
B_HEADS = 4
B_KEY_DIM = 64
B_CHUNK = 64
C_HEADS = 6
C_KV_HEADS = 2
C_BRANCHES = ((128, 1), (512, 4), (2048, 16))
D_FF = 2816
CONV_W = 3

A_W = A_HEADS * HEAD_DIM
B_W = B_HEADS * HEAD_DIM
B_K = B_HEADS * B_KEY_DIM
C_W = C_HEADS * HEAD_DIM
MIX_W = A_W + B_W + C_W
SPLITS = (A_W, A_KV_HEADS * HEAD_DIM, A_KV_HEADS * HEAD_DIM,
          B_K, B_K, B_K, B_W, B_W,
          C_W, C_KV_HEADS * HEAD_DIM, C_KV_HEADS * HEAD_DIM)
IN_W = sum(SPLITS)


def rms_norm_2(x, g):
    xf = x.astype(jnp.float32)
    y = xf * lax.rsqrt(jnp.mean(xf * xf, axis=-1, keepdims=True) + EPS)
    return (y * g.astype(jnp.float32)).astype(x.dtype)

def _rope_half(x, cos, sin):
    h = x.shape[-1] // 2
    x1, x2 = x[..., :h], x[..., h:]
    return jnp.concatenate([x1 * cos - x2 * sin, x2 * cos + x1 * sin], axis=-1)

def axial_rope(x):
    S = x.shape[1]
    n_rows = S // GRID_W
    row = jnp.repeat(jnp.arange(n_rows), GRID_W).astype(jnp.float32)
    col = jnp.tile(jnp.arange(GRID_W), n_rows).astype(jnp.float32)
    half = HEAD_DIM // 2
    inv = ROPE_THETA ** (-jnp.arange(0, half, 2, dtype=jnp.float32) / half)
    ang_r = (row[:, None] * inv)[:, None, :]
    ang_c = (col[:, None] * inv)[:, None, :]
    xf = x.astype(jnp.float32)
    xr = _rope_half(xf[..., :half], jnp.cos(ang_r), jnp.sin(ang_r))
    xc = _rope_half(xf[..., half:], jnp.cos(ang_c), jnp.sin(ang_c))
    return jnp.concatenate([xr, xc], axis=-1).astype(x.dtype)

def _to_query_blocks(q, n_kv):
    B_, S, H, D = q.shape
    nb = S // Q_BLOCK
    return q.reshape(B_, nb, Q_BLOCK, n_kv, H // n_kv, D).transpose(1, 0, 3, 4, 2, 5)

def _from_query_blocks(o):
    nb, B_, hk, g, qb, d = o.shape
    return o.transpose(1, 0, 4, 2, 3, 5).reshape(B_, nb * qb, hk * g * d)

def mixer_a(q, k, v, gq, gk):
    q = axial_rope(rms_norm_2(q, gq))
    k = axial_rope(rms_norm_2(k, gk))
    qb = _to_query_blocks(q, A_KV_HEADS)
    kt = k.transpose(0, 2, 1, 3)
    vt = v.transpose(0, 2, 1, 3)
    scale = HEAD_DIM ** -0.5

    def block(qi):
        s = jnp.einsum('bhgqd,bhkd->bhgqk', qi, kt).astype(jnp.float32) * scale
        p = jax.nn.softmax(s, axis=-1).astype(vt.dtype)
        return jnp.einsum('bhgqk,bhkd->bhgqd', p, vt)

    return _from_query_blocks(lax.map(block, qb))

def mixer_c(q, k, v, gq, gk):
    S = q.shape[1]
    q = rms_norm_2(q, gq)
    k = rms_norm_2(k, gk)
    qb = _to_query_blocks(q, C_KV_HEADS)
    kt = k.transpose(0, 2, 1, 3)
    vt = v.transpose(0, 2, 1, 3)
    nb = S // Q_BLOCK
    starts = jnp.arange(nb) * Q_BLOCK
    scale = HEAD_DIM ** -0.5
    slopes = (2.0 ** (-8.0 * np.arange(1, C_HEADS + 1) / C_HEADS)).astype(np.float32)
    slopes = jnp.asarray(slopes).reshape(C_KV_HEADS, C_HEADS // C_KV_HEADS, 1, 1)
    offsets = [r * np.arange(-(w // (2 * r)), w // (2 * r) + 1) for (w, r) in C_BRANCHES]

    def block(args):
        qi, t0 = args
        t = t0 + jnp.arange(Q_BLOCK)
        lses, outs = [], []
        for off in offsets:
            idx = t[:, None] + jnp.asarray(off)[None, :]
            valid = (idx >= 0) & (idx < S)
            idx = jnp.clip(idx, 0, S - 1)
            kg = kt[:, :, idx, :]
            vg = vt[:, :, idx, :]
            dist = jnp.asarray(np.abs(off).astype(np.float32))
            s = jnp.einsum('bhgqd,bhqkd->bhgqk', qi, kg).astype(jnp.float32) * scale - slopes * dist
            s = jnp.where(valid, s, NEG_BIG)
            lse = jax.nn.logsumexp(s, axis=-1)
            p = jnp.exp(s - lse[..., None]).astype(vg.dtype)
            outs.append(jnp.einsum('bhgqk,bhqkd->bhgqd', p, vg).astype(jnp.float32))
            lses.append(lse)
        w = jax.nn.softmax(jnp.stack(lses, axis=0), axis=0)
        o = jnp.einsum('nbhgq,nbhgqd->bhgqd', w, jnp.stack(outs, axis=0))
        return o.astype(qi.dtype)

    return _from_query_blocks(lax.map(block, (qb, starts)))

def hgrn2_scan(q, k, v, logf):
    B_, S, H, dk = q.shape
    dv = v.shape[-1]
    nc = S // B_CHUNK

    def to_chunks(a):
        return a.astype(jnp.float32).reshape(B_, nc, B_CHUNK, H, a.shape[-1]).transpose(1, 0, 3, 2, 4)

    qc, kc, vc, lc = to_chunks(q), to_chunks(k), to_chunks(v), to_chunks(logf)
    mask = jnp.tril(jnp.ones((B_CHUNK, B_CHUNK), dtype=bool))[:, :, None]

    def step(state, inp):
        q_, k_, v_, l_ = inp
        b = jnp.cumsum(l_, axis=2)
        o_inter = jnp.einsum('bhtk,bhkv->bhtv', q_ * jnp.exp(b), state)
        diff = b[:, :, :, None, :] - b[:, :, None, :, :]
        dec = jnp.where(mask, jnp.exp(jnp.where(mask, diff, 0.0)), 0.0)
        attn = jnp.einsum('bhtk,bhsk,bhtsk->bhts', q_, k_, dec)
        o_intra = jnp.einsum('bhts,bhsv->bhtv', attn, v_)
        b_last = b[:, :, -1:, :]
        new_state = jnp.exp(b_last[:, :, 0, :])[..., None] * state + \
            jnp.einsum('bhsk,bhsv->bhkv', k_ * jnp.exp(b_last - b), v_)
        return new_state, o_inter + o_intra

    state0 = jnp.zeros((B_, H, dk, dv), jnp.float32)
    _, o = lax.scan(step, state0, (qc, kc, vc, lc))
    return o.transpose(1, 0, 3, 2, 4).reshape(B_, S, H, dv).astype(v.dtype)

def mixer_b(q, f_fwd, f_bwd, i, g, lb_fwd, lb_bwd, g_norm):
    def log_forget(fpre, lb):
        lb = lb.reshape(B_HEADS, B_KEY_DIM)
        f = lb + (1.0 - lb) * jax.nn.sigmoid(fpre.astype(jnp.float32))
        return jnp.log(jnp.maximum(f, F_MIN))

    lff = log_forget(f_fwd, lb_fwd)
    lfb = log_forget(f_bwd, lb_bwd)
    o_f = hgrn2_scan(q, -jnp.expm1(lff), i, lff)
    flip = lambda a: jnp.flip(a, axis=1)
    o_b = flip(hgrn2_scan(flip(q), flip(-jnp.expm1(lfb)), flip(i), flip(lfb)))
    o = rms_norm_2(o_f + o_b, g_norm) * jax.nn.silu(g)
    return o.reshape(o.shape[0], o.shape[1], B_W)

def conv_ffn(h, w_up, conv_w, conv_b, w_down):
    u = h @ w_up
    up = jnp.pad(u, ((0, 0), (1, 1), (0, 0)))
    u = conv_w[0] * up[:, :-2] + conv_w[1] * up[:, 1:-1] + conv_w[2] * up[:, 2:] + conv_b
    a, b = jnp.split(u, 2, axis=-1)
    return (jax.nn.silu(a) * b) @ w_down

def second_inputs(seed: int = 0) -> dict:
    key = jax.random.key(seed)
    ks = jax.random.split(key, 20)
    nrm = lambda k, shape, s: jax.random.normal(k, shape, jnp.float32) * s
    return {
        "x": nrm(ks[0], (BATCH, SEQ, D_MODEL), 1.0),
        "c": nrm(ks[1], (BATCH, D_MODEL), 1.0),
        "w_ada": nrm(ks[2], (DEPTH, D_MODEL, 6 * D_MODEL), D_MODEL ** -0.5),
        "b_ada": nrm(ks[3], (DEPTH, 6 * D_MODEL), 0.01),
        "norm_g": 1.0 + nrm(ks[4], (DEPTH, 2, D_MODEL), 0.01),
        "w_in": nrm(ks[5], (DEPTH, D_MODEL, IN_W), D_MODEL ** -0.5),
        "a_q_norm": 1.0 + nrm(ks[6], (DEPTH, HEAD_DIM), 0.01),
        "a_k_norm": 1.0 + nrm(ks[7], (DEPTH, HEAD_DIM), 0.01),
        "b_lb": nrm(ks[8], (2, DEPTH, B_K), 0.5),
        "b_out_norm": 1.0 + nrm(ks[9], (DEPTH, HEAD_DIM), 0.01),
        "c_q_norm": 1.0 + nrm(ks[10], (DEPTH, HEAD_DIM), 0.01),
        "c_k_norm": 1.0 + nrm(ks[11], (DEPTH, HEAD_DIM), 0.01),
        "w_out": nrm(ks[12], (DEPTH, MIX_W, D_MODEL), MIX_W ** -0.5),
        "w_up": nrm(ks[13], (DEPTH, D_MODEL, 2 * D_FF), D_MODEL ** -0.5),
        "conv_w": nrm(ks[14], (DEPTH, CONV_W, 2 * D_FF), CONV_W ** -0.5),
        "conv_b": nrm(ks[15], (DEPTH, 2 * D_FF), 0.01),
        "w_down": nrm(ks[16], (DEPTH, D_FF, D_MODEL), D_FF ** -0.5),
    }

def second_block(x, c, w_ada, b_ada, norm_g, w_in, a_q_norm, a_k_norm, b_lb, b_out_norm,
              c_q_norm, c_k_norm, w_out, w_up, conv_w, conv_b, w_down):
    B_, S, _ = x.shape
    sm = jax.nn.softmax(b_lb.astype(jnp.float32), axis=1)
    lb_all = jnp.cumsum(sm, axis=1) - sm[:, :1]
    split_idx = np.cumsum(SPLITS)[:-1].tolist()
    for l in range(DEPTH):
        mod = jax.nn.silu(c) @ w_ada[l] + b_ada[l]
        sh1, sc1, g1, sh2, sc2, g2 = jnp.split(mod[:, None, :], 6, axis=-1)
        h = rms_norm_2(x, norm_g[l, 0]) * (1.0 + sc1) + sh1
        parts = jnp.split(h @ w_in[l], split_idx, axis=-1)
        hd = lambda a, n: a.reshape(B_, S, n, a.shape[-1] // n)
        aq, ak, av, bq, bff, bfb, bi, bg, cq, ck, cv = parts
        o_a = mixer_a(hd(aq, A_HEADS), hd(ak, A_KV_HEADS), hd(av, A_KV_HEADS), a_q_norm[l], a_k_norm[l])
        o_b = mixer_b(hd(bq, B_HEADS), hd(bff, B_HEADS), hd(bfb, B_HEADS), hd(bi, B_HEADS), hd(bg, B_HEADS),
                      lb_all[0, l], lb_all[1, l], b_out_norm[l])
        o_c = mixer_c(hd(cq, C_HEADS), hd(ck, C_KV_HEADS), hd(cv, C_KV_HEADS), c_q_norm[l], c_k_norm[l])
        mix = jnp.concatenate([o_a, o_b, o_c], axis=-1) @ w_out[l]
        x = x + g1 * mix
        h = rms_norm_2(x, norm_g[l, 1]) * (1.0 + sc2) + sh2
        x = x + g2 * conv_ffn(h, w_up[l], conv_w[l], conv_b[l], w_down[l])
    return x


def setup_inputs(seed=0):
    out = dict(first_inputs(seed))
    for name, value in second_inputs(seed + 1).items():
        if name != "x":
            out[name + "_2"] = value
    return out


def reference(
    x, c, ctx, c_ctx, w_mod, b_mod, g_pre, g_post, w_in, sink, g_qa, w_qb, g_kva, w_kvb, conv_w,
    w_branch, w_o, c_2, w_ada_2, b_ada_2, norm_g_2, w_in_2, a_q_norm_2, a_k_norm_2, b_lb_2,
    b_out_norm_2, c_q_norm_2, c_k_norm_2, w_out_2, w_up_2, conv_w_2, conv_b_2, w_down_2,
):
    x = first_block(
        x, c, ctx, c_ctx, w_mod, b_mod, g_pre, g_post, w_in, sink, g_qa, w_qb, g_kva, w_kvb,
        conv_w, w_branch, w_o,
    )
    return second_block(
        x, c_2, w_ada_2, b_ada_2, norm_g_2, w_in_2, a_q_norm_2, a_k_norm_2, b_lb_2,
        b_out_norm_2, c_q_norm_2, c_k_norm_2, w_out_2, w_up_2, conv_w_2, conv_b_2, w_down_2,
    )


_drawn_inputs = setup_inputs


def setup_inputs(seed=0):
    import zlib

    import numpy as np

    out = dict(_drawn_inputs(seed))
    spreads = {}
    factors = {'sink': 8.0,
     'g_qa': 8.0,
     'g_kva': 8.0,
     'b_ada_2': 2.681,
     'norm_g_2': 4.975,
     'a_q_norm_2': 8.0,
     'a_k_norm_2': 8.0,
     'b_out_norm_2': 8.0,
     'c_q_norm_2': 8.0,
     'c_k_norm_2': 8.0,
     'conv_b_2': 7.842}
    for name, (base, spread) in spreads.items():
        noise = np.random.default_rng([zlib.crc32(name.encode()), seed]).standard_normal(out[name].shape)
        drawn = base * np.exp(spread * noise) if base else spread * noise
        out[name] = jnp.asarray(drawn.astype(out[name].dtype))
    for name, factor in factors.items():
        out[name] = (out[name] * factor).astype(out[name].dtype)
    return out
```

```python
import numpy as np
import concourse.bass as bass
from concourse import mybir
from contextlib import ExitStack

F32 = mybir.dt.float32
F32R = mybir.dt.float32r
I32 = mybir.dt.int32
ALU = mybir.AluOpType
ACT = mybir.ActivationFunctionType
AX = mybir.AxisListType

P = 128
DM = 1024
KD = DM // P
SEQ = 512
CTX = 256
NT = SEQ + CTX
NXB = SEQ // P
NTB = NT // P
DEPTH = 2
EPS = 1e-6
ARENA_KB = 207
NEG = -1e30

IN1 = dict(qa=0, ka=512, va=640, za=768, qlb=1280, kvlb=1664, krb=1920, zb=1952,
           bc=2464, cc=2976, uc=3488, zc=4000, g0=4512, g1=5536, g2=6560)
Z1 = ("za", "zb", "zc")
HEADS_A, HEADS_B = 8, 8
SCALE_B = float(96) ** -0.5
IN2 = dict(aq=0, ak=384, av=512, bq=640, bff=896, bfb=1152, bi=1408, bg=1664,
           cq=1920, ck=2304, cv=2432)
DFF = 2816
KF = DFF // P
HEADS_2 = 6
F_MIN = 1e-6
LEVELS = (4, 8, 16, 32, 64)

def vector_rows():
    rows = []

    def add(name, key, source, start, n):
        rows.append((name, key, source, start, n))

    add("c", 0, "c", 0, 8)
    add("c", 1, "c_ctx", 0, 8)
    add("c2", 0, "c_2", 0, 8)
    add("b_lb", 0, "b_lb_2", 0, 8)
    for l in range(DEPTH):
        add("b_mod", l, "b_mod", 24 * l, 24)
        add("g_pre", l, "g_pre", 8 * l, 8)
        add("g_post", l, "g_post", 8 * l, 8)
        add("g_qa", l, "g_qa", 3 * l, 3)
        add("g_kva", l, "g_kva", 2 * l, 2)
        add("conv1", l, "conv_w", 12 * l, 12)
    for l in range(DEPTH):
        add("b_ada", l, "b_ada_2", 48 * l, 48)
        add("norm2", l, "norm_g_2", 16 * l, 16)
        for g in ("a_q_norm_2", "a_k_norm_2", "b_out_norm_2", "c_q_norm_2", "c_k_norm_2"):
            add(g, l, g, l, 1)
    for l in range(DEPTH):
        add("conv_b", l, "conv_b_2", 44 * l, 44)
        for tap in range(3):
            add("conv2", (l, tap), "conv_w_2", 132 * l + 44 * tap, 44)
    batches, used = [], P + 1
    column = {}
    for name, key, source, start, n in rows:
        if used + n > P:
            batches.append([])
            used = 0
        batches[-1].append((used, source, start, n))
        column[name, key] = P * (len(batches) - 1) + used
        used += n
    return batches, column


VECTOR_BATCHES, COLUMN = vector_rows()
VCOLS = P * len(VECTOR_BATCHES)


def rope_tables(half, theta_dim, rows):
    pos_row = np.repeat(np.arange(rows, dtype=np.float32), 64)
    pos_col = np.tile(np.arange(64, dtype=np.float32), rows)
    inv = (np.float32(10000.0) ** (-np.arange(0, theta_dim, 2, dtype=np.float32) / np.float32(theta_dim))).astype(np.float32)
    return pos_row, pos_col, inv


def constants():
    ident = np.eye(P, dtype=np.float32)
    ones = np.ones((P, P), np.float32)
    blocks = np.kron(np.eye(2, dtype=np.float32), np.ones((64, 64), np.float32))

    def rotation(n, group):
        half = group // 2
        r = np.zeros((n, n), np.float32)
        for g in range(0, n, group):
            for i in range(half):
                r[g + i, g + half + i] = -1.0
                r[g + half + i, g + i] = 1.0
        return np.ascontiguousarray(r.T)

    rows = SEQ // 64

    def joint(rot_dim):
        row, col, inv = rope_tables(None, rot_dim // 2, rows)
        return np.concatenate([row[:, None] * inv, col[:, None] * inv], axis=-1).astype(np.float32).T

    ang = joint(64)
    ang_a = np.concatenate([ang, ang, ang, ang], 0)
    ang = joint(32)
    ang_b = np.zeros((P, SEQ), np.float32)
    ang_b[64:96] = np.concatenate([ang, ang], 0)
    rot_b = np.zeros((P, 32), np.float32)
    rot_b[64:96] = rotation(32, 32)
    q = np.arange(P)[:, None]
    k = np.arange(P)[None, :]
    prev = np.where(k >= q, 0.0, NEG).astype(np.float32)
    after = np.where(k <= q, 0.0, NEG).astype(np.float32)
    one = np.concatenate([ident, ones, blocks, rotation(P, 64), rot_b, prev, after,
                          np.cos(ang_a), np.sin(ang_a), np.cos(ang_b), np.sin(ang_b)], 1)
    row, col, inv = rope_tables(None, 32, rows)
    ar, ac = (row[:, None] * inv).astype(np.float32).T, (col[:, None] * inv).astype(np.float32).T
    ang_2 = np.concatenate([ar, ar, ac, ac] * 2, 0)
    two = np.concatenate([rotation(P, 32), np.cos(ang_2), np.sin(ang_2)], 1)
    d = np.arange(896)[None, :] - 384 - np.arange(P)[:, None]
    count = np.zeros(d.shape, np.float64)
    for w, r in ((128, 1), (512, 4), (2048, 16)):
        count += (np.abs(d) <= r * (w // (2 * r))) & (d % r == 0)
    slopes = (2.0 ** (-8.0 * np.arange(1, HEADS_2 + 1) / HEADS_2)).astype(np.float32)
    bias = [np.where(count > 0, -float(s) * np.abs(d) + np.log(np.maximum(count, 1)), NEG) for s in slopes]
    bias = np.concatenate(bias, 1)
    s, t = np.arange(P)[:, None], np.arange(P)[None, :]
    masks = [(s <= t) & (s // 8 == t // 8)]
    for h in LEVELS[1:]:
        masks.append((s // (2 * h) == t // (2 * h)) & (s % (2 * h) < h) & (t % (2 * h) >= h))
    masks = masks + [m.T for m in masks]
    masks = np.concatenate(masks, 1).astype(np.int32)
    return (np.ascontiguousarray(one, np.float32), np.ascontiguousarray(two, np.float32),
            np.ascontiguousarray(bias, np.float32), np.ascontiguousarray(masks))


class Ledger:

    def __init__(self, known):
        self.known, self.events, self.count = known, {}, {}

    def up(self, sem, key=None):
        n = self.count[sem.name] = self.count.get(sem.name, 0) + 1
        if key is not None:
            assert (sem.name, key) not in self.events, (sem.name, key)
            self.events[sem.name, key] = n
        return sem, 1

    def at(self, sem, key):
        if sem.name.startswith("evacuated"):
            return self.events["use", key]
        return self.known[sem.name, key] if self.known else 1

    def slot(self, key):
        return self.events["slot", key]


def program(nc, D, out, known, stop=None):
    led = Ledger(known)
    up, at = led.up, led.at
    ctx = ExitStack()
    with ctx:
        BASE = 16544
        ctx.enter_context(nc.sbuf_tensor("arena", [P, ARENA_KB * 256], F32))

        def place(name, shape, kb, dt=F32):
            return nc.alloc_sbuf_tensor_at(name, shape, dt, offset=BASE + int(kb * 1024))

        XT = place("XT", [P, KD, NT], 0)
        R0 = 24
        HH = place("HH", [P, KD, NT], R0, F32R)
        HL = place("HL", [P, KD, NT], R0 + 24, F32R)
        XIN = place("XIN", [P, NTB, DM], R0)
        OUT = place("OUT", [P, KD, NT], R0)
        XOUT = place("XOUT", [P, NXB, DM], R0)
        MA = R0 + 48
        MACC = place("MACC", [P, KD, NT], MA)
        MH = place("MH", [P, KD, NT], MA, F32R)
        WK = MA + 24
        RAWK = WK + 60
        NRAW, NWS = 3, 2
        RAW = [place(f"RAW{i}", [P, 1024], RAWK + 4 * i) for i in range(NRAW)]
        WH = [place(f"WH{i}", [P, 1024], RAWK + 12 + 4 * i, F32R) for i in range(NWS)]
        WL = [place(f"WL{i}", [P, 1024], RAWK + 20 + 4 * i, F32R) for i in range(NWS)]
        GV = [place(f"GV{i}", [P, NT], RAWK + 28 + 3 * i) for i in range(2)]
        CK = RAWK + 34
        VEC = place("VEC", [P, VCOLS], CK)
        CK += VCOLS * 4 / 1024
        CONST = place("CONST", [P, 4 * P + 32 + 2 * P], CK)
        CK += (6 * P + 32) * 4 / 1024
        ROPE = place("ROPE", [P, 4 * SEQ], CK)
        CK += 8
        ident, ones, blockones, rot_a = (CONST[:, i * P:(i + 1) * P] for i in range(4))
        rot_b = CONST[64:96, 512:544]
        mask_prev, mask_next = CONST[:, 544:672], CONST[:, 672:800]
        cos_a, sin_a, cos_b, sin_b = (ROPE[:, i * SEQ:(i + 1) * SEQ] for i in range(4))
        ROT2 = place("ROT2", [P, P], CK); CK += .5
        SINK = place("SINK", [P, DEPTH * HEADS_A], CK); CK += .0625
        MOD1 = place("MOD1", [P, 24, 2], CK); CK += .1875
        MOD1b = place("MOD1b", [P, 24, 2], CK); CK += .1875
        MOD2 = [place(f"MOD2{i}", [P, 48], CK + .1875 * i) for i in range(2)]; CK += .375
        MOD1 = [MOD1, MOD1b]
        SCG = place("SCG", [P, KD, 2], CK); CK += .0625
        SC = place("SC", [P, 24], CK); CK += .125
        CS = place("CS", [P, 24], CK); CK += .125
        GG = place("GG", [P, KD, 2], CK); CK += .0625
        LB = place("LB", [P, 32], CK); CK += .125
        SMALL = place("SMALL", [P, 64], CK); CK += .25
        epsb = place("epsb", [P, 8], CK); CK += .0625
        assert CK <= ARENA_KB, CK
        nmax = [SMALL[:, i:i + 1] for i in range(2)]
        rowsum = [SMALL[:, 2 + i:3 + i] for i in range(2)]
        rowinv = [SMALL[:, 4 + i:5 + i] for i in range(2)]
        smalls = SMALL[:, 8:64]

        YH = place("YH", [P, 4, NT], WK, F32R)
        YL = place("YL", [P, 4, NT], WK + 12, F32R)
        YTOK = place("YTOK", [P, NTB, 512], WK + 24)
        SZ = [place(f"SZ{i}", [P, NT], WK + 36 + 3 * i) for i in range(2)]
        SG = [place(f"SG{i}", [P, NT], WK + 54 + 3 * i) for i in range(2)]
        TM = [place(f"TM{i}", [P, NT], WK + 48 + 3 * i) for i in range(2)]
        ML = place("ML", [P, KD, NT], WK + 24, F32R)
        SQ = [place(f"SQ{i}", [P, NT], WK + 48 + 3 * i) for i in range(2)]
        ACC = place("ACC", [P, NT], WK + 54)
        RSTD = place("RSTD", [P, NT], WK + 57)
        PR = [place(f"PR{i}", [P, NT], WK + 48 + 3 * i) for i in range(2)]
        PT = [place(f"PT{i}", [P, NT], WK + 54 + 3 * i) for i in range(2)]
        QNH = place("QNH", [P, 3, NT], MA, F32R)
        QNL = place("QNL", [P, 3, NT], MA + 9, F32R)
        KVNH = place("KVNH", [P, 2, NT], MA + 18, F32R)
        KVNL = place("KVNL", [P, 2, NT], WK, F32R)
        QB = [place(f"QB{i}", [P, NT], WK + 6 + 3 * i) for i in range(2)]
        KB = [place(f"KB{i}", [P, NT], WK + 12 + 3 * i) for i in range(2)]
        KR = place("KR", [P, NT], WK + 18)
        T1 = place("T1", [P, SEQ], WK + 21)
        QLRAW = place("QLRAW", [P, 5, NT], WK + 24)
        VB = place("VB", [P, NTB, 512], WK + 36)
        QA = place("QA", [P, 4, NT], WK)
        KA = place("KA", [P, NT], WK + 12)
        VA = place("VA", [P, NTB, P], WK + 15)
        QRAW = [place(f"QRAW{i}", [P, NT], WK + 18 + 3 * i) for i in range(2)]
        T1a = place("T1a", [P, SEQ], WK + 36)
        T2a = place("T2a", [P, SEQ], WK + 38)
        CU = place("CU", [P, NT], WK + 24)
        ZP = place("ZP", [P, NT + 4], WK + 27)
        CV = place("CV", [P, NT], WK + 31)
        VROWS = place("VROWS", [P, len(VECTOR_BATCHES) * P], WK)

        HH2 = place("HH2", [P, KD, SEQ], R0, F32R)
        HL2 = place("HL2", [P, KD, SEQ], R0 + 16, F32R)
        XH2 = place("MIXH", [P, KD, SEQ], R0 + 32, F32R)
        XL2 = place("MIXL", [P, KD, SEQ], R0 + 48, F32R)
        B0 = R0 + 64
        FH = place("FH", [P, KF, SEQ], R0 + 32, F32R)
        FL = place("FL", [P, KF, SEQ], R0 + 76, F32R)
        UA = place("UA", [P, SEQ], R0 + 120)
        UB = place("UB", [P, SEQ], R0 + 122)
        SQ2 = [place(f"SQ2{i}", [P, SEQ], R0 + 124 + 2 * i) for i in range(2)]
        ACC2 = place("ACC2", [P, SEQ], R0 + 128)
        RSTD2 = place("RSTD2", [P, SEQ], R0 + 130)
        Q2 = place("Q2", [P, 3, SEQ], B0)
        K2 = place("K2", [P, SEQ], B0 + 6)
        V2 = place("V2", [P, NXB, P], B0 + 8)
        Y2 = place("Y2", [P, NXB, 384], B0 + 10)
        P2 = [place(f"P2{i}", [P, SEQ], B0 + 16 + 2 * i) for i in range(2)]
        PT2 = [place(f"PT2{i}", [P, SEQ], B0 + 20 + 2 * i) for i in range(2)]
        S2 = [place(f"S2{i}", [P, SEQ], B0 + 24 + 2 * i) for i in range(2)]
        QR2 = [place(f"QR2{i}", [P, SEQ], B0 + 28 + 2 * i) for i in range(2)]
        SS2 = [place(f"SS2{i}", [P, SEQ], B0 + 32 + 2 * i) for i in range(2)]
        RS2 = [place(f"RS2{i}", [P, SEQ], B0 + 36 + 2 * i) for i in range(2)]
        TA2 = place("TA2", [P, SEQ], B0 + 40)
        TB2 = place("TB2", [P, SEQ], B0 + 42)
        CBIAS = place("CBIAS", [P, HEADS_2 * 896], B0 + 44)
        QH = place("QH", [P, 2, SEQ], B0)
        FS = place("FS", [P, 4, SEQ], B0 + 4)
        LF = place("LF", [P, 4, SEQ], B0 + 12)
        KK = place("KK", [P, 4, SEQ], B0 + 20)
        VH = place("VH", [P, NXB, 256], B0 + 28)
        QP = [place(f"QP{i}", [P, SEQ], B0 + 32 + 2 * i) for i in range(2)]
        KP = [place(f"KP{i}", [P, SEQ], B0 + 36 + 2 * i) for i in range(2)]
        DD = [place(f"DD{i}", [P, SEQ], B0 + 40 + 2 * i) for i in range(2)]
        EE = [place(f"EE{i}", [P, SEQ], B0 + 44 + 2 * i) for i in range(2)]
        DIAG = [place(f"DIAG{i}", [P, 2, SEQ], B0 + 48 + 4 * i) for i in range(2)]
        OFF = [place(f"OFF{i}", [P, 2, 768], B0 + 56 + 6 * i) for i in range(2)]
        OTOK = place("OTOK", [P, NXB, 256], R0 + 32)
        OSQ = place("OSQ", [P, NXB * 256], R0 + 36)
        HMASK = place("HMASK", [P, 10 * P], R0 + 40, I32)
        ONE_ROW = place("ONE_ROW", [P, P], R0 + 45)
        QX = place("QX", [P, P], R0 + 45.5)
        KX = place("KX", [P, P], R0 + 46)
        EX = place("EX", [P, 4, 4], R0 + 46.5)
        QPX = place("QPX", [P, 4, SEQ], R0 + 48)
        SZ2 = [place(f"SZ2{i}", [P, SEQ], R0 + 56 + 2 * i) for i in range(2)]

        psum = [ctx.enter_context(nc.psum_tensor(f"ps{g}", [P, 1024], F32)) for g in range(4)]

        def sem(name):
            return ctx.enter_context(nc.semaphore(name))

        product_ready = sem("product_ready")
        evacuated = [sem(f"evacuated{g}") for g in range(4)]
        loaded = [sem(f"loaded{i}") for i in range(NRAW)]
        w_high = sem("w_high")
        w_low = sem("w_low")
        split_value = sem("split_value")
        split_high = sem("split_high")
        split_low = sem("split_low")
        act_step = sem("act_step")
        dve_step = sem("dve_step")
        pool_step = sem("pool_step")
        const_in = sem("const_in")
        x_in = sem("x_in")
        vec_in = sem("vec_in")
        out_done = sem("out_done")
        const2_in = sem("const2_in")
        masks_in = sem("masks_in")
        bias_in = sem("bias_in")
        to_act = sem("to_act")
        to_pe = sem("to_pe")
        to_pool = sem("to_pool")
        act_out = sem("act_out")
        probs_ready = sem("probs_ready")
        pool_out = sem("pool_out")

        units = []
        block = ctx.enter_context(nc.Block())

        def n_dmas(loads):
            return sum(2 if x[0] == "w_kvb_v" else 1 for x in loads)

        def used_columns(unit):
            return max((load[2] * load[5] if load[4] == load[5] or load[5] == P else 0)
                       + (load[6] if len(load) > 6 and load[4] == load[5] else 0) for load in unit[1])

        def at_split(key):
            return known["split", key] if known else 0

        def exponentials(eng, kind, l, n):
            if kind == "c":
                eng.wait_ge(probs_ready, at(probs_ready, (kind, l, n)))
            else:
                key = (kind, l, n, "s")
                eng.wait_ge(evacuated[led.slot(key)], at(evacuated[led.slot(key)], key))

        def vec(name, key, i=0):
            c = COLUMN[name, key] + i
            return VEC[:, c:c + 1]

        def segs(T):
            return [(0, SEQ)] if T == SEQ else [(0, SEQ), (SEQ, CTX)]

        def tokens(l):
            return NT if l == 0 else SEQ

        def attention_units(kind, l):
            got = []
            blocks = range(NTB) if l == 0 else range(NXB)
            if kind == "A":
                for qb in blocks:
                    for h in range(HEADS_A):
                        if qb < NXB:
                            lo, hi = max(qb - 1, 0), min(qb + 1, NXB - 1)
                            got.append((h, qb, lo * P, (hi - lo + 1) * P, CTX))
                        else:
                            got.append((h, qb, 0, 0, CTX))
            else:
                for h in range(HEADS_B):
                    for qb in blocks:
                        got.append((h, qb, 0, SEQ if qb < NXB else 0, CTX))
            return got

        def levels_order():
            return [(d, t, i) for d in range(2) for t in range(2) for i in range(len(LEVELS) + 1)]

        def PREF(n):
            return FS[:, n, :]

        def pr_of(kind, n):
            return (PR if kind in "AB" else P2)[n % 2]

        def pt_of(kind, n):
            return (PT if kind in "AB" else PT2)[n % 2]

        def cross_blocks(d):
            q = [QPX[:, 2 * d, c * P:(c + 1) * P] for c in range(4)]
            k = [QPX[:, 2 * d + 1, c * P:(c + 1) * P] for c in range(4)]
            if d == 0:
                return [(q[1], k[0], 0, 1), (q[3], k[2], 2, 3), (q[2], KX, 0, 2), (QX, KX, 0, 3),
                        (q[2], k[1], 1, 2), (QX, k[1], 1, 3)]
            return [(q[0], k[1], 1, 0), (q[2], k[3], 3, 2), (QX, k[2], 2, 0), (q[1], k[2], 2, 1),
                    (QX, KX, 3, 0), (q[1], KX, 3, 1)]


        @block.tensor
        def _(pe):
            group = [0]
            uses = [0] * 4
            raw_n, gemm_n = [0], [0]

            def open_group(key):
                g = group[0] % 4
                group[0] += 1
                led.events["slot", key] = g
                if uses[g]:
                    pe.wait_ge(evacuated[g], uses[g])
                uses[g] += 1
                led.events["use", key] = uses[g]
                return psum[g]

            def take(key, loads, split=True):
                n = len(units)
                s = sum(1 for u in units if u[2])
                units.append((key, loads, split))
                led.events["unit", key] = n
                if split:
                    pe.wait_ge(w_low, s + 1)
                    return WH[s % NWS], WL[s % NWS]
                pe.wait_ge(loaded[n % NRAW], 16 * sum(n_dmas(u[1]) for u in units[n % NRAW::NRAW]))
                return RAW[n % NRAW], None

            def given_back(key):
                led.events["unit_used", key] = led.count[product_ready.name]

            def channels(ps, unit, kt, c0, width, H, L, T, k0=0, first=True, last=True, stride=P):
                wh, wl = unit
                for k in range(kt):
                    w = [x[:, k * stride + c0:k * stride + c0 + width] for x in (wh, wl)]
                    for i, (a, b) in enumerate(((w[0], H), (w[0], L), (w[1], H))):
                        for t0, tn in segs(T):
                            ins = nc.tensor.matmul(ps[0:width, t0:t0 + tn], a, b[:, k0 + k, t0:t0 + tn],
                                                   start=first and k == 0 and i == 0,
                                                   stop=last and k == kt - 1 and i == 2)
                return ins

            def token_major(ps, unit, kt, width, H, L, tb, off=0, stride=P):
                wh, wl = unit
                for k in range(kt):
                    w = [x[:, k * stride:k * stride + width] for x in (wh, wl)]
                    for i, (a, b) in enumerate(((H, w[0]), (H, w[1]), (L, w[0]))):
                        ins = nc.tensor.matmul(ps[:, off:off + width], a[:, k, tb * P:(tb + 1) * P], b,
                                               start=k == 0 and i == 0, stop=k == kt - 1 and i == 2)
                return ins

            def w_in1(key, l, col):
                return take(key, [("w_in", l * DM, KD, col, P, P)])

            def gemm1(l, name, j, col, T, width=P):
                unit = w_in1((l, name, j), l, col)
                ps = open_group((l, name, j))
                channels(ps, unit, KD, 0, width, HH, HL, T).then_inc(*up(product_ready, (l, name, j)))
                given_back((l, name, j))

            def modulation(key, source, row0, col, vecs):
                w, _ = take(key, [(source, row0, KD, col, P, P)], split=False)
                ps = open_group(key)
                for k in range(KD):
                    ins = nc.tensor.matmul(ps[:, 0:len(vecs)], w[:, k * P:(k + 1) * P],
                                           CS[:, 8 * vecs[0] + k:8 * vecs[-1] + k + 1:8],
                                           start=k == 0, stop=k == KD - 1)
                ins.then_inc(*up(product_ready, key))
                given_back(key)

            def mods1(l, j):
                modulation(("mod1", l, j), "w_mod", l * DM, j * P, (0, 1))

            def mods2(l, j):
                modulation(("mod2", l, j), "w_ada_2", l * DM, j * P, (2,))

            def norm_sum(key, acc, T, mat=ones):
                pe.wait_ge(to_pe, at(to_pe, key))
                ps = open_group(key)
                for t0, tn in segs(T):
                    ins = nc.tensor.matmul(ps[:, t0:t0 + tn], mat, acc[:, t0:t0 + tn], start=True, stop=True)
                ins.then_inc(*up(product_ready, key))

            def attention(kind, l, us, q_of, k_of, v_of, ready, before=None):
                def scores(n):
                    h, qb, k0, nloc, nctx = us[n]
                    if before:
                        before(n)
                    ready(n, "scores")
                    ps = open_group((kind, l, n, "s"))
                    q, pieces, at_col = q_of(n), [], 0
                    for start, length in ((k0, nloc), (SEQ, nctx)):
                        while length:
                            m = min(length, 512 - at_col % 512)
                            pieces.append((at_col, start, m))
                            at_col, start, length = at_col + m, start + m, length - m
                    for c, start, m in pieces:
                        ins = nc.tensor.matmul(ps[:, c:c + m], q, k_of(n, start, m), start=True, stop=True)
                    ins.then_inc(*up(product_ready, (kind, l, n, "s")))

                def rest(n):
                    h, qb, k0, nloc, nctx = us[n]
                    kb = (nloc + nctx) // P
                    exponentials(pe, kind, l, n)
                    ps = open_group((kind, l, n, "t"))
                    pr = pr_of(kind, n)
                    for b in range(kb):
                        ins = nc.tensor.transpose(ps[:, b * P:(b + 1) * P], pr[:, b * P:(b + 1) * P], ident)
                    ins.then_inc(*up(product_ready, (kind, l, n, "t")))
                    g = led.slot((kind, l, n, "t"))
                    ps = open_group((kind, l, n, "o"))
                    pe.wait_ge(evacuated[g], at(evacuated[g], (kind, l, n, "t")))
                    ready(n, "values")
                    pt = pt_of(kind, n)
                    for b in range(kb):
                        start = k0 + b * P if b * P < nloc else SEQ + b * P - nloc
                        ins = nc.tensor.matmul(ps[:, 0:64], pt[:, b * P:(b + 1) * P], v_of(n, start // P),
                                               start=b == 0, stop=b == kb - 1)
                    ins.then_inc(*up(product_ready, (kind, l, n, "o")))

                for n in range(len(us)):
                    scores(n)
                    if n:
                        rest(n - 1)
                rest(len(us) - 1)

            def got(key):
                g = led.slot(key)
                pe.wait_ge(evacuated[g], at(evacuated[g], key))

            def head(h):
                return slice(64 * (h // 4), 64 * (h // 4) + 64)

            pe.wait_ge(const_in, 48)
            pe.wait_ge(x_in, 32)
            for k in range(KD):
                ps = open_group(("xT", k))
                for tb in range(NTB):
                    ins = nc.tensor.transpose(ps[:, tb * P:(tb + 1) * P], XIN[:, tb, k * P:(k + 1) * P], ident)
                ins.then_inc(*up(product_ready, ("xT", k)))
            pe.wait_ge(vec_in, 16 * sum(len(b) for b in VECTOR_BATCHES) + 16 * 10)
            for b in range(len(VECTOR_BATCHES)):
                ps = open_group(("vec", b))
                nc.tensor.transpose(ps[:, 0:P], VROWS[:, b * P:(b + 1) * P], ident).then_inc(
                    *up(product_ready, ("vec", b)))
            pe.wait_ge(act_out, at(act_out, "silu_c"))
            for j in range(24):
                mods1(0, j)

            def merge(l, b, T):
                for j in range(4):
                    gemm1(l, Z1[b], j, IN1[Z1[b]] + j * P, T)
                    if b < 2:
                        if j == 0:
                            last = len(attention_units("AB"[b], l)) - 1
                            got(("AB"[b], l, last, "o"))
                        ps = open_group((l, "yT", b, j))
                        for tb in range(T // P):
                            ins = nc.tensor.transpose(ps[:, tb * P:(tb + 1) * P],
                                                      YTOK[:, tb, j * P:(j + 1) * P], ident)
                        ins.then_inc(*up(product_ready, (l, "yT", b, j)))
                branch(l, b, T)

            def branch(l, b, T):
                for m0 in range(0, KD, 2):
                    unit = take((l, "wb", b, m0), [("w_branch", (l * 3 + b) * 512, 4, m0 * P, 2 * P, 2 * P)])
                    if m0 == 0:
                        pe.wait_ge(split_low, at(split_low, (l, "y", b, 3)))
                    for m in (m0, m0 + 1):
                        ps = open_group((l, "br", b, m))
                        channels(ps, unit, 4, (m % 2) * P, P, YH, YL, T, stride=2 * P).then_inc(
                            *up(product_ready, (l, "br", b, m)))
                    given_back((l, "wb", b, m0))
                    for m in (m0, m0 + 1):
                        gemm1(l, f"g{b}", m, IN1[f"g{b}"] + m * P, T)
                    for m in (m0, m0 + 1):
                        extra(l, b, m)

            def extra(l, b, m):
                i = b * KD + m
                if l == 0:
                    mods1(1, i)
                    mods2(0, 2 * i)
                    mods2(0, 2 * i + 1)
                else:
                    mods2(1, 2 * i)
                    mods2(1, 2 * i + 1)

            def first_layer(l):
                T = tokens(l)
                norm_sum((l, "pre"), ACC, NT)
                for j in range(3):
                    if j == 0:
                        pe.wait_ge(split_low, at(split_low, (l, "h", KD - 1)))
                    gemm1(l, "qlb", j, IN1["qlb"] + j * P, T)
                for j in range(2):
                    gemm1(l, "kvlb", j, IN1["kvlb"] + j * P, NT)
                gemm1(l, "krb", 0, IN1["krb"] - 64, NT, width=96)
                norm_sum((l, "qlb"), ACC, T)
                norm_sum((l, "kvlb"), ACC, NT)
                got((l, "krb", 0))
                ps = open_group((l, "kr_rot"))
                nc.tensor.matmul(ps[64:96, 0:SEQ], rot_b, KR[64:96, 0:SEQ], start=True, stop=True).then_inc(
                    *up(product_ready, (l, "kr_rot")))
                unit = take((l, "wv"), [("w_kvb_v", l * 256, 2, 0, 512, 512)])
                pe.wait_ge(split_low, at(split_low, (l, "kvn", 1)))
                for tb in range(NTB):
                    ps = open_group((l, "vb", tb))
                    token_major(ps, unit, 2, 512, KVNH, KVNL, tb, stride=512).then_inc(
                        *up(product_ready, (l, "vb", tb)))
                given_back((l, "wv"))
                us = attention_units("B", l)
                per_head = T // P

                def project(n):
                    if n % per_head:
                        return
                    h = n // per_head
                    unit = take((l, "wqk", h), [("w_qb", l * 384, 3, h * 96, 96, 96),
                                                ("w_kvb", l * 256, 2, h * P, P, P, 288)])
                    ps = open_group((l, "q", h))
                    wh, wl = unit
                    channels(ps, unit, 3, 0, 96, QNH, QNL, T, stride=96).then_inc(*up(product_ready, (l, "q", h)))
                    ps = open_group((l, "k", h))
                    channels(ps, (wh[:, 288:], wl[:, 288:]), 2, 0, P, KVNH, KVNL, NT).then_inc(
                        *up(product_ready, (l, "k", h)))
                    given_back((l, "wqk", h))
                    got((l, "q", h))
                    ps = open_group((l, "q_rot", h))
                    nc.tensor.matmul(ps[64:96, 0:SEQ], rot_b, QB[h % 2][64:96, 0:SEQ], start=True, stop=True).then_inc(
                        *up(product_ready, (l, "q_rot", h)))

                def ready(n, what):
                    h = n // per_head
                    if what == "scores" and n % per_head == 0:
                        got((l, "k", h))
                        pe.wait_ge(to_pe, at(to_pe, (l, "qb", h)))
                        if h == 0:
                            pe.wait_ge(to_pe, at(to_pe, (l, "kr")))
                    if what == "values" and n == 0:
                        for tb in range(NTB):
                            got((l, "vb", tb))

                attention("B", l, us,
                          lambda n: QB[us[n][0] % 2][0:96, us[n][1] * P:(us[n][1] + 1) * P],
                          lambda n, s, m: KB[us[n][0] % 2][0:96, s:s + m],
                          lambda n, tb: VB[:, tb, us[n][0] * 64:us[n][0] * 64 + 64],
                          ready, before=project)
                merge(l, 1, T)
                for j in range(5):
                    T_j = T if j < 4 else NT
                    if j < 4:
                        col = [IN1["qa"] + j * 64, IN1["qa"] + (j + 4) * 64]
                        unit = take((l, "qa", j), [("w_in", l * DM, KD, col[0], 64, P),
                                                   ("w_in", l * DM, KD, col[1], 64, P, 64)])
                    else:
                        unit = w_in1((l, "qa", j), l, IN1["ka"])
                    ps = open_group((l, "qa", j))
                    channels(ps, unit, KD, 0, P, HH, HL, T_j).then_inc(*up(product_ready, (l, "qa", j)))
                    given_back((l, "qa", j))
                    if j:
                        rotate_a(l, j - 1)
                unit = w_in1((l, "va"), l, IN1["va"])
                for tb in range(NTB):
                    ps = open_group((l, "va", tb))
                    token_major(ps, unit, KD, P, HH, HL, tb).then_inc(*up(product_ready, (l, "va", tb)))
                given_back((l, "va"))
                rotate_a(l, 4)
                us_a = attention_units("A", l)

                def ready_a(n, what):
                    if n == 0 and what == "scores":
                        pe.wait_ge(to_pe, at(to_pe, (l, "qa", 4)))
                    if n == 0 and what == "values":
                        for tb in range(NTB):
                            got((l, "va", tb))

                attention("A", l, us_a,
                          lambda n: QA[head(us_a[n][0]), us_a[n][0] % 4, us_a[n][1] * P:(us_a[n][1] + 1) * P],
                          lambda n, s, m: KA[head(us_a[n][0]), s:s + m],
                          lambda n, tb: VA[:, tb, head(us_a[n][0])],
                          ready_a)
                merge(l, 0, T)
                for j in range(4):
                    for name in ("cc", "uc", "bc"):
                        gemm1(l, name, j, IN1[name] + j * P, T)
                    gemm1(l, "zc", j, IN1["zc"] + j * P, T)
                branch(l, 2, T)
                for m in range(KD):
                    unit = take((l, "wo", m), [("w_o", l * DM, KD, m * P, P, P)])
                    if m == 0:
                        pe.wait_ge(split_low, at(split_low, (l, "m", KD - 1)))
                    ps = open_group((l, "o", m))
                    channels(ps, unit, KD, 0, P, MH, ML, T).then_inc(*up(product_ready, (l, "o", m)))
                    given_back((l, "wo", m))
                norm_sum((l, "post"), ACC, T)

            def rotate_a(l, j):
                got((l, "qa", j))
                ps = open_group((l, "qa_rot", j))
                nc.tensor.matmul(ps[:, 0:SEQ], rot_a, QRAW[j % 2][:, 0:SEQ], start=True, stop=True).then_inc(
                    *up(product_ready, (l, "qa_rot", j)))

            for l in range(DEPTH):
                first_layer(l)
                if stop == ("first", l):
                    break

            def gemm2(l, name, j, col, pieces=None):
                loads = [("w_in_2", l * DM, KD, col, P, P)] if pieces is None else \
                    [("w_in_2", l * DM, KD, c, 64, P, 64 * i) for i, c in enumerate(pieces)]
                unit = take(("2", l, name, j), loads)
                ps = open_group(("2", l, name, j))
                channels(ps, unit, KD, 0, P, HH2, HL2, SEQ).then_inc(*up(product_ready, ("2", l, name, j)))
                given_back(("2", l, name, j))

            def values2(l, name, col, width, first=0):
                unit = take(("2", l, name), [("w_in_2", l * DM, KD, col, P, P)])
                for tb in range(NXB):
                    ps = open_group(("2", l, name, tb))
                    token_major(ps, unit, KD, P, HH2, HL2, tb).then_inc(*up(product_ready, ("2", l, name, tb)))
                given_back(("2", l, name))

            def heads2(l, a):
                for j in range(4):
                    if j < 3:
                        gemm2(l, a + "q", j, None, [IN2[a + "q"] + j * 64, IN2[a + "q"] + (j + 3) * 64])
                    else:
                        gemm2(l, a + "q", j, IN2[a + "k"])
                    if j:
                        norm_rotate(l, a, j - 1)
                values2(l, a + "v", IN2[a + "v"], P)
                norm_rotate(l, a, 3)
                us = [(h, qb, 0, SEQ, 0) for h in range(HEADS_2) for qb in range(NXB)]

                def hd(h):
                    return slice(64 * (h // 3), 64 * (h // 3) + 64)

                def ready(n, what):
                    if n == 0 and what == "scores":
                        pe.wait_ge(to_pe, at(to_pe, ("2", l, a, 3)))
                    if n == 0 and what == "values":
                        for tb in range(NXB):
                            got(("2", l, a + "v", tb))

                attention(a, l, us,
                          lambda n: Q2[hd(us[n][0]), us[n][0] % 3, us[n][1] * P:(us[n][1] + 1) * P],
                          lambda n, s, m: K2[hd(us[n][0]), s:s + m],
                          lambda n, tb: V2[:, tb, hd(us[n][0])], ready)
                got((a, l, len(us) - 1, "o"))
                for j in range(3):
                    ps = open_group(("2", l, a + "yT", j))
                    for tb in range(NXB):
                        ins = nc.tensor.transpose(ps[:, tb * P:(tb + 1) * P], Y2[:, tb, j * P:(j + 1) * P], ident)
                    ins.then_inc(*up(product_ready, ("2", l, a + "yT", j)))

            def norm_rotate(l, a, j):
                pe.wait_ge(act_out, at(act_out, ("2", l, a, j, "sq")))
                ps = open_group(("2", l, a, j, "sum"))
                nc.tensor.matmul(ps[:, 0:SEQ], blockones, SS2[j % 2][:, :], start=True, stop=True).then_inc(
                    *up(product_ready, ("2", l, a, j, "sum")))
                if a == "a":
                    pe.wait_ge(to_pe, at(to_pe, ("2", l, a, j, "n")))
                    pe.wait_ge(const2_in, 32)
                    ps = open_group(("2", l, a, j, "rot"))
                    nc.tensor.matmul(ps[:, 0:SEQ], ROT2[:, :], QR2[j % 2][:, :], start=True, stop=True).then_inc(
                        *up(product_ready, ("2", l, a, j, "rot")))

            def recurrence(l):
                for name in ("bff", "bfb"):
                    for j in range(2):
                        gemm2(l, name, j, IN2[name] + j * P)
                for j in range(2):
                    gemm2(l, "bq", j, IN2["bq"] + j * P)
                for j in range(2):
                    values2(l, f"bi{j}", IN2["bi"] + j * P, P)
                for j in range(2):
                    gemm2(l, "bg", j, IN2["bg"] + j * P)
                for t in range(2):
                    for d in range(2):
                        for i in range(len(LEVELS)):
                            pe.wait_ge(to_pe, at(to_pe, ("2", l, "qp", t, d, i)))
                            pe.wait_ge(pool_out, at(pool_out, ("2", l, "kp", t, d, i)))
                            qp, kp = QP[i % 2], KP[i % 2]
                            for h in range(2):
                                ps = open_group(("2", l, "lev", t, d, i, h))
                                hs = slice(64 * h, 64 * h + 64)
                                for c in range(NXB):
                                    ins = nc.tensor.matmul(ps[:, c * P:(c + 1) * P], kp[hs, c * P:(c + 1) * P],
                                                           qp[hs, c * P:(c + 1) * P], start=True, stop=True)
                                ins.then_inc(*up(product_ready, ("2", l, "lev", t, d, i, h)))
                        pe.wait_ge(to_pe, at(to_pe, ("2", l, "cross", t, d)))
                        for h in range(2):
                            hs = slice(64 * h, 64 * h + 64)
                            ps = open_group(("2", l, "cross", t, d, h))
                            for n, (q, k, _, _) in enumerate(cross_blocks(d)):
                                ins = nc.tensor.matmul(ps[:, n * P:(n + 1) * P], k[hs, :], q[hs, :],
                                                       start=True, stop=True)
                            ins.then_inc(*up(product_ready, ("2", l, "cross", t, d, h)))
                    for h in range(2):
                        for d in range(2):
                            for i in range(len(LEVELS)):
                                got(("2", l, "lev", t, d, i, h))
                            got(("2", l, "cross", t, d, h))
                        for b in range(4):
                            got(("2", l, "bi0" if t == 0 else "bi1", b))
                        ps = open_group(("2", l, "pv", t, h))
                        cols = slice((2 * t + h) * 64, (2 * t + h) * 64 + 64)
                        for tb in range(NXB):
                            parts = [(DIAG[h][:, d, tb * P:(tb + 1) * P], tb) for d in range(2)]
                            for d in range(2):
                                for n, (_, _, s_c, t_c) in enumerate(cross_blocks(d)):
                                    if t_c == tb:
                                        parts.append((OFF[h][:, d, n * P:(n + 1) * P], s_c))
                            for n, (lhs, s_c) in enumerate(parts):
                                ins = nc.tensor.matmul(ps[:, tb * 64:(tb + 1) * 64], lhs, VH[:, s_c, cols],
                                                       start=n == 0, stop=n == len(parts) - 1)
                        ins.then_inc(*up(product_ready, ("2", l, "pv", t, h)))
                pe.wait_ge(to_pe, at(to_pe, ("2", l, "otok")))
                for j in range(2):
                    ps = open_group(("2", l, "byT", j))
                    for tb in range(NXB):
                        ins = nc.tensor.transpose(ps[:, tb * P:(tb + 1) * P], OTOK[:, tb, j * P:(j + 1) * P], ident)
                    ins.then_inc(*up(product_ready, ("2", l, "byT", j)))

            def second_layer(l):
                norm_sum(("2", l, "n", 0), ACC2, SEQ)
                pe.wait_ge(split_low, at(split_low, ("2", l, "h", 0, KD - 1)))
                recurrence(l)
                heads2(l, "a")
                heads2(l, "c")
                for m in range(KD):
                    unit = take(("2", l, "wout", m), [("w_out_2", l * DM, KD, m * P, P, P)])
                    if m == 0:
                        pe.wait_ge(split_low, at(split_low, ("2", l, "mix", "c", 2)))
                    ps = open_group(("2", l, "out", m))
                    channels(ps, unit, KD, 0, P, XH2, XL2, SEQ).then_inc(*up(product_ready, ("2", l, "out", m)))
                    given_back(("2", l, "wout", m))
                norm_sum(("2", l, "n", 1), ACC2, SEQ)
                pe.wait_ge(split_low, at(split_low, ("2", l, "h", 1, KD - 1)))
                for j in range(KF):
                    for s in range(2):
                        unit = take(("2", l, "up", j, s), [("w_up_2", l * DM, KD, s * DFF + j * P, P, P)])
                        ps = open_group(("2", l, "up", j, s))
                        channels(ps, unit, KD, 0, P, HH2, HL2, SEQ).then_inc(
                            *up(product_ready, ("2", l, "up", j, s)))
                        given_back(("2", l, "up", j, s))
                for m in range(KD):
                    ps = open_group(("2", l, "down", m))
                    for i, (k0, kt) in enumerate(((0, 8), (8, 8), (16, 6))):
                        unit = take(("2", l, "down", m, i), [("w_down_2", l * DFF + k0 * P, kt, m * P, P, P)])
                        if m == 0 and i == 0:
                            pe.wait_ge(split_low, at(split_low, ("2", l, "f", KF - 1)))
                        ins = channels(ps, unit, kt, 0, P, FH, FL, SEQ, k0=k0, first=i == 0, last=i == 2)
                        ins.then_inc(*up(product_ready, ("2", l, "down", m, i)))
                        given_back(("2", l, "down", m, i))

            if stop is None or stop[0] == "second":
                for l in range(DEPTH):
                    second_layer(l)
                    if stop == ("second", l):
                        break
            if stop is None:
                for m in range(KD):
                    got(("2", DEPTH - 1, "down", m))
            elif stop[0] == "first":
                pe.wait_ge(dve_step, at(dve_step, (stop[1], "x", KD - 1)))
            else:
                for m in range(KD):
                    got(("2", stop[1], "down", m))
            for tb in range(NXB):
                ps = open_group(("outT", tb))
                for k in range(KD):
                    ins = nc.tensor.transpose(ps[:, k * P:(k + 1) * P], XT[:, k, tb * P:(tb + 1) * P], ident)
                ins.then_inc(*up(product_ready, ("outT", tb)))

        split_units = [i for i, u in enumerate(units) if u[2]]

        def w_index(key):
            n = led.events["unit", key]
            return sum(1 for i in split_units if i <= n) - 1

        @block.sync
        def _(sp):
            sp.dma_start(CONST[:, :], D["const1"][:, 0:800]).then_inc(const_in, 16)
            sp.dma_start(ROPE[:, :], D["const1"][:, 800:800 + 4 * SEQ]).then_inc(const_in, 16)
            sp.dma_start(SINK[:, :], D["sink"].to_broadcast([P, DEPTH * HEADS_A])).then_inc(const_in, 16)
            for s in range(0, NTB, 4):
                src = D["x"].rearrange("(b p) n -> p b n", p=P) if s == 0 else \
                    D["ctx"].rearrange("(b p) n -> p b n", p=P)
                n = src.shape[1]
                sp.dma_start(XIN[:, s:s + n, :], src).then_inc(x_in, 16)
            sp.wait_ge(pool_step, 1)
            for b, batch in enumerate(VECTOR_BATCHES):
                for used, source, start, n in batch:
                    dst = VROWS[used:used + n, b * P:(b + 1) * P]
                    if D[source].shape[1] == 64:
                        sp.dma_start(dst[:, 0:64], D[source][start:start + n, :]).then_inc(vec_in, 16)
                        sp.dma_start(dst[:, 64:P], D[source][start:start + n, :]).then_inc(vec_in, 16)
                    else:
                        sp.dma_start(dst, D[source][start:start + n, :]).then_inc(vec_in, 16)
            for n, (key, loads, split) in enumerate(units):
                if n >= NRAW:
                    old, _, was_split = units[n - NRAW]
                    if was_split:
                        sp.wait_ge(w_low, sum(1 for i in split_units if i <= n - NRAW))
                    else:
                        sp.wait_ge(product_ready, led.events["unit_used", old])
                for load in loads:
                    source, row0, kt, col, width, stride = load[:6]
                    off = load[6] if len(load) > 6 else 0
                    dst = RAW[n % NRAW][:, off:off + (kt - 1) * stride + width] if width == stride else \
                        RAW[n % NRAW][:, 0:kt * stride]
                    if width == stride:
                        dst = dst.rearrange("p (k c) -> p k c", k=kt)
                    else:
                        dst = dst.rearrange("p (k c) -> p k c", k=kt)[:, :, off:off + width]
                    if source == "w_kvb_v":
                        for k in range(kt):
                            src = D["w_kvb"][row0 + k * P:row0 + (k + 1) * P, :]
                            src = src.rearrange("p (h c) -> p h c", c=P)[:, :, 64:P]
                            sp.dma_start(dst[:, k, :].rearrange("p (h c) -> p h c", c=64), src).then_inc(
                                loaded[n % NRAW], 16)
                    else:
                        src = D[source][row0:row0 + kt * P, :].rearrange("(k p) n -> p k n", p=P)
                        sp.dma_start(dst, src[:, :, col:col + width]).then_inc(loaded[n % NRAW], 16)
                if key == ("2", 0, "bff", 0):
                    sp.wait_ge(dve_step, at(dve_step, (1, "x", KD - 1)))
                    sp.dma_start(ROT2[:, :], D["const2"][:, 0:P]).then_inc(const2_in, 16)
                    sp.dma_start(ROPE[:, 0:2 * SEQ], D["const2"][:, P:P + 2 * SEQ]).then_inc(const2_in, 16)
                if key[0] == "2" and key[2:] == ("bff", 1):
                    l = key[1]
                    if l == 0:
                        sp.wait_ge(dve_step, at(dve_step, (1, "x", KD - 1)))
                    else:
                        sp.wait_ge(product_ready, led.events[product_ready.name, ("2", 0, "down", KD - 1, 2)])
                    sp.dma_start(HMASK[:, :], D["masks"][:, :]).then_inc(masks_in, 16)
                if key[0] == "2" and key[2:] == ("aq", 0):
                    l = key[1]
                    sp.wait_ge(product_ready, led.events[product_ready.name, ("2", l, "pv", 1, 1)])
                    sp.dma_start(CBIAS[:, :], D["bias"][:, :]).then_inc(bias_in, 16)
            for tb in range(NXB):
                sp.wait_ge(act_out, at(act_out, ("outT", tb)))
                sp.dma_start(out[tb * P:(tb + 1) * P, :], XOUT[:, tb, :]).then_inc(out_done, 16)
            sp.wait_ge(out_done, 16 * NXB)

        raw_count = {}
        for n, (key, loads, split) in enumerate(units):
            raw_count[n] = 16 * n_dmas(loads) + (raw_count[n - NRAW] if n >= NRAW else 0)

        def make_ahead(eng, emit):
            done = [0]

            def ahead(key, by=1):
                upto = min(w_index(key) + by, len(split_units) - 1)
                while done[0] <= upto:
                    emit(done[0])
                    done[0] += 1
            return ahead

        @block.scalar
        def _(act):
            A = nc.scalar.activation

            def split_weights(s):
                n = split_units[s]
                act.wait_ge(loaded[n % NRAW], raw_count[n])
                if s >= NWS:
                    act.wait_ge(product_ready, led.events["unit_used", units[split_units[s - NWS]][0]])
                w = units[n]
                used = used_columns(w)
                A(WH[s % NWS][:, 0:used], RAW[n % NRAW][:, 0:used], ACT.Copy).then_inc(*up(w_high))

            ahead = make_ahead(act, split_weights)

            def ready(key):
                act.wait_ge(product_ready, at(product_ready, key))
                return psum[led.slot(key)]

            def freed(key):
                return up(evacuated[led.slot(key)], key)

            def value_is_there(n_key, source=None):
                if source:
                    act.wait_ge(evacuated[led.slot(source)], at(evacuated[led.slot(source)], source))
                else:
                    act.wait_ge(split_value, at(split_value, n_key))

            def high(n_key, H, T, source=None):
                n = at_split(n_key)
                value_is_there(n_key, source)
                A(H, GV[n % 2][:, 0:T], ACT.Copy).then_inc(*up(split_high, n_key))

            def norm(key, tiles, sq, T, n, rstd_acc, wait=None):
                for i, x in enumerate(tiles):
                    if wait:
                        wait(i)
                    if i >= 2:
                        act.wait_ge(dve_step, at(dve_step, (key, "add", i - 2)))
                    A(sq[i % 2][:, 0:T], x, ACT.Square).then_inc(*up(act_out, (key, "sq", i)))
                root(key, T, n, rstd_acc)

            def root(key, T, n, rstd):
                ps = ready(key)
                A(rstd[:, 0:T], ps[:, 0:T], ACT.Sqrt, bias=epsb[:, 0:1], scale=1.0 / n).then_inc(*freed(key))

            for k in range(KD):
                ps = ready(("xT", k))
                A(XT[:, k, :], ps[:, 0:NT], ACT.Copy).then_inc(*freed(("xT", k)))
            act.wait_ge(dve_step, at(dve_step, "eps"))
            for b in range(len(VECTOR_BATCHES)):
                value_is_there(None, ("vec", b))
            A(CS[:, 0:16], VEC[:, COLUMN["c", 0]:COLUMN["c", 0] + 16], ACT.Silu).then_inc(*up(act_step, "cs"))
            A(CS[:, 16:24], VEC[:, COLUMN["c2", 0]:COLUMN["c2", 0] + 8], ACT.Silu).then_inc(*up(act_out, "silu_c"))
            act.wait_ge(dve_step, at(dve_step, "lb_max"))
            A(LB[:, 8:16], LB[:, 0:8], ACT.Exp).then_inc(*up(act_out, "lb_exp"))

            def attention(kind, l, us, width, dve_turns):
                for n in range(len(us)):
                    h, qb, k0, nloc, nctx = us[n]
                    keys = nloc + nctx + (1 if kind == "A" else 0)
                    if kind == "B" and n % width == 0:
                        hh = n // width
                        key = (l, "q", hh)
                        ahead((l, "wqk", hh))
                        T = tokens(l)
                        ps = ready(key)
                        if hh >= 2:
                            act.wait_ge(product_ready, at(product_ready, ("B", l, (hh - 1) * width - 1, "s")))
                        A(QB[hh % 2][0:96, 0:T], ps[0:96, 0:T], ACT.Copy, scale=SCALE_B).then_inc(*freed(key))
                        key = (l, "k", hh)
                        ps = ready(key)
                        A(KB[hh % 2][0:64, :], ps[0:64, 0:NT], ACT.Copy).then_inc(*freed(key))
                    act.wait_ge(to_act, at(to_act, (kind, l, n)))
                    if n >= 2:
                        act.wait_ge(product_ready, at(product_ready, (kind, l, n - 2, "t")))
                        act.wait_ge(dve_step, at(dve_step, (kind, l, n - 2, "inv")))
                    src = S2[n % 2][:, 0:keys] if kind == "c" else psum[led.slot((kind, l, n, "s"))][:, 0:keys]
                    pr = pr_of(kind, n)
                    ins = A(pr[:, 0:keys], src, ACT.Exp, bias=nmax[n % 2], accum_out=rowsum[n % 2])
                    if kind == "c":
                        ins.then_inc(*up(probs_ready, (kind, l, n)))
                    else:
                        ins.then_inc(*freed((kind, l, n, "s")))
                    if n and (n - 1) % dve_turns[1] >= dve_turns[0]:
                        evac_t(kind, l, us, n - 1)
                n = len(us) - 1
                if n % dve_turns[1] >= dve_turns[0]:
                    evac_t(kind, l, us, n)

            def evac_t(kind, l, us, n):
                h, qb, k0, nloc, nctx = us[n]
                keys = nloc + nctx
                key = (kind, l, n, "t")
                ps = ready(key)
                if n >= 2:
                    act.wait_ge(product_ready, at(product_ready, (kind, l, n - 2, "o")))
                A(pt_of(kind, n)[:, 0:keys], ps[:, 0:keys], ACT.Copy).then_inc(*freed(key))

            def merge(l, b, T):
                for j in range(4):
                    z_high(l, b, j, T)
                gates(l, b, T)

            def z_high(l, b, j, T):
                key = (l, Z1[b], j)
                ahead(key)
                ps = ready(key)
                if j >= 2:
                    value_is_there((l, "y", b, j - 2), (l, "yT", b, j - 2) if b < 2 else None)
                A(SZ[j % 2][:, 0:T], ps[:, 0:T], ACT.Silu).then_inc(*freed(key))
                high((l, "y", b, j), YH[:, j, 0:T], T, (l, "yT", b, j) if b < 2 else None)

            def gates(l, b, T):
                for m0 in range(0, KD, 2):
                    ahead((l, "wb", b, m0))
                    for m in (m0, m0 + 1):
                        key = (l, f"g{b}", m)
                        ahead(key, 1 - m % 2)
                        ps = ready(key)
                        if m >= 2:
                            old = (l, "br", b, m - 2)
                            act.wait_ge(evacuated[led.slot(old)], at(evacuated[led.slot(old)], old))
                        A(SG[m % 2][:, 0:T], ps[:, 0:T], ACT.Sigmoid).then_inc(*freed(key))
                    ahead((l, f"g{b}", m0 + 1))
                    if b == 2:
                        for m in (m0, m0 + 1):
                            high((l, "m", m), MH[:, m, 0:T], T)

            def first_layer(l):
                T = tokens(l)
                if l == 0:
                    wait = lambda k: act.wait_ge(evacuated[led.slot(("xT", k))], at(evacuated[led.slot(("xT", k))], ("xT", k)))
                else:
                    wait = lambda k: act.wait_ge(dve_step, at(dve_step, (0, "x", k)))
                norm((l, "pre"), [XT[:, k, :] for k in range(KD)], SQ, NT, DM, RSTD, wait)
                for k in range(KD):
                    high((l, "h", k), HH[:, k, :], NT)
                for j in range(6):
                    name, jj = (("qlb", j), ("kvlb", j - 3), ("krb", 0))[0 if j < 3 else 1 if j < 5 else 2]
                    key = (l, name, jj)
                    Tj = T if j < 3 else NT
                    ahead(key)
                    ps = ready(key)
                    if j < 5:
                        A(QLRAW[:, j, 0:Tj], ps[:, 0:Tj], ACT.Copy).then_inc(*freed(key))
                    else:
                        A(KR[64:96, :], ps[64:96, 0:NT], ACT.Copy).then_inc(*freed(key))
                ahead((l, "wv"), 0)
                own = lambda key: (lambda i: act.wait_ge(evacuated[led.slot((l, key, i))],
                                                         at(evacuated[led.slot((l, key, i))], (l, key, i))))
                norm((l, "qlb"), [QLRAW[:, j, 0:T] for j in range(3)], SQ, T, 384, RSTD, own("qlb"))
                for j in range(3):
                    high((l, "qn", j), QNH[:, j, 0:T], T)
                norm((l, "kvlb"), [QLRAW[:, 3 + j, :] for j in range(2)], SQ, NT, 256, RSTD, own("kvlb"))
                for j in range(2):
                    high((l, "kvn", j), KVNH[:, j, :], NT)
                for tb in range(NTB):
                    key = (l, "vb", tb)
                    if tb == 0:
                        ahead((l, "wv"))
                    ps = ready(key)
                    A(VB[:, tb, :], ps[:, 0:512], ACT.Copy).then_inc(*freed(key))
                attention("B", l, attention_units("B", l), T // P, (1, 2))
                merge(l, 1, T)
                for j in range(5):
                    Tj = T if j < 4 else NT
                    key = (l, "qa", j)
                    ahead(key)
                    ps = ready(key)
                    if j >= 2:
                        act.wait_ge(to_pe, at(to_pe, (l, "qa", j - 2)))
                    A(QRAW[j % 2][:, 0:Tj], ps[:, 0:Tj], ACT.Copy, scale=0.125 if j < 4 else 1.0).then_inc(*freed(key))
                for tb in range(NTB):
                    key = (l, "va", tb)
                    if tb == 0:
                        ahead((l, "va"))
                    ps = ready(key)
                    A(VA[:, tb, :], ps[:, 0:P], ACT.Copy).then_inc(*freed(key))
                attention("A", l, attention_units("A", l), 0, (0, 1))
                merge(l, 0, T)
                for j in range(4):
                    key = (l, "cc", j)
                    ahead(key)
                    ps = ready(key)
                    if j:
                        act.wait_ge(evacuated[led.slot((l, "uc", j - 1))],
                                    at(evacuated[led.slot((l, "uc", j - 1))], (l, "uc", j - 1)))
                    A(CU[:, 0:T], ps[:, 0:T], ACT.Copy).then_inc(*freed(key))
                    ahead((l, "uc", j))
                    ahead((l, "bc", j))
                    z_high(l, 2, j, T)
                gates(l, 2, T)
                for m in range(KD):
                    key = (l, "o", m)
                    ahead((l, "wo", m))
                    ps = ready(key)
                    A(OUT[:, m, 0:T], ps[:, 0:T], ACT.Copy).then_inc(*freed(key))
                norm((l, "post"), [OUT[:, m, 0:T] for m in range(KD)], SQ, T, DM, RSTD,
                     lambda m: act.wait_ge(evacuated[led.slot((l, "o", m))], at(evacuated[led.slot((l, "o", m))], (l, "o", m))))

            for l in range(DEPTH):
                first_layer(l)
                if stop == ("first", l):
                    break

            def norm2(l, i):
                if i == 0:
                    wait = (lambda k: act.wait_ge(dve_step, at(dve_step, (1, "x", k)))) if l == 0 else \
                        (lambda k: value_is_there(None, ("2", 0, "down", k)))
                else:
                    wait = lambda k: value_is_there(None, ("2", l, "out", k))
                norm(("2", l, "n", i), [XT[:, k, 0:SEQ] for k in range(KD)], SQ2, SEQ, DM, RSTD2, wait)
                for k in range(KD):
                    high(("2", l, "h", i, k), HH2[:, k, :], SEQ)

            def heads2(l, a):
                for j in range(4):
                    key = ("2", l, a + "q", j)
                    ahead(key)
                    ps = ready(key)
                    if j >= 2:
                        act.wait_ge(to_pe, at(to_pe, ("2", l, a, j - 2)))
                    A(QR2[j % 2][:, :], ps[:, 0:SEQ], ACT.Copy).then_inc(*freed(key))
                    act.wait_ge(evacuated[led.slot(key)], at(evacuated[led.slot(key)], key))
                    if j >= 2:
                        act.wait_ge(product_ready, at(product_ready, ("2", l, a, j - 2, "sum")))
                    A(SS2[j % 2][:, :], QR2[j % 2][:, :], ACT.Square).then_inc(*up(act_out, ("2", l, a, j, "sq")))
                    if j:
                        root2(l, a, j - 1)
                for tb in range(NXB):
                    key = ("2", l, a + "v", tb)
                    if tb == 0:
                        ahead(("2", l, a + "v"))
                    ps = ready(key)
                    A(V2[:, tb, :], ps[:, 0:P], ACT.Copy).then_inc(*freed(key))
                root2(l, a, 3)
                attention(a, l, [(h, qb, 0, SEQ, 0) for h in range(HEADS_2) for qb in range(NXB)], 0,
                          (0, 1) if a == "c" else (1, 2))
                for j in range(3):
                    high(("2", l, "mix", a, j), XH2[:, (0 if a == "a" else 5) + j, :], SEQ, ("2", l, a + "yT", j))

            def root2(l, a, j):
                key = ("2", l, a, j, "sum")
                if j >= 2:
                    act.wait_ge(to_pe, at(to_pe, ("2", l, a, j - 2)))
                ps = ready(key)
                A(RS2[j % 2][:, :], ps[:, 0:SEQ], ACT.Sqrt, bias=epsb[:, 0:1], scale=1.0 / 64).then_inc(*freed(key))

            def recurrence(l):
                for n in range(4):
                    name, j = (("bff", "bfb")[n // 2], n % 2)
                    key = ("2", l, name, j)
                    ahead(key)
                    ps = ready(key)
                    A(FS[:, n, :], ps[:, 0:SEQ], ACT.Sigmoid).then_inc(*freed(key))
                for j in range(2):
                    key = ("2", l, "bq", j)
                    ahead(key)
                    ps = ready(key)
                    A(QH[:, j, :], ps[:, 0:SEQ], ACT.Copy).then_inc(*freed(key))
                for j in range(2):
                    for tb in range(NXB):
                        key = ("2", l, f"bi{j}", tb)
                        if tb == 0:
                            ahead(("2", l, f"bi{j}"))
                        ps = ready(key)
                        A(VH[:, tb, j * P:(j + 1) * P], ps[:, 0:P], ACT.Copy).then_inc(*freed(key))
                for j in range(2):
                    key = ("2", l, "bg", j)
                    ahead(key)
                    ps = ready(key)
                    A(SZ2[j][:, :], ps[:, 0:SEQ], ACT.Silu).then_inc(*freed(key))
                for n in range(4):
                    act.wait_ge(to_act, at(to_act, ("2", l, "f", n)))
                    A(LF[:, n, :], FS[:, n, :], ACT.Ln).then_inc(*up(act_out, ("2", l, "lf", n)))
                for t in range(2):
                    for d in range(2):
                        n = 2 * d + t
                        for i in range(len(LEVELS)):
                            act.wait_ge(to_act, at(to_act, ("2", l, "dd", t, d, i)))
                            if i == 0:
                                sign = 1.0 if d == 0 else -1.0
                                A(EE[0][:, :], DD[0][:, :], ACT.Exp, scale=sign).then_inc(
                                    *up(act_out, ("2", l, "ee", t, d, "q")))
                                A(EE[1][:, :], DD[0][:, :], ACT.Exp, scale=-sign).then_inc(
                                    *up(act_out, ("2", l, "ee", t, d, 0)))
                            else:
                                e = (i + 1) % 2
                                A(EE[e][:, :], DD[i % 2][:, :], ACT.Exp, scale=-1.0).then_inc(
                                    *up(act_out, ("2", l, "ee", t, d, i)))
                        act.wait_ge(to_act, at(to_act, ("2", l, "dx", t, d)))
                        A(EE[0][:, :], PREF(n), ACT.Exp).then_inc(*up(act_out, ("2", l, "ex", t, d, 0)))
                        A(EE[1][:, :], DD[1][:, :], ACT.Exp, scale=-1.0).then_inc(*up(act_out, ("2", l, "ex", t, d, 1)))
                        A(EX[:, n, 0:4], SMALL[:, 16 + 4 * n:20 + 4 * n], ACT.Exp).then_inc(
                            *up(act_out, ("2", l, "ex", t, d, 2)))
                act.wait_ge(to_act, at(to_act, ("2", l, "oss")))
                A(smalls[:, 24:40], smalls[:, 24:40], ACT.Sqrt, bias=epsb[:, 0:1], scale=1.0 / 64).then_inc(
                    *up(act_out, ("2", l, "oss")))
                for j in range(2):
                    high(("2", l, "mix", "b", j), XH2[:, 3 + j, :], SEQ, ("2", l, "byT", j))

            def second_layer(l):
                norm2(l, 0)
                recurrence(l)
                heads2(l, "a")
                heads2(l, "c")
                for m in range(KD):
                    ahead(("2", l, "wout", m))
                norm2(l, 1)
                for j in range(KF):
                    for s in range(2):
                        key = ("2", l, "up", j, s)
                        ahead(key)
                        U = (UA, UB)[s]
                        ps = ready(key)
                        if j:
                            act.wait_ge(split_value, at(split_value, ("2", l, "f", j - 1)))
                        c = s * KF + j
                        A(U[:, :], ps[:, 0:SEQ], ACT.Identity, bias=vec("conv_b", l, c),
                          scale=vec("conv2", (l, 1), c)).then_inc(*up(act_out, ("2", l, "u", j, s)))
                    value_is_there(None, ("2", l, "up", j, 0))
                    A(UA[:, :], UA[:, :], ACT.Silu).then_inc(*up(act_out, ("2", l, "silu", j)))
                    high(("2", l, "f", j), FH[:, j, :], SEQ)
                for m in range(KD):
                    for i in range(3):
                        ahead(("2", l, "down", m, i))

            if stop is None or stop[0] == "second":
                for l in range(DEPTH):
                    second_layer(l)
                    if stop == ("second", l):
                        break
            for tb in range(NXB):
                key = ("outT", tb)
                ps = ready(key)
                A(XOUT[:, tb, :], ps[:, 0:DM], ACT.Copy).then_inc(*up(act_out, key))

        @block.gpsimd
        def _(pool):
            def split_weights(s):
                n = split_units[s]
                pool.wait_ge(w_high, s + 1)
                if s >= NWS:
                    pool.wait_ge(product_ready, led.events["unit_used", units[split_units[s - NWS]][0]])
                used = used_columns(units[n])
                nc.gpsimd.tensor_tensor(WL[s % NWS][:, 0:used], RAW[n % NRAW][:, 0:used],
                                        WH[s % NWS][:, 0:used].bitcast(F32), ALU.subtract).then_inc(*up(w_low))

            ahead = make_ahead(pool, split_weights)

            def low(key, L, H, T):
                n = at_split(key)
                pool.wait_ge(split_high, at(split_high, key))
                nc.gpsimd.tensor_tensor(L, GV[n % 2][:, 0:T], H.bitcast(F32), ALU.subtract).then_inc(
                    *up(split_low, key))

            nc.gpsimd.memset(VROWS[:, :], 0.0).then_inc(*up(pool_step))

            def gates(l, b, T):
                for m0 in range(0, KD, 2):
                    ahead((l, "wb", b, m0))
                    ahead((l, f"g{b}", m0))
                    ahead((l, f"g{b}", m0 + 1))
                    if b == 2:
                        for m in (m0, m0 + 1):
                            low((l, "m", m), ML[:, m, 0:T], MH[:, m, 0:T], T)

            def first_layer(l):
                T = tokens(l)
                for k in range(KD):
                    low((l, "h", k), HL[:, k, :], HH[:, k, :], NT)
                for j in range(3):
                    ahead((l, "qlb", j))
                for j in range(2):
                    ahead((l, "kvlb", j))
                ahead((l, "krb", 0))
                for j in range(3):
                    low((l, "qn", j), QNL[:, j, 0:T], QNH[:, j, 0:T], T)
                for j in range(2):
                    low((l, "kvn", j), KVNL[:, j, :], KVNH[:, j, :], NT)
                ahead((l, "wv"))
                for h in range(HEADS_B):
                    ahead((l, "wqk", h))
                for b in (1, 0):
                    for j in range(4):
                        ahead((l, Z1[b], j))
                        low((l, "y", b, j), YL[:, j, 0:T], YH[:, j, 0:T], T)
                    gates(l, b, T)
                    if b == 1:
                        for j in range(5):
                            ahead((l, "qa", j))
                        ahead((l, "va"))
                for j in range(4):
                    for name in ("cc", "uc", "bc", "zc"):
                        ahead((l, name, j))
                    low((l, "y", 2, j), YL[:, j, 0:T], YH[:, j, 0:T], T)
                gates(l, 2, T)
                for m in range(KD):
                    ahead((l, "wo", m))

            for l in range(DEPTH):
                first_layer(l)
                if stop == ("first", l):
                    break

            def heads2(l, a):
                for j in range(4):
                    ahead(("2", l, a + "q", j))
                ahead(("2", l, a + "v"))
                for j in range(3):
                    c = (0 if a == "a" else 5) + j
                    low(("2", l, "mix", a, j), XL2[:, c, :], XH2[:, c, :], SEQ)

            def recurrence(l):
                for name in ("bff", "bfb", "bq"):
                    for j in range(2):
                        ahead(("2", l, name, j))
                for j in range(2):
                    ahead(("2", l, f"bi{j}"))
                for j in range(2):
                    ahead(("2", l, "bg", j))
                for t in range(2):
                    for d in range(2):
                        n = 2 * d + t
                        for i in range(len(LEVELS)):
                            pool.wait_ge(act_out, at(act_out, ("2", l, "ee", t, d, i)))
                            pool.wait_ge(to_pool, at(to_pool, ("2", l, "kk", n)))
                            prev = (t, d, i - 2, 1) if i >= 2 else None
                            if prev:
                                pool.wait_ge(product_ready, at(product_ready, ("2", l, "lev") + prev))
                            elif (t, d) != (0, 0):
                                td = (t, d - 1) if d else (t - 1, 1)
                                pool.wait_ge(product_ready, at(product_ready, ("2", l, "lev") + td + (4, 1)))
                            nc.gpsimd.tensor_tensor(KP[i % 2][:, :], KK[:, n, :], EE[(i + 1) % 2][:, :],
                                                    ALU.mult).then_inc(*up(pool_out, ("2", l, "kp", t, d, i)))
                for j in range(2):
                    low(("2", l, "mix", "b", j), XL2[:, 3 + j, :], XH2[:, 3 + j, :], SEQ)

            def second_layer(l):
                for k in range(KD):
                    low(("2", l, "h", 0, k), HL2[:, k, :], HH2[:, k, :], SEQ)
                recurrence(l)
                heads2(l, "a")
                heads2(l, "c")
                for m in range(KD):
                    ahead(("2", l, "wout", m))
                for k in range(KD):
                    low(("2", l, "h", 1, k), HL2[:, k, :], HH2[:, k, :], SEQ)
                for j in range(KF):
                    for s in range(2):
                        ahead(("2", l, "up", j, s))
                    low(("2", l, "f", j), FL[:, j, :], FH[:, j, :], SEQ)
                for m in range(KD):
                    for i in range(3):
                        ahead(("2", l, "down", m, i))

            if stop is None or stop[0] == "second":
                for l in range(DEPTH):
                    second_layer(l)
                    if stop == ("second", l):
                        break

        splits = [0]
        split_n = {}

        @block.vector
        def _(dve):
            V = nc.vector

            def ready(key):
                dve.wait_ge(product_ready, at(product_ready, key))
                return psum[led.slot(key)]

            def freed(key):
                return up(evacuated[led.slot(key)], key)

            def own(key):
                dve.wait_ge(evacuated[led.slot(key)], at(evacuated[led.slot(key)], key))

            def step(ins, key=None):
                s, _ = up(dve_step, key)
                ins.then_inc(s, 1)
                dve.wait_ge(s, led.count[s.name])

            def value(key):
                n = splits[0]
                splits[0] += 1
                led.events["split", key] = n
                split_n[n] = key
                if n >= 2:
                    dve.wait_ge(split_low, n - 1)
                return GV[n % 2]

            def valued(key):
                return up(split_value, key)

            def norm(key, tiles, sq, acc, rstd, T):
                for i in range(tiles):
                    dve.wait_ge(act_out, at(act_out, (key, "sq", i)))
                    if i == 0:
                        step(V.tensor_copy(acc[:, 0:T], sq[0][:, 0:T]), (key, "add", 0))
                    elif i < tiles - 1:
                        step(V.tensor_tensor(acc[:, 0:T], acc[:, 0:T], sq[i % 2][:, 0:T], ALU.add), (key, "add", i))
                    else:
                        V.tensor_tensor(acc[:, 0:T], acc[:, 0:T], sq[i % 2][:, 0:T], ALU.add).then_inc(
                            *up(to_pe, key))
                        dve.wait_ge(to_pe, led.count[to_pe.name])
                own(key)
                step(V.reciprocal(rstd[:, 0:T], rstd[:, 0:T]))

            step(V.memset(epsb[:, :], EPS), "eps")
            step(V.memset(SMALL[:, :], 0.0))
            for b in range(len(VECTOR_BATCHES)):
                key = ("vec", b)
                ps = ready(key)
                V.tensor_copy(VEC[:, b * P:(b + 1) * P], ps[:, 0:P]).then_inc(*freed(key))
                own(key)
            raw = VEC[:, COLUMN["b_lb", 0]:COLUMN["b_lb", 0] + 8].rearrange("p (d l t) -> p d l t", d=2, l=2)
            lb = LB[:, 0:8].rearrange("p (d l t) -> p d l t", d=2, l=2)
            ex = LB[:, 8:16].rearrange("p (d l t) -> p d l t", d=2, l=2)
            m4 = LB[:, 16:20].rearrange("p (d t) -> p d t", d=2)
            step(V.tensor_tensor(m4, raw[:, :, 0, :], raw[:, :, 1, :], ALU.max))
            step(V.tensor_tensor(lb[:, :, 0, :], raw[:, :, 0, :], m4, ALU.subtract))
            step(V.tensor_tensor(lb[:, :, 1, :], raw[:, :, 1, :], m4, ALU.subtract), "lb_max")
            dve.wait_ge(act_out, at(act_out, "lb_exp"))
            step(V.tensor_tensor(m4, ex[:, :, 0, :], ex[:, :, 1, :], ALU.add))
            step(V.reciprocal(LB[:, 20:24], LB[:, 16:20]))
            r4 = LB[:, 20:24].rearrange("p (d t) -> p d t", d=2)
            for i in range(2):
                step(V.tensor_tensor(ex[:, :, i, :], ex[:, :, i, :], r4, ALU.mult))
            l0 = LB[:, 24:28].rearrange("p (d t) -> p d t", d=2)
            l1 = LB[:, 28:32].rearrange("p (d t) -> p d t", d=2)
            step(V.tensor_tensor(l0, ex[:, :, 0, :], ex[:, :, 0, :], ALU.subtract))
            step(V.tensor_tensor(m4, ex[:, :, 0, :], ex[:, :, 1, :], ALU.add))
            step(V.tensor_tensor(l1, m4, ex[:, :, 0, :], ALU.subtract))
            dve.wait_ge(const_in, 48)

            def mod1(l, j):
                key = ("mod1", l, j)
                ps = ready(key)
                V.tensor_scalar(MOD1[l][:, j, :], ps[:, 0:2], vec("b_mod", l, j), None, ALU.add).then_inc(*freed(key))

            def mod2(l, j):
                key = ("mod2", l, j)
                ps = ready(key)
                V.tensor_scalar(MOD2[l][:, j:j + 1], ps[:, 0:1], vec("b_ada", l, j), None, ALU.add).then_inc(*freed(key))

            def extra(l, b, m):
                i = b * KD + m
                if l == 0:
                    mod1(1, i)
                    mod2(0, 2 * i)
                    mod2(0, 2 * i + 1)
                else:
                    mod2(1, 2 * i)
                    mod2(1, 2 * i + 1)

            for j in range(24):
                mod1(0, j)

            def attention(kind, l, us, width, dve_turns, y_of):
                for n in range(len(us) + 1):
                    if n < len(us):
                        h, qb, k0, nloc, nctx = us[n]
                        keys = nloc + nctx
                        if kind == "B" and n % width == 0:
                            rotate_q(l, n // width)
                        ps = ready((kind, l, n, "s"))
                        if n >= 2:
                            exponentials(dve, kind, l, n - 2)
                        src = ps[:, 0:keys]
                        if kind == "A":
                            if qb < NXB and qb > 0:
                                step(V.tensor_tensor(ps[:, 0:P], ps[:, 0:P], mask_prev, ALU.add))
                            if qb < NXB - 1:
                                step(V.tensor_tensor(ps[:, nloc - P:nloc], ps[:, nloc - P:nloc], mask_next, ALU.add))
                            step(V.tensor_copy(ps[:, keys:keys + 1], SINK[:, l * HEADS_A + h:l * HEADS_A + h + 1]))
                            src = ps[:, 0:keys + 1]
                        elif kind == "c":
                            off = h * 896 + 384 - qb * P
                            V.tensor_tensor(S2[n % 2][:, :], ps[:, 0:SEQ], CBIAS[:, off:off + SEQ], ALU.add).then_inc(
                                *freed((kind, l, n, "s")))
                            own((kind, l, n, "s"))
                            src = S2[n % 2][:, :]
                        V.tensor_reduce(nmax[n % 2], src, AX.X, ALU.max, negate=True).then_inc(*up(to_act, (kind, l, n)))
                    if n:
                        m = n - 1
                        h, qb, k0, nloc, nctx = us[m]
                        keys = nloc + nctx
                        if m % dve_turns[1] < dve_turns[0]:
                            key = (kind, l, m, "t")
                            ps = ready(key)
                            if m >= 2:
                                dve.wait_ge(product_ready, at(product_ready, (kind, l, m - 2, "o")))
                            V.tensor_copy(pt_of(kind, m)[:, 0:keys], ps[:, 0:keys]).then_inc(*freed(key))
                        exponentials(dve, kind, l, m)
                        step(V.reciprocal(rowinv[m % 2], rowsum[m % 2]), (kind, l, m, "inv"))
                        key = (kind, l, m, "o")
                        ps = ready(key)
                        V.tensor_scalar(y_of(us[m]), ps[:, 0:64], rowinv[m % 2], None, ALU.mult).then_inc(*freed(key))

            def rotate_q(l, h):
                key = (l, "q_rot", h)
                ps = ready(key)
                g = led.slot((l, "q", h))
                dve.wait_ge(evacuated[g], at(evacuated[g], (l, "q", h)))
                step(V.tensor_tensor(T1[64:96, :], ps[64:96, 0:SEQ], sin_b[64:96, :], ALU.mult))
                V.tensor_tensor(QB[h % 2][64:96, 0:SEQ], QB[h % 2][64:96, 0:SEQ], cos_b[64:96, :], ALU.mult).then_inc(
                    *freed(key))
                own(key)
                V.tensor_tensor(QB[h % 2][64:96, 0:SEQ], QB[h % 2][64:96, 0:SEQ], T1[64:96, :], ALU.add).then_inc(
                    *up(to_pe, (l, "qb", h)))
                dve.wait_ge(to_pe, led.count[to_pe.name])

            def rotate_a(l, j):
                T = tokens(l) if j < 4 else NT
                dst = QA[:, j, :] if j < 4 else KA[:, :]
                key = (l, "qa_rot", j)
                ps = ready(key)
                own((l, "qa", j))
                step(V.tensor_tensor(T1a[:, :], ps[:, 0:SEQ], sin_a, ALU.mult))
                V.tensor_tensor(T2a[:, :], QRAW[j % 2][:, 0:SEQ], cos_a, ALU.mult).then_inc(*freed(key))
                own(key)
                if T > SEQ:
                    step(V.tensor_copy(dst[:, SEQ:T], QRAW[j % 2][:, SEQ:T]))
                V.tensor_tensor(dst[:, 0:SEQ], T1a[:, :], T2a[:, :], ALU.add).then_inc(*up(to_pe, (l, "qa", j)))
                dve.wait_ge(to_pe, led.count[to_pe.name])

            def z_gate(l, b, j, T):
                if b < 2:
                    key = (l, "yT", b, j)
                    ps = ready(key)
                    own((l, Z1[b], j))
                    gv = value((l, "y", b, j))
                    V.tensor_tensor(gv[:, 0:T], ps[:, 0:T], SZ[j % 2][:, 0:T], ALU.mult).then_inc(*freed(key))
                    own(key)

            def gates(l, b, T):
                for m in range(KD):
                    key = (l, "br", b, m)
                    ps = ready(key)
                    own((l, f"g{b}", m))
                    first = b == 1
                    if first:
                        V.tensor_tensor(MACC[:, m, 0:T], ps[:, 0:T], SG[m % 2][:, 0:T], ALU.mult).then_inc(*freed(key))
                        own(key)
                    else:
                        V.tensor_tensor(TM[m % 2][:, 0:T], ps[:, 0:T], SG[m % 2][:, 0:T], ALU.mult).then_inc(*freed(key))
                        own(key)
                        if b == 0:
                            step(V.tensor_tensor(MACC[:, m, 0:T], MACC[:, m, 0:T], TM[m % 2][:, 0:T], ALU.add))
                        else:
                            gv = value((l, "m", m))
                            V.tensor_tensor(gv[:, 0:T], MACC[:, m, 0:T], TM[m % 2][:, 0:T], ALU.add).then_inc(
                                *valued((l, "m", m)))
                    if m % 2:
                        extra(l, b, m - 1)
                        extra(l, b, m)

            def first_layer(l):
                T = tokens(l)
                for k in range(24):
                    own(("mod1", l, k))
                for k in range(KD):
                    V.tensor_scalar(SCG[:, k, :], MOD1[l][:, KD + k, :], 1.0, vec("g_pre", l, k), ALU.add,
                                    ALU.mult).then_inc(*up(dve_step))
                    step(V.tensor_scalar(GG[:, k, :], MOD1[l][:, 2 * KD + k, :], vec("g_post", l, k), None, ALU.mult))
                norm((l, "pre"), KD, SQ, ACC, RSTD, NT)
                if l == 0:
                    for k in range(KD):
                        own(("xT", k))
                for k in range(KD):
                    key = (l, "h", k)
                    gv = value(key)
                    step(V.tensor_tensor(gv[:, :], XT[:, k, :], RSTD[:, :], ALU.mult))
                    for s, (t0, tn) in enumerate(segs(NT)):
                        ins = V.tensor_scalar(gv[:, t0:t0 + tn], gv[:, t0:t0 + tn], SCG[:, k, s:s + 1],
                                              MOD1[l][:, k, s:s + 1], ALU.mult, ALU.add)
                        if s == 0:
                            step(ins)
                    ins.then_inc(*valued(key))
                norm((l, "qlb"), 3, SQ, ACC, RSTD, T)
                for j in range(3):
                    own((l, "qlb", j))
                    gv = value((l, "qn", j))
                    ins = V.scalar_tensor_tensor(gv[:, 0:T], QLRAW[:, j, 0:T], vec("g_qa", l, j), RSTD[:, 0:T],
                                                 ALU.mult, ALU.mult)
                    ins.then_inc(*valued((l, "qn", j)))
                dve.wait_ge(split_value, led.count[split_value.name])
                norm((l, "kvlb"), 2, SQ, ACC, RSTD, NT)
                for j in range(2):
                    own((l, "kvlb", j))
                    gv = value((l, "kvn", j))
                    ins = V.scalar_tensor_tensor(gv[:, :], QLRAW[:, 3 + j, :], vec("g_kva", l, j), RSTD[:, :],
                                                 ALU.mult, ALU.mult)
                    ins.then_inc(*valued((l, "kvn", j)))
                key = (l, "kr_rot")
                own((l, "krb", 0))
                ps = ready(key)
                step(V.tensor_tensor(T1[64:96, :], ps[64:96, 0:SEQ], sin_b[64:96, :], ALU.mult))
                V.tensor_tensor(KR[64:96, 0:SEQ], KR[64:96, 0:SEQ], cos_b[64:96, :], ALU.mult).then_inc(*freed(key))
                own(key)
                step(V.tensor_tensor(KR[64:96, 0:SEQ], KR[64:96, 0:SEQ], T1[64:96, :], ALU.add))
                step(V.tensor_copy(KB[0][64:96, :], KR[64:96, :]))
                V.tensor_copy(KB[1][64:96, :], KR[64:96, :]).then_inc(*up(to_pe, (l, "kr")))
                us = attention_units("B", l)
                attention("B", l, us, T // P, (1, 2), lambda u: YTOK[:, u[1], u[0] * 64:u[0] * 64 + 64])
                for j in range(4):
                    z_gate(l, 1, j, T)
                gates(l, 1, T)
                for j in range(5):
                    rotate_a(l, j)
                us = attention_units("A", l)
                attention("A", l, us, 0, (0, 1), lambda u: YTOK[:, u[1], u[0] * 64:u[0] * 64 + 64])
                for j in range(4):
                    z_gate(l, 0, j, T)
                gates(l, 0, T)
                for j in range(4):
                    ends = [0, SEQ + 1] + ([SEQ + 2, NT + 3] if T == NT else [])
                    for e in ends:
                        step(V.memset(ZP[:, e:e + 1], 0.0))
                    key = (l, "uc", j)
                    ps = ready(key)
                    own((l, "cc", j))
                    spans = [(0, SEQ, 1)] + ([(SEQ, CTX, SEQ + 3)] if T == NT else [])
                    for t0, tn, z0 in spans:
                        ins = V.tensor_tensor(ZP[:, z0:z0 + tn], CU[:, t0:t0 + tn], ps[:, t0:t0 + tn], ALU.mult)
                        if (t0, tn, z0) != spans[-1]:
                            step(ins)
                    ins.then_inc(*freed(key))
                    own(key)
                    for tap in range(3):
                        w = vec("conv1", l, 4 * tap + j)
                        for t0, tn, z0 in spans:
                            z = ZP[:, z0 + tap - 1:z0 + tap - 1 + tn]
                            c = CV[:, t0:t0 + tn]
                            step(V.tensor_scalar(c, z, w, None, ALU.mult) if tap == 0 else
                                 V.scalar_tensor_tensor(c, z, w, c, ALU.mult, ALU.add))
                    key = (l, "bc", j)
                    ps = ready(key)
                    V.tensor_tensor(CV[:, 0:T], CV[:, 0:T], ps[:, 0:T], ALU.mult).then_inc(*freed(key))
                    own(key)
                    own((l, "zc", j))
                    gv = value((l, "y", 2, j))
                    V.tensor_tensor(gv[:, 0:T], CV[:, 0:T], SZ[j % 2][:, 0:T], ALU.mult).then_inc(
                        *valued((l, "y", 2, j)))
                    dve.wait_ge(split_value, led.count[split_value.name])
                gates(l, 2, T)
                norm((l, "post"), KD, SQ, ACC, RSTD, T)
                for m in range(KD):
                    own((l, "o", m))
                    for s, (t0, tn) in enumerate(segs(T)):
                        o = OUT[:, m, t0:t0 + tn]
                        step(V.scalar_tensor_tensor(o, o, GG[:, m, s:s + 1], RSTD[:, t0:t0 + tn], ALU.mult, ALU.mult))
                        x = XT[:, m, t0:t0 + tn]
                        step(V.tensor_tensor(x, x, o, ALU.add), (l, "x", m) if t0 + tn == T else None)

            for l in range(DEPTH):
                first_layer(l)
                if stop == ("first", l):
                    break

            def norm2(l, i):
                norm(("2", l, "n", i), KD, SQ2, ACC2, RSTD2, SEQ)
                for k in range(KD):
                    step(V.tensor_scalar(SC[:, k:k + 1], MOD2[l][:, 24 * i + KD + k:24 * i + KD + k + 1], 1.0,
                                         vec("norm2", l, KD * i + k), ALU.add, ALU.mult))
                for k in range(KD):
                    key = ("2", l, "h", i, k)
                    gv = value(key)
                    step(V.tensor_tensor(gv[:, 0:SEQ], XT[:, k, 0:SEQ], RSTD2[:, :], ALU.mult))
                    V.tensor_scalar(gv[:, 0:SEQ], gv[:, 0:SEQ], SC[:, k:k + 1],
                                    MOD2[l][:, 24 * i + k:24 * i + k + 1], ALU.mult, ALU.add).then_inc(*valued(key))

            def heads2(l, a):
                for j in range(4):
                    dst = Q2[:, j, :] if j < 3 else K2[:, :]
                    gain = vec(f"{a}_q_norm_2" if j < 3 else f"{a}_k_norm_2", l)
                    key = ("2", l, a, j, "sum")
                    own(("2", l, a + "q", j))
                    own(key)
                    rs = RS2[j % 2]
                    step(V.reciprocal(rs[:, :], rs[:, :]))
                    if j < 3:
                        step(V.tensor_scalar(rs[:, :], rs[:, :], 0.125, None, ALU.mult))
                    if a == "a":
                        V.scalar_tensor_tensor(QR2[j % 2][:, :], QR2[j % 2][:, :], gain, rs[:, :], ALU.mult,
                                               ALU.mult).then_inc(*up(to_pe, ("2", l, a, j, "n")))
                        dve.wait_ge(to_pe, led.count[to_pe.name])
                        dve.wait_ge(const2_in, 32)
                        key = ("2", l, a, j, "rot")
                        ps = ready(key)
                        step(V.tensor_tensor(TA2[:, :], QR2[j % 2][:, :], ROPE[:, 0:SEQ], ALU.mult))
                        V.tensor_tensor(TB2[:, :], ps[:, 0:SEQ], ROPE[:, SEQ:2 * SEQ], ALU.mult).then_inc(*freed(key))
                        own(key)
                        V.tensor_tensor(dst, TA2[:, :], TB2[:, :], ALU.add).then_inc(*up(to_pe, ("2", l, a, j)))
                    else:
                        V.scalar_tensor_tensor(dst, QR2[j % 2][:, :], gain, rs[:, :], ALU.mult,
                                               ALU.mult).then_inc(*up(to_pe, ("2", l, a, j)))
                    dve.wait_ge(to_pe, led.count[to_pe.name])
                us = [(h, qb, 0, SEQ, 0) for h in range(HEADS_2) for qb in range(NXB)]
                if a == "c":
                    dve.wait_ge(bias_in, 16 * (l + 1))
                attention(a, l, us, 0, (0, 1) if a == "c" else (1, 2),
                          lambda u: Y2[:, u[1], u[0] * 64:u[0] * 64 + 64])
                for j in range(3):
                    key = ("2", l, a + "yT", j)
                    ps = ready(key)
                    gv = value(("2", l, "mix", a, j))
                    V.tensor_copy(gv[:, 0:SEQ], ps[:, 0:SEQ]).then_inc(*freed(key))
                    own(key)

            def recurrence(l):
                step(V.memset(ONE_ROW[:, :], 1.0))
                lbv = LB[:, 24 + 4 * l:28 + 4 * l]
                step(V.tensor_scalar(SMALL[:, 8:12], lbv, -1.0, 1.0, ALU.mult, ALU.add))
                for n in range(4):
                    own(("2", l, ("bff", "bfb")[n // 2], n % 2))
                    f = FS[:, n, :]
                    step(V.tensor_scalar(f, f, SMALL[:, 8 + n:9 + n], lbv[:, n:n + 1], ALU.mult, ALU.add))
                    V.tensor_scalar(f, f, F_MIN, None, ALU.max).then_inc(*up(to_act, ("2", l, "f", n)))
                    dve.wait_ge(to_act, led.count[to_act.name])
                    V.tensor_scalar(KK[:, n, :], f, -1.0, 1.0, ALU.mult, ALU.add).then_inc(*up(to_pool, ("2", l, "kk", n)))
                    dve.wait_ge(to_pool, led.count[to_pool.name])
                for n in range(4):
                    dve.wait_ge(act_out, at(act_out, ("2", l, "lf", n)))
                    for c in range(NXB):
                        cs = slice(c * P, (c + 1) * P)
                        step(V.tensor_tensor_scan(FS[:, n, cs], ONE_ROW[:, :], LF[:, n, cs], 0.0, ALU.mult, ALU.add))
                    ends = FS[:, n, :].rearrange("p (c t) -> p c t", t=P)[:, :, P - 1:P]
                    step(V.tensor_copy(SMALL[:, 16 + 4 * n:20 + 4 * n].rearrange("p (c o) -> p c o", o=1), ends))
                    if n >= 2:
                        step(V.tensor_tensor(FS[:, n, :], FS[:, n, :], LF[:, n, :], ALU.subtract))
                dve.wait_ge(masks_in, 16 * (l + 1))
                for t in range(2):
                    if t:
                        dve.wait_ge(product_ready, at(product_ready, ("2", l, "pv", 0, 1)))
                    for h in range(2):
                        step(V.memset(DIAG[h][:, :, :], 0.0))
                    for d in range(2):
                        n = 2 * d + t
                        for i, half in enumerate(LEVELS):
                            pref = PREF(n).rearrange("p (b w) -> p b w", w=2 * half)
                            r = half - 1 + d
                            ref = pref[:, :, r:r + 1].to_broadcast([P, SEQ // (2 * half), 2 * half])
                            dd = DD[i % 2]
                            if i >= 2:
                                dve.wait_ge(act_out, at(act_out, ("2", l, "ee", t, d, i - 2)))
                            ins = V.tensor_tensor(dd[:, :].rearrange("p (b w) -> p b w", w=2 * half), pref, ref, ALU.subtract)
                            if i:
                                step(ins)
                                ins = V.scalar_tensor_tensor(dd[:, :], dd[:, :], -1.0, dd[:, :], ALU.mult, ALU.max)
                            if i:
                                dve.wait_ge(pool_out, at(pool_out, ("2", l, "kp", t, d, i - 1)))
                            ins.then_inc(*up(to_act, ("2", l, "dd", t, d, i)))
                            if i == 0:
                                dve.wait_ge(act_out, at(act_out, ("2", l, "ee", t, d, "q")))
                                e = EE[0]
                            else:
                                dve.wait_ge(act_out, at(act_out, ("2", l, "ee", t, d, i)))
                                e = EE[(i + 1) % 2]
                            own(("2", l, "bq", t))
                            if i >= 2:
                                dve.wait_ge(product_ready, at(product_ready, ("2", l, "lev", t, d, i - 2, 1)))
                            elif (t, d) != (0, 0):
                                td = (t, d - 1) if d else (t - 1, 1)
                                dve.wait_ge(product_ready, at(product_ready, ("2", l, "lev") + td + (4, 1)))
                            V.tensor_tensor(QP[i % 2][:, :], QH[:, t, :], e[:, :], ALU.mult).then_inc(
                                *up(to_pe, ("2", l, "qp", t, d, i)))
                            dve.wait_ge(to_pe, led.count[to_pe.name])
                            for h in range(2):
                                key = ("2", l, "lev", t, d, i, h)
                                ps = ready(key)
                                mask = HMASK[:, (5 * d + i) * P:(5 * d + i + 1) * P]
                                mask = mask.rearrange("p (o t) -> p o t", o=1).to_broadcast([P, 4, P])
                                V.copy_predicated(DIAG[h][:, d, :].rearrange("p (c t) -> p c t", t=P), mask,
                                                  ps[:, 0:SEQ].rearrange("p (c t) -> p c t", t=P)).then_inc(*freed(key))
                                own(key)
                        pref = PREF(n).rearrange("p (c t) -> p c t", t=P)
                        tot = SMALL[:, 16 + 4 * n:20 + 4 * n]
                        end = tot.rearrange("p (c o) -> p c o", o=1).to_broadcast([P, 4, P])
                        dve.wait_ge(pool_out, at(pool_out, ("2", l, "kp", t, d, 4)))
                        V.tensor_tensor(DD[1][:, :].rearrange("p (c t) -> p c t", t=P), pref, end, ALU.subtract).then_inc(
                            *up(to_act, ("2", l, "dx", t, d)))
                        dve.wait_ge(act_out, at(act_out, ("2", l, "ex", t, d, 2)))
                        q_e, k_e = (EE[0], EE[1]) if d == 0 else (EE[1], EE[0])
                        q, k = QPX[:, 2 * d, :], QPX[:, 2 * d + 1, :]
                        if (t, d) != (0, 0):
                            td = (t, d - 1) if d else (t - 1, 1)
                            dve.wait_ge(product_ready, at(product_ready, ("2", l, "cross") + td + (1,)))
                        step(V.tensor_tensor(q, QH[:, t, :], q_e[:, :], ALU.mult))
                        step(V.tensor_tensor(k, KK[:, n, :], k_e[:, :], ALU.mult))
                        qc, kc = (3, 0) if d == 0 else (0, 3)
                        q_tot, k_tot = (2, 1) if d == 0 else (1, 2)
                        step(V.tensor_scalar(QX[:, :], q[:, qc * P:(qc + 1) * P], EX[:, n, q_tot:q_tot + 1], None, ALU.mult))
                        V.tensor_scalar(KX[:, :], k[:, kc * P:(kc + 1) * P], EX[:, n, k_tot:k_tot + 1], None,
                                        ALU.mult).then_inc(*up(to_pe, ("2", l, "cross", t, d)))
                        dve.wait_ge(to_pe, led.count[to_pe.name])
                        for h in range(2):
                            key = ("2", l, "cross", t, d, h)
                            ps = ready(key)
                            V.tensor_copy(OFF[h][:, d, :], ps[:, 0:768]).then_inc(*freed(key))
                            own(key)
                    for h in range(2):
                        key = ("2", l, "pv", t, h)
                        ps = ready(key)
                        col = (2 * t + h) * 64
                        V.tensor_copy(OTOK[:, :, col:col + 64], ps[:, 0:256].rearrange("p (b v) -> p b v", v=64)).then_inc(
                            *freed(key))
                        own(key)
                step(V.tensor_tensor(OSQ[:, :], OTOK[:, :, :].rearrange("p b v -> p (b v)"),
                                     OTOK[:, :, :].rearrange("p b v -> p (b v)"), ALU.mult))
                V.tensor_reduce(smalls[:, 24:40], OSQ[:, :].rearrange("p (g v) -> p g v", v=64), AX.X, ALU.add).then_inc(
                    *up(to_act, ("2", l, "oss")))
                dve.wait_ge(act_out, at(act_out, ("2", l, "oss")))
                step(V.reciprocal(smalls[:, 24:40], smalls[:, 24:40]))
                o3 = OTOK[:, :, :].rearrange("p b (h v) -> p (b h) v", v=64)
                V.tensor_tensor(o3, o3, smalls[:, 24:40].rearrange("p (g o) -> p g o", o=1).to_broadcast([P, 16, 64]),
                                ALU.mult).then_inc(*up(to_pe, ("2", l, "otok")))
                for j in range(2):
                    key = ("2", l, "byT", j)
                    ps = ready(key)
                    own(("2", l, "bg", j))
                    gv = value(("2", l, "mix", "b", j))
                    V.scalar_tensor_tensor(gv[:, 0:SEQ], ps[:, 0:SEQ], vec("b_out_norm_2", l), SZ2[j][:, :],
                                           ALU.mult, ALU.mult).then_inc(*freed(key))
                    own(key)

            def second_layer(l):
                for k in range(48):
                    own(("mod2", l, k))
                norm2(l, 0)
                recurrence(l)
                heads2(l, "a")
                heads2(l, "c")
                for m in range(KD):
                    key = ("2", l, "out", m)
                    ps = ready(key)
                    x = XT[:, m, 0:SEQ]
                    V.scalar_tensor_tensor(x, ps[:, 0:SEQ], MOD2[l][:, 16 + m:17 + m], x, ALU.mult, ALU.add).then_inc(
                        *freed(key))
                    own(key)
                norm2(l, 1)
                for j in range(KF):
                    for s in range(2):
                        key = ("2", l, "up", j, s)
                        U = (UA, UB)[s]
                        c = s * KF + j
                        dve.wait_ge(act_out, at(act_out, ("2", l, "u", j, s)))
                        ps = psum[led.slot(key)]
                        step(V.scalar_tensor_tensor(U[:, 1:SEQ], ps[:, 0:SEQ - 1], vec("conv2", (l, 0), c), U[:, 1:SEQ],
                                                    ALU.mult, ALU.add))
                        V.scalar_tensor_tensor(U[:, 0:SEQ - 1], ps[:, 1:SEQ], vec("conv2", (l, 2), c), U[:, 0:SEQ - 1],
                                               ALU.mult, ALU.add).then_inc(*freed(key))
                        own(key)
                    dve.wait_ge(act_out, at(act_out, ("2", l, "silu", j)))
                    gv = value(("2", l, "f", j))
                    V.tensor_tensor(gv[:, 0:SEQ], UA[:, :], UB[:, :], ALU.mult).then_inc(*valued(("2", l, "f", j)))
                    dve.wait_ge(split_value, led.count[split_value.name])
                for m in range(KD):
                    key = ("2", l, "down", m)
                    dve.wait_ge(product_ready, at(product_ready, ("2", l, "down", m, 2)))
                    ps = psum[led.slot(key)]
                    x = XT[:, m, 0:SEQ]
                    V.scalar_tensor_tensor(x, ps[:, 0:SEQ], MOD2[l][:, 40 + m:41 + m], x, ALU.mult, ALU.add).then_inc(
                        *freed(key))
                    own(key)

            if stop is None or stop[0] == "second":
                for l in range(DEPTH):
                    second_layer(l)
                    if stop == ("second", l):
                        break
    return led.events


LAYOUT = dict(
    x=(SEQ, DM), ctx=(CTX, DM), sink=(1, DEPTH * HEADS_A),
    c=(8, P), c_ctx=(8, P), c_2=(8, P), b_lb_2=(8, P),
    b_mod=(48, P), g_pre=(16, P), g_post=(16, P), g_qa=(6, P), g_kva=(4, P), conv_w=(24, P),
    b_ada_2=(96, P), norm_g_2=(32, P), conv_b_2=(88, P), conv_w_2=(264, P),
    a_q_norm_2=(2, 64), a_k_norm_2=(2, 64), b_out_norm_2=(2, 64), c_q_norm_2=(2, 64), c_k_norm_2=(2, 64),
    w_mod=(DEPTH * DM, 3 * DM), w_in=(DEPTH * DM, 7584), w_qb=(DEPTH * 384, 768), w_kvb=(DEPTH * 256, 1024),
    w_branch=(DEPTH * 3 * 512, DM), w_o=(DEPTH * DM, DM), w_ada_2=(DEPTH * DM, 6 * DM),
    w_in_2=(DEPTH * DM, 2560), w_out_2=(DEPTH * DM, DM), w_up_2=(DEPTH * DM, 2 * DFF), w_down_2=(DEPTH * DFF, DM),
)

STOP = None


def kernel(**inputs):
    import concourse.bacc as bacc
    from concourse.bass_utils import run_bass_kernel_spmd as run

    arrays = {f"in_{k}": np.ascontiguousarray(np.asarray(inputs[k]).reshape(shape)) for k, shape in LAYOUT.items()}
    for k, a in zip(("const1", "const2", "bias", "masks"), constants()):
        arrays[f"in_{k}"] = a

    def build(known):
        nc = bacc.Bacc("TRN2", target_bir_lowering=False, num_devices=1)
        D = {k[3:]: nc.dram_tensor(k, a.shape, mybir.dt.from_np(a.dtype), kind="ExternalInput").ap()
             for k, a in arrays.items()}
        out = nc.dram_tensor("out", (SEQ, DM), F32, kind="ExternalOutput").ap()
        return nc, program(nc, D, out, known, STOP)

    _, counts = build({})
    nc, _ = build(counts)
    r = run(nc, [arrays], core_ids=[0])
    return np.asarray(r.results[0]["out"]).reshape(1, SEQ, DM)
```

```python
import numpy as np
import concourse.bass as bass
from concourse import mybir
from contextlib import ExitStack

F32 = mybir.dt.float32
F32R = mybir.dt.float32r
I32 = mybir.dt.int32
ALU = mybir.AluOpType
ACT = mybir.ActivationFunctionType
AX = mybir.AxisListType

P = 128
DM = 1024
KD = DM // P
SEQ = 512
CTX = 256
NT = SEQ + CTX
NXB = SEQ // P
NTB = NT // P
DEPTH = 2
EPS = 1e-6
ARENA_KB = 207
NEG = -1e30

IN1 = dict(qa=0, ka=512, va=640, za=768, qlb=1280, kvlb=1664, krb=1920, zb=1952,
           bc=2464, cc=2976, uc=3488, zc=4000, g0=4512, g1=5536, g2=6560)
Z1 = ("za", "zb", "zc")
HEADS_A, HEADS_B = 8, 8
SCALE_B = float(96) ** -0.5
IN2 = dict(aq=0, ak=384, av=512, bq=640, bff=896, bfb=1152, bi=1408, bg=1664,
           cq=1920, ck=2304, cv=2432)
DFF = 2816
KF = DFF // P
HEADS_2 = 6
F_MIN = 1e-6
LEVELS = (4, 8, 16, 32, 64)

def vector_rows():
    rows = []

    def add(name, key, source, start, n):
        rows.append((name, key, source, start, n))

    add("c", 0, "c", 0, 8)
    add("c", 1, "c_ctx", 0, 8)
    add("c2", 0, "c_2", 0, 8)
    add("b_lb", 0, "b_lb_2", 0, 8)
    for l in range(DEPTH):
        add("b_mod", l, "b_mod", 24 * l, 24)
        add("g_pre", l, "g_pre", 8 * l, 8)
        add("g_post", l, "g_post", 8 * l, 8)
        add("g_qa", l, "g_qa", 3 * l, 3)
        add("g_kva", l, "g_kva", 2 * l, 2)
        add("conv1", l, "conv_w", 12 * l, 12)
    for l in range(DEPTH):
        add("b_ada", l, "b_ada_2", 48 * l, 48)
        add("norm2", l, "norm_g_2", 16 * l, 16)
        for g in ("a_q_norm_2", "a_k_norm_2", "b_out_norm_2", "c_q_norm_2", "c_k_norm_2"):
            add(g, l, g, l, 1)
    for l in range(DEPTH):
        add("conv_b", l, "conv_b_2", 44 * l, 44)
        for tap in range(3):
            add("conv2", (l, tap), "conv_w_2", 132 * l + 44 * tap, 44)
    batches, used = [], P + 1
    column = {}
    for name, key, source, start, n in rows:
        if used + n > P:
            batches.append([])
            used = 0
        batches[-1].append((used, source, start, n))
        column[name, key] = P * (len(batches) - 1) + used
        used += n
    return batches, column


VECTOR_BATCHES, COLUMN = vector_rows()
VCOLS = P * len(VECTOR_BATCHES)


def rope_tables(half, theta_dim, rows):
    pos_row = np.repeat(np.arange(rows, dtype=np.float32), 64)
    pos_col = np.tile(np.arange(64, dtype=np.float32), rows)
    inv = (np.float32(10000.0) ** (-np.arange(0, theta_dim, 2, dtype=np.float32) / np.float32(theta_dim))).astype(np.float32)
    return pos_row, pos_col, inv


def constants():
    ident = np.eye(P, dtype=np.float32)
    ones = np.ones((P, P), np.float32)
    blocks = np.kron(np.eye(2, dtype=np.float32), np.ones((64, 64), np.float32))

    def rotation(n, group):
        half = group // 2
        r = np.zeros((n, n), np.float32)
        for g in range(0, n, group):
            for i in range(half):
                r[g + i, g + half + i] = -1.0
                r[g + half + i, g + i] = 1.0
        return np.ascontiguousarray(r.T)

    rows = SEQ // 64

    def joint(rot_dim):
        row, col, inv = rope_tables(None, rot_dim // 2, rows)
        return np.concatenate([row[:, None] * inv, col[:, None] * inv], axis=-1).astype(np.float32).T

    ang = joint(64)
    ang_a = np.concatenate([ang, ang, ang, ang], 0)
    ang = joint(32)
    ang_b = np.zeros((P, SEQ), np.float32)
    ang_b[64:96] = np.concatenate([ang, ang], 0)
    rot_b = np.zeros((P, 32), np.float32)
    rot_b[64:96] = rotation(32, 32)
    q = np.arange(P)[:, None]
    k = np.arange(P)[None, :]
    prev = np.where(k >= q, 0.0, NEG).astype(np.float32)
    after = np.where(k <= q, 0.0, NEG).astype(np.float32)
    one = np.concatenate([ident, ones, blocks, rotation(P, 64), rot_b, prev, after,
                          np.cos(ang_a), np.sin(ang_a), np.cos(ang_b), np.sin(ang_b)], 1)
    row, col, inv = rope_tables(None, 32, rows)
    ar, ac = (row[:, None] * inv).astype(np.float32).T, (col[:, None] * inv).astype(np.float32).T
    ang_2 = np.concatenate([ar, ar, ac, ac] * 2, 0)
    two = np.concatenate([rotation(P, 32), np.cos(ang_2), np.sin(ang_2)], 1)
    d = np.arange(896)[None, :] - 384 - np.arange(P)[:, None]
    count = np.zeros(d.shape, np.float64)
    for w, r in ((128, 1), (512, 4), (2048, 16)):
        count += (np.abs(d) <= r * (w // (2 * r))) & (d % r == 0)
    slopes = (2.0 ** (-8.0 * np.arange(1, HEADS_2 + 1) / HEADS_2)).astype(np.float32)
    bias = [np.where(count > 0, -float(s) * np.abs(d) + np.log(np.maximum(count, 1)), NEG) for s in slopes]
    bias = np.concatenate(bias, 1)
    s, t = np.arange(P)[:, None], np.arange(P)[None, :]
    masks = [(s <= t) & (s // 8 == t // 8)]
    for h in LEVELS[1:]:
        masks.append((s // (2 * h) == t // (2 * h)) & (s % (2 * h) < h) & (t % (2 * h) >= h))
    masks = masks + [m.T for m in masks]
    masks = np.concatenate(masks, 1).astype(np.int32)
    return (np.ascontiguousarray(one, np.float32), np.ascontiguousarray(two, np.float32),
            np.ascontiguousarray(bias, np.float32), np.ascontiguousarray(masks))


CHUNK = 1024
CHUNK_PARTS = (range(0, 3), range(3, 6), range(6, KD))
MOD1_CHUNKS, MOD2_CHUNKS = 3 * DM // CHUNK, 6 * DM // CHUNK
LATER_CHUNKS = [("mod1", 1, c) for c in range(MOD1_CHUNKS)] + \
    [("mod2", l, c) for l in range(DEPTH) for c in range(MOD2_CHUNKS)]


class Ledger:

    def __init__(self, known):
        self.known, self.events, self.count = known, {}, {}

    def up(self, sem, key=None):
        n = self.count[sem.name] = self.count.get(sem.name, 0) + 1
        if key is not None:
            assert (sem.name, key) not in self.events, (sem.name, key)
            self.events[sem.name, key] = n
        return sem, 1

    def at(self, sem, key):
        if sem.name.startswith("evacuated"):
            return self.events["use", key]
        return self.known[sem.name, key] if self.known else 1

    def slot(self, key):
        return self.events["slot", key]


def program(nc, D, out, known, stop=None):
    led = Ledger(known)
    up, at = led.up, led.at
    ctx = ExitStack()
    with ctx:
        BASE = 16544
        ctx.enter_context(nc.sbuf_tensor("arena", [P, ARENA_KB * 256], F32))

        def place(name, shape, kb, dt=F32):
            return nc.alloc_sbuf_tensor_at(name, shape, dt, offset=BASE + int(kb * 1024))

        XT = place("XT", [P, KD, NT], 0)
        R0 = 24
        HH = place("HH", [P, KD, NT], R0, F32R)
        HL = place("HL", [P, KD, NT], R0 + 24, F32R)
        XIN = place("XIN", [P, NTB, DM], R0)
        OUT = place("OUT", [P, KD, NT], R0)
        XOUT = place("XOUT", [P, NXB, DM], R0)
        MA = R0 + 48
        MACC = place("MACC", [P, KD, NT], MA)
        MH = place("MH", [P, KD, NT], MA, F32R)
        WK = MA + 24
        RAWK = WK + 60
        NRAW, NWS = 3, 2
        RAW = [place(f"RAW{i}", [P, 1024], RAWK + 4 * i) for i in range(NRAW)]
        WH = [place(f"WH{i}", [P, 1024], RAWK + 12 + 4 * i, F32R) for i in range(NWS)]
        WL = [place(f"WL{i}", [P, 1024], RAWK + 20 + 4 * i, F32R) for i in range(NWS)]
        GV = [place(f"GV{i}", [P, NT], RAWK + 28 + 3 * i) for i in range(2)]
        CK = RAWK + 34
        VEC = place("VEC", [P, VCOLS], CK)
        CK += VCOLS * 4 / 1024
        CONST = place("CONST", [P, 4 * P + 32 + 2 * P], CK)
        CK += (6 * P + 32) * 4 / 1024
        ROPE = place("ROPE", [P, 4 * SEQ], CK)
        CK += 8
        ident, ones, blockones, rot_a = (CONST[:, i * P:(i + 1) * P] for i in range(4))
        rot_b = CONST[64:96, 512:544]
        mask_prev, mask_next = CONST[:, 544:672], CONST[:, 672:800]
        cos_a, sin_a, cos_b, sin_b = (ROPE[:, i * SEQ:(i + 1) * SEQ] for i in range(4))
        ROT2 = place("ROT2", [P, P], CK); CK += .5
        SINK = place("SINK", [P, DEPTH * HEADS_A], CK); CK += .0625
        MOD1 = place("MOD1", [P, 24, 2], CK); CK += .1875
        MOD1b = place("MOD1b", [P, 24, 2], CK); CK += .1875
        MOD2 = [place(f"MOD2{i}", [P, 48], CK + .1875 * i) for i in range(2)]; CK += .375
        MOD1 = [MOD1, MOD1b]
        SCG = place("SCG", [P, KD, 2], CK); CK += .0625
        SC = place("SC", [P, 24], CK); CK += .125
        CS = place("CS", [P, 24], CK); CK += .125
        GG = place("GG", [P, KD, 2], CK); CK += .0625
        LB = place("LB", [P, 32], CK); CK += .125
        SMALL = place("SMALL", [P, 64], CK); CK += .25
        epsb = place("epsb", [P, 8], CK); CK += .0625
        assert CK <= ARENA_KB, CK
        nmax = [SMALL[:, i:i + 1] for i in range(2)]
        rowsum = [SMALL[:, 2 + i:3 + i] for i in range(2)]
        rowinv = [SMALL[:, 4 + i:5 + i] for i in range(3)]
        smalls = SMALL[:, 8:64]

        YH = place("YH", [P, 4, NT], WK, F32R)
        YL = place("YL", [P, 4, NT], WK + 12, F32R)
        YTOK = place("YTOK", [P, NTB, 512], WK + 24)
        SZ = [place(f"SZ{i}", [P, NT], WK + 36 + 3 * i) for i in range(2)]
        SG = [place(f"SG{i}", [P, NT], WK + 54 + 3 * i) for i in range(2)]
        TM = [place(f"TM{i}", [P, NT], WK + 48 + 3 * i) for i in range(2)]
        ML = place("ML", [P, KD, NT], WK + 24, F32R)
        SQ = [place(f"SQ{i}", [P, NT], WK + 48 + 3 * i) for i in range(2)]
        ACC = place("ACC", [P, NT], WK + 54)
        RSTD = place("RSTD", [P, NT], WK + 57)
        PR = [place(f"PR{i}", [P, NT], WK + 48 + 3 * i) for i in range(2)]
        PT = [place(f"PT{i}", [P, NT], WK + 54 + 3 * i) for i in range(2)]
        QNH = place("QNH", [P, 3, NT], MA, F32R)
        QNL = place("QNL", [P, 3, NT], MA + 9, F32R)
        KVNH = place("KVNH", [P, 2, NT], MA + 18, F32R)
        KVNL = place("KVNL", [P, 2, NT], WK, F32R)
        QB = [place(f"QB{i}", [P, NT], WK + 6 + 3 * i) for i in range(2)]
        KB = [place(f"KB{i}", [P, NT], WK + 12 + 3 * i) for i in range(2)]
        KR = place("KR", [P, NT], WK + 18)
        T1 = place("T1", [P, SEQ], WK + 21)
        QLRAW = place("QLRAW", [P, 5, NT], WK + 24)
        VB = place("VB", [P, NTB, 512], WK + 36)
        QA = place("QA", [P, 4, NT], WK)
        KA = place("KA", [P, NT], WK + 12)
        VA = place("VA", [P, NTB, P], WK + 15)
        QRAW = [place(f"QRAW{i}", [P, NT], WK + 18 + 3 * i) for i in range(2)]
        T1a = place("T1a", [P, SEQ], WK + 36)
        T2a = place("T2a", [P, SEQ], WK + 38)
        CU = place("CU", [P, NT], WK + 24)
        ZP = place("ZP", [P, NT + 4], WK + 27)
        CV = place("CV", [P, NT], WK + 31)
        MSUM = [place(f"MSUM{i}", [P, CHUNK], WK + kb) for i, kb in enumerate((36, 40, 44, 32))]
        VROWS = place("VROWS", [P, len(VECTOR_BATCHES) * P], WK)

        HH2 = place("HH2", [P, KD, SEQ], R0, F32R)
        HL2 = place("HL2", [P, KD, SEQ], R0 + 16, F32R)
        XH2 = place("MIXH", [P, KD, SEQ], R0 + 32, F32R)
        XL2 = place("MIXL", [P, KD, SEQ], R0 + 48, F32R)
        B0 = R0 + 64
        FH = place("FH", [P, KF, SEQ], R0 + 32, F32R)
        FL = place("FL", [P, KF, SEQ], R0 + 76, F32R)
        UA = place("UA", [P, SEQ], R0 + 120)
        UB = place("UB", [P, SEQ], R0 + 122)
        SQ2 = [place(f"SQ2{i}", [P, SEQ], R0 + 124 + 2 * i) for i in range(2)]
        ACC2 = place("ACC2", [P, SEQ], R0 + 128)
        RSTD2 = place("RSTD2", [P, SEQ], R0 + 130)
        Q2 = place("Q2", [P, 3, SEQ], B0)
        K2 = place("K2", [P, SEQ], B0 + 6)
        V2 = place("V2", [P, NXB, P], B0 + 8)
        Y2 = place("Y2", [P, NXB, 384], B0 + 10)
        P2 = [place(f"P2{i}", [P, SEQ], B0 + 16 + 2 * i) for i in range(2)]
        PT2 = [place(f"PT2{i}", [P, SEQ], B0 + 20 + 2 * i) for i in range(2)]
        S2 = [place(f"S2{i}", [P, SEQ], B0 + 24 + 2 * i) for i in range(2)]
        QR2 = [place(f"QR2{i}", [P, SEQ], B0 + 28 + 2 * i) for i in range(2)]
        SS2 = [place(f"SS2{i}", [P, SEQ], B0 + 32 + 2 * i) for i in range(2)]
        RS2 = [place(f"RS2{i}", [P, SEQ], B0 + 36 + 2 * i) for i in range(2)]
        TA2 = place("TA2", [P, SEQ], B0 + 40)
        TB2 = place("TB2", [P, SEQ], B0 + 42)
        CBIAS = place("CBIAS", [P, HEADS_2 * 896], B0 + 44)
        QH = place("QH", [P, 2, SEQ], B0)
        FS = place("FS", [P, 4, SEQ], B0 + 4)
        LF = place("LF", [P, 4, SEQ], B0 + 12)
        KK = place("KK", [P, 4, SEQ], B0 + 20)
        VH = place("VH", [P, NXB, 256], B0 + 28)
        QP = [place(f"QP{i}", [P, SEQ], B0 + 32 + 2 * i) for i in range(2)]
        KP = [place(f"KP{i}", [P, SEQ], B0 + 36 + 2 * i) for i in range(2)]
        DD = [place(f"DD{i}", [P, SEQ], B0 + 40 + 2 * i) for i in range(2)]
        EE = [place(f"EE{i}", [P, SEQ], B0 + 44 + 2 * i) for i in range(2)]
        DIAG = [place(f"DIAG{i}", [P, 2, SEQ], B0 + 48 + 4 * i) for i in range(2)]
        OFF = [place(f"OFF{i}", [P, 2, 768], B0 + 56 + 6 * i) for i in range(2)]
        OTOK = place("OTOK", [P, NXB, 256], R0 + 32)
        OSQ = place("OSQ", [P, NXB * 256], R0 + 36)
        HMASK = place("HMASK", [P, 10 * P], R0 + 40, I32)
        ONE_ROW = place("ONE_ROW", [P, P], R0 + 45)
        QX = place("QX", [P, P], R0 + 45.5)
        KX = place("KX", [P, P], R0 + 46)
        EX = place("EX", [P, 4, 4], R0 + 46.5)
        QPX = place("QPX", [P, 4, SEQ], R0 + 48)
        SZ2 = [place(f"SZ2{i}", [P, SEQ], R0 + 56 + 2 * i) for i in range(2)]

        psum = [ctx.enter_context(nc.psum_tensor(f"ps{g}", [P, 1024], F32)) for g in range(4)]

        def sem(name):
            return ctx.enter_context(nc.semaphore(name))

        product_ready = sem("product_ready")
        evacuated = [sem(f"evacuated{g}") for g in range(4)]
        loaded = [sem(f"loaded{i}") for i in range(NRAW)]
        w_high = sem("w_high")
        w_low = sem("w_low")
        split_value = sem("split_value")
        split_high = sem("split_high")
        split_low = sem("split_low")
        act_step = sem("act_step")
        dve_step = sem("dve_step")
        pool_step = sem("pool_step")
        const_in = sem("const_in")
        x_in = sem("x_in")
        vec_in = sem("vec_in")
        out_done = sem("out_done")
        const2_in = sem("const2_in")
        masks_in = sem("masks_in")
        mod_summed = sem("mod_summed")
        bias_in = sem("bias_in")
        to_act = sem("to_act")
        to_pe = sem("to_pe")
        to_pool = sem("to_pool")
        act_out = sem("act_out")
        probs_ready = sem("probs_ready")
        pool_out = sem("pool_out")

        units = []
        block = ctx.enter_context(nc.Block())

        def n_dmas(loads):
            return sum(2 if x[0] == "w_kvb_v" else 1 for x in loads)

        def used_columns(unit):
            return max((load[2] * load[5] if load[4] == load[5] or load[5] == P else 0)
                       + (load[6] if len(load) > 6 and load[4] == load[5] else 0) for load in unit[1])

        def at_split(key):
            return known["split", key] if known else 0

        def exponentials(eng, kind, l, n):
            if kind == "c":
                eng.wait_ge(probs_ready, at(probs_ready, (kind, l, n)))
            else:
                key = (kind, l, n, "s")
                eng.wait_ge(evacuated[led.slot(key)], at(evacuated[led.slot(key)], key))

        def vec(name, key, i=0):
            c = COLUMN[name, key] + i
            return VEC[:, c:c + 1]

        def segs(T):
            return [(0, SEQ)] if T == SEQ else [(0, SEQ), (SEQ, CTX)]

        def tokens(l):
            return NT if l == 0 else SEQ

        def attention_units(kind, l):
            got = []
            blocks = range(NTB) if l == 0 else range(NXB)
            if kind == "A":
                for qb in blocks:
                    for h in range(HEADS_A):
                        if qb < NXB:
                            lo, hi = max(qb - 1, 0), min(qb + 1, NXB - 1)
                            got.append((h, qb, lo * P, (hi - lo + 1) * P, CTX))
                        else:
                            got.append((h, qb, 0, 0, CTX))
            else:
                for h in range(HEADS_B):
                    for qb in blocks:
                        got.append((h, qb, 0, SEQ if qb < NXB else 0, CTX))
            return got

        def vectors_of(chunk):
            return (0, 1) if chunk[0] == "mod1" else (2,)

        def chunk_beside(l, b, m0):
            n = (l * 2 + 1 - b) * (KD // 2) + m0 // 2
            return LATER_CHUNKS[n] if b < 2 and n < len(LATER_CHUNKS) else None

        def levels_order():
            return [(d, t, i) for d in range(2) for t in range(2) for i in range(len(LEVELS) + 1)]

        def PREF(n):
            return FS[:, n, :]

        def pr_of(kind, n):
            return (PR if kind in "AB" else P2)[n % 2]

        def pt_of(kind, n):
            return (PT if kind in "AB" else PT2)[n % 2]

        def cross_blocks(d):
            q = [QPX[:, 2 * d, c * P:(c + 1) * P] for c in range(4)]
            k = [QPX[:, 2 * d + 1, c * P:(c + 1) * P] for c in range(4)]
            if d == 0:
                return [(q[1], k[0], 0, 1), (q[3], k[2], 2, 3), (q[2], KX, 0, 2), (QX, KX, 0, 3),
                        (q[2], k[1], 1, 2), (QX, k[1], 1, 3)]
            return [(q[0], k[1], 1, 0), (q[2], k[3], 3, 2), (QX, k[2], 2, 0), (q[1], k[2], 2, 1),
                    (QX, KX, 3, 0), (q[1], KX, 3, 1)]


        @block.tensor
        def _(pe):
            group = [0]
            uses = [0] * 4
            raw_n, gemm_n = [0], [0]

            def open_group(key, g=None):
                if g is None:
                    g = group[0] % 4
                    group[0] += 1
                led.events["slot", key] = g
                if uses[g]:
                    pe.wait_ge(evacuated[g], uses[g])
                uses[g] += 1
                led.events["use", key] = uses[g]
                return psum[g]

            def take(key, loads):
                n = len(units)
                s = sum(1 for u in units if u[2])
                units.append((key, loads, True))
                led.events["unit", key] = n
                pe.wait_ge(w_low, s + 1)
                return WH[s % NWS], WL[s % NWS]

            def given_back(key):
                led.events["unit_used", key] = led.count[product_ready.name]

            def channels(ps, unit, kt, c0, width, H, L, T, k0=0, first=True, last=True, stride=P, new=None):
                wh, wl = unit
                for k in range(kt):
                    if new is not None:
                        pe.wait_ge(split_low, at(split_low, new(k0 + k)))
                    w = [x[:, k * stride + c0:k * stride + c0 + width] for x in (wh, wl)]
                    for i, (a, b) in enumerate(((w[0], H), (w[0], L), (w[1], H))):
                        for t0, tn in segs(T):
                            ins = nc.tensor.matmul(ps[0:width, t0:t0 + tn], a, b[:, k0 + k, t0:t0 + tn],
                                                   start=first and k == 0 and i == 0,
                                                   stop=last and k == kt - 1 and i == 2)
                return ins

            def token_major(ps, unit, kt, width, H, L, tb, off=0, stride=P):
                wh, wl = unit
                for k in range(kt):
                    w = [x[:, k * stride:k * stride + width] for x in (wh, wl)]
                    for i, (a, b) in enumerate(((H, w[0]), (H, w[1]), (L, w[0]))):
                        ins = nc.tensor.matmul(ps[:, off:off + width], a[:, k, tb * P:(tb + 1) * P], b,
                                               start=k == 0 and i == 0, stop=k == kt - 1 and i == 2)
                return ins

            def w_in1(key, l, col):
                return take(key, [("w_in", l * DM, KD, col, P, P)])

            def gemm1(l, name, j, col, T, width=P, new=None):
                unit = w_in1((l, name, j), l, col)
                ps = open_group((l, name, j))
                channels(ps, unit, KD, 0, width, HH, HL, T, new=new).then_inc(*up(product_ready, (l, name, j)))
                given_back((l, name, j))

            def modulation_units(chunk, rows):
                name, l, c = chunk
                source = "w_mod" if name == "mod1" else "w_ada_2"
                for k in rows:
                    key = chunk + (k,)
                    led.events["unit", key] = len(units)
                    units.append((key, [(source, l * DM + k * P, 1, c * CHUNK, CHUNK, CHUNK)], False))

            def modulation_columns(chunk, slot):
                pe.wait_ge(mod_summed, at(mod_summed, chunk + (KD - 1,)))
                ps = open_group(chunk)
                for v in range(len(vectors_of(chunk))):
                    for j in range(CHUNK // P):
                        c = v * CHUNK // P + j
                        ins = nc.tensor.matmul(ps[:, c:c + 1], MSUM[slot + v][:, j * P:(j + 1) * P],
                                               ones[:, 0:1], start=True, stop=True)
                ins.then_inc(*up(product_ready, chunk))

            def norm_sum(key, acc, T, mat=ones):
                pe.wait_ge(to_pe, at(to_pe, key))
                ps = open_group(key)
                for t0, tn in segs(T):
                    ins = nc.tensor.matmul(ps[:, t0:t0 + tn], mat, acc[:, t0:t0 + tn], start=True, stop=True)
                ins.then_inc(*up(product_ready, key))

            def attention(kind, l, us, q_of, k_of, v_of, ready, piece=None):
                def scores(n):
                    h, qb, k0, nloc, nctx = us[n]
                    ready(n, "scores")
                    ps = open_group((kind, l, n, "s"), n % 2)
                    q, pieces, at_col = q_of(n), [], 0
                    for start, length in ((k0, nloc), (SEQ, nctx)):
                        while length:
                            m = min(length, 512 - at_col % 512)
                            pieces.append((at_col, start, m))
                            at_col, start, length = at_col + m, start + m, length - m
                    for c, start, m in pieces:
                        ins = nc.tensor.matmul(ps[:, c:c + m], q, k_of(n, start, m), start=True, stop=True)
                    ins.then_inc(*up(product_ready, (kind, l, n, "s")))

                def transposes(n):
                    h, qb, k0, nloc, nctx = us[n]
                    kb = (nloc + nctx) // P
                    exponentials(pe, kind, l, n)
                    ps = open_group((kind, l, n, "t"), 2)
                    pr = pr_of(kind, n)
                    for b in range(kb):
                        ins = nc.tensor.transpose(ps[:, b * P:(b + 1) * P], pr[:, b * P:(b + 1) * P], ident)
                    ins.then_inc(*up(product_ready, (kind, l, n, "t")))

                def values(n):
                    h, qb, k0, nloc, nctx = us[n]
                    kb = (nloc + nctx) // P
                    got((kind, l, n, "t"))
                    ps = open_group((kind, l, n, "o"), 3)
                    ready(n, "values")
                    pt = pt_of(kind, n)
                    for b in range(kb):
                        start = k0 + b * P if b * P < nloc else SEQ + b * P - nloc
                        ins = nc.tensor.matmul(ps[:, 0:64], pt[:, b * P:(b + 1) * P], v_of(n, start // P),
                                               start=b == 0, stop=b == kb - 1)
                    ins.then_inc(*up(product_ready, (kind, l, n, "o")))

                N = len(us)
                for n in range(N + 2):
                    if n < N:
                        scores(n)
                    extra_piece = piece is not None and piece(n)
                    if n >= 2 and not extra_piece:
                        values(n - 2)
                    if 1 <= n <= N:
                        transposes(n - 1)
                    if n >= 2 and extra_piece:
                        values(n - 2)

            def got(key):
                g = led.slot(key)
                pe.wait_ge(evacuated[g], at(evacuated[g], key))

            def head(h):
                return slice(64 * (h // 4), 64 * (h // 4) + 64)

            pe.wait_ge(const_in, 48)
            pe.wait_ge(x_in, 32)
            for k in range(KD):
                ps = open_group(("xT", k))
                for tb in range(NTB):
                    ins = nc.tensor.transpose(ps[:, tb * P:(tb + 1) * P], XIN[:, tb, k * P:(k + 1) * P], ident)
                ins.then_inc(*up(product_ready, ("xT", k)))
            pe.wait_ge(vec_in, 16 * sum(len(b) for b in VECTOR_BATCHES) + 16 * 10)
            for b in range(len(VECTOR_BATCHES)):
                ps = open_group(("vec", b))
                nc.tensor.transpose(ps[:, 0:P], VROWS[:, b * P:(b + 1) * P], ident).then_inc(
                    *up(product_ready, ("vec", b)))
            pe.wait_ge(act_out, at(act_out, "silu_c"))
            for c in range(MOD1_CHUNKS):
                modulation_units(("mod1", 0, c), range(KD))
            for c in range(MOD1_CHUNKS):
                modulation_columns(("mod1", 0, c), 2 * (c % 2))

            def merge(l, b, T):
                for j in range(4):
                    gemm1(l, Z1[b], j, IN1[Z1[b]] + j * P, T)
                    if b < 2:
                        if j == 0:
                            last = len(attention_units("AB"[b], l)) - 1
                            got(("AB"[b], l, last, "o"))
                        ps = open_group((l, "yT", b, j))
                        for tb in range(T // P):
                            ins = nc.tensor.transpose(ps[:, tb * P:(tb + 1) * P],
                                                      YTOK[:, tb, j * P:(j + 1) * P], ident)
                        ins.then_inc(*up(product_ready, (l, "yT", b, j)))
                branch(l, b, T)

            def branch(l, b, T):
                for m0 in range(0, KD, 2):
                    chunk = chunk_beside(l, b, m0)
                    unit = take((l, "wb", b, m0), [("w_branch", (l * 3 + b) * 512, 4, m0 * P, 2 * P, 2 * P)])
                    for m in (m0, m0 + 1):
                        ps = open_group((l, "br", b, m))
                        channels(ps, unit, 4, (m % 2) * P, P, YH, YL, T, stride=2 * P,
                                 new=None if m else lambda k: (l, "y", b, k)).then_inc(
                            *up(product_ready, (l, "br", b, m)))
                    given_back((l, "wb", b, m0))
                    for m in (m0, m0 + 1):
                        if chunk:
                            modulation_units(chunk, CHUNK_PARTS[m - m0])
                        gemm1(l, f"g{b}", m, IN1[f"g{b}"] + m * P, T)
                    if chunk:
                        modulation_units(chunk, CHUNK_PARTS[2])
                        modulation_columns(chunk, 0)

            def first_layer(l):
                T = tokens(l)
                norm_sum((l, "pre"), ACC, NT)
                for j in range(3):
                    gemm1(l, "qlb", j, IN1["qlb"] + j * P, T, new=None if j else lambda k: (l, "h", k))
                for j in range(2):
                    gemm1(l, "kvlb", j, IN1["kvlb"] + j * P, NT)
                gemm1(l, "krb", 0, IN1["krb"] - 64, NT, width=96)
                norm_sum((l, "qlb"), ACC, T)
                norm_sum((l, "kvlb"), ACC, NT)
                got((l, "krb", 0))
                ps = open_group((l, "kr_rot"))
                nc.tensor.matmul(ps[64:96, 0:SEQ], rot_b, KR[64:96, 0:SEQ], start=True, stop=True).then_inc(
                    *up(product_ready, (l, "kr_rot")))
                unit = take((l, "wv"), [("w_kvb_v", l * 256, 2, 0, 512, 512)])
                pe.wait_ge(split_low, at(split_low, (l, "kvn", 1)))
                for tb in range(NTB):
                    ps = open_group((l, "vb", tb))
                    token_major(ps, unit, 2, 512, KVNH, KVNL, tb, stride=512).then_inc(
                        *up(product_ready, (l, "vb", tb)))
                given_back((l, "wv"))
                us = attention_units("B", l)
                per_head = T // P

                def project(h, part, g=None):
                    if part == 0:
                        heads_unit[0] = take((l, "wqk", h), [("w_qb", l * 384, 3, h * 96, 96, 96),
                                                             ("w_kvb", l * 256, 2, h * P, P, P, 288)])
                        ps = open_group((l, "q", h), g)
                        channels(ps, heads_unit[0], 3, 0, 96, QNH, QNL, T, stride=96).then_inc(
                            *up(product_ready, (l, "q", h)))
                    elif part == 1:
                        wh, wl = heads_unit[0]
                        ps = open_group((l, "k", h), g)
                        channels(ps, (wh[:, 288:], wl[:, 288:]), 2, 0, P, KVNH, KVNL, NT).then_inc(
                            *up(product_ready, (l, "k", h)))
                        given_back((l, "wqk", h))
                    else:
                        got((l, "q", h))
                        ps = open_group((l, "q_rot", h), g)
                        nc.tensor.matmul(ps[64:96, 0:SEQ], rot_b, QB[h % 2][64:96, 0:SEQ],
                                         start=True, stop=True).then_inc(*up(product_ready, (l, "q_rot", h)))

                def piece(n):
                    h, part = n // per_head + 1, n % per_head
                    if h >= HEADS_B or part > 2:
                        return False
                    project(h, part, 3)
                    return True

                heads_unit = [None]
                for part in range(3):
                    project(0, part)

                def ready(n, what):
                    h = n // per_head
                    if what == "scores" and n % per_head == 0:
                        got((l, "k", h))
                        pe.wait_ge(to_pe, at(to_pe, (l, "qb", h)))
                        if h == 0:
                            pe.wait_ge(to_pe, at(to_pe, (l, "kr")))
                    if what == "values" and n == 0:
                        for tb in range(NTB):
                            got((l, "vb", tb))

                attention("B", l, us,
                          lambda n: QB[us[n][0] % 2][0:96, us[n][1] * P:(us[n][1] + 1) * P],
                          lambda n, s, m: KB[us[n][0] % 2][0:96, s:s + m],
                          lambda n, tb: VB[:, tb, us[n][0] * 64:us[n][0] * 64 + 64],
                          ready, piece)
                merge(l, 1, T)
                for j in range(5):
                    T_j = T if j < 4 else NT
                    if j < 4:
                        col = [IN1["qa"] + j * 64, IN1["qa"] + (j + 4) * 64]
                        unit = take((l, "qa", j), [("w_in", l * DM, KD, col[0], 64, P),
                                                   ("w_in", l * DM, KD, col[1], 64, P, 64)])
                    else:
                        unit = w_in1((l, "qa", j), l, IN1["ka"])
                    ps = open_group((l, "qa", j))
                    channels(ps, unit, KD, 0, P, HH, HL, T_j).then_inc(*up(product_ready, (l, "qa", j)))
                    given_back((l, "qa", j))
                    if j:
                        rotate_a(l, j - 1)
                unit = w_in1((l, "va"), l, IN1["va"])
                for tb in range(NTB):
                    ps = open_group((l, "va", tb))
                    token_major(ps, unit, KD, P, HH, HL, tb).then_inc(*up(product_ready, (l, "va", tb)))
                given_back((l, "va"))
                rotate_a(l, 4)
                us_a = attention_units("A", l)

                def ready_a(n, what):
                    if n == 0 and what == "scores":
                        pe.wait_ge(to_pe, at(to_pe, (l, "qa", 4)))
                    if n == 0 and what == "values":
                        for tb in range(NTB):
                            got((l, "va", tb))

                attention("A", l, us_a,
                          lambda n: QA[head(us_a[n][0]), us_a[n][0] % 4, us_a[n][1] * P:(us_a[n][1] + 1) * P],
                          lambda n, s, m: KA[head(us_a[n][0]), s:s + m],
                          lambda n, tb: VA[:, tb, head(us_a[n][0])],
                          ready_a)
                merge(l, 0, T)
                for j in range(4):
                    for name in ("cc", "uc", "bc"):
                        gemm1(l, name, j, IN1[name] + j * P, T)
                    gemm1(l, "zc", j, IN1["zc"] + j * P, T)
                branch(l, 2, T)
                for m in range(KD):
                    unit = take((l, "wo", m), [("w_o", l * DM, KD, m * P, P, P)])
                    ps = open_group((l, "o", m))
                    channels(ps, unit, KD, 0, P, MH, ML, T, new=None if m else lambda k: (l, "m", k)).then_inc(*up(product_ready, (l, "o", m)))
                    given_back((l, "wo", m))
                norm_sum((l, "post"), ACC, T)

            def rotate_a(l, j):
                got((l, "qa", j))
                ps = open_group((l, "qa_rot", j))
                nc.tensor.matmul(ps[:, 0:SEQ], rot_a, QRAW[j % 2][:, 0:SEQ], start=True, stop=True).then_inc(
                    *up(product_ready, (l, "qa_rot", j)))

            for l in range(DEPTH):
                first_layer(l)
                if stop == ("first", l):
                    break

            def gemm2(l, name, j, col, pieces=None, new=None):
                loads = [("w_in_2", l * DM, KD, col, P, P)] if pieces is None else \
                    [("w_in_2", l * DM, KD, c, 64, P, 64 * i) for i, c in enumerate(pieces)]
                unit = take(("2", l, name, j), loads)
                ps = open_group(("2", l, name, j))
                channels(ps, unit, KD, 0, P, HH2, HL2, SEQ, new=new).then_inc(*up(product_ready, ("2", l, name, j)))
                given_back(("2", l, name, j))

            def values2(l, name, col, width, first=0):
                unit = take(("2", l, name), [("w_in_2", l * DM, KD, col, P, P)])
                for tb in range(NXB):
                    ps = open_group(("2", l, name, tb))
                    token_major(ps, unit, KD, P, HH2, HL2, tb).then_inc(*up(product_ready, ("2", l, name, tb)))
                given_back(("2", l, name))

            def heads2(l, a):
                for j in range(4):
                    if j < 3:
                        gemm2(l, a + "q", j, None, [IN2[a + "q"] + j * 64, IN2[a + "q"] + (j + 3) * 64])
                    else:
                        gemm2(l, a + "q", j, IN2[a + "k"])
                    if j:
                        norm_rotate(l, a, j - 1)
                values2(l, a + "v", IN2[a + "v"], P)
                norm_rotate(l, a, 3)
                us = [(h, qb, 0, SEQ, 0) for h in range(HEADS_2) for qb in range(NXB)]

                def hd(h):
                    return slice(64 * (h // 3), 64 * (h // 3) + 64)

                def ready(n, what):
                    if n == 0 and what == "scores":
                        pe.wait_ge(to_pe, at(to_pe, ("2", l, a, 3)))
                    if n == 0 and what == "values":
                        for tb in range(NXB):
                            got(("2", l, a + "v", tb))

                attention(a, l, us,
                          lambda n: Q2[hd(us[n][0]), us[n][0] % 3, us[n][1] * P:(us[n][1] + 1) * P],
                          lambda n, s, m: K2[hd(us[n][0]), s:s + m],
                          lambda n, tb: V2[:, tb, hd(us[n][0])], ready)
                got((a, l, len(us) - 1, "o"))
                for j in range(3):
                    ps = open_group(("2", l, a + "yT", j))
                    for tb in range(NXB):
                        ins = nc.tensor.transpose(ps[:, tb * P:(tb + 1) * P], Y2[:, tb, j * P:(j + 1) * P], ident)
                    ins.then_inc(*up(product_ready, ("2", l, a + "yT", j)))

            def norm_rotate(l, a, j):
                pe.wait_ge(act_out, at(act_out, ("2", l, a, j, "sq")))
                ps = open_group(("2", l, a, j, "sum"))
                nc.tensor.matmul(ps[:, 0:SEQ], blockones, SS2[j % 2][:, :], start=True, stop=True).then_inc(
                    *up(product_ready, ("2", l, a, j, "sum")))
                if a == "a":
                    pe.wait_ge(to_pe, at(to_pe, ("2", l, a, j, "n")))
                    pe.wait_ge(const2_in, 32)
                    ps = open_group(("2", l, a, j, "rot"))
                    nc.tensor.matmul(ps[:, 0:SEQ], ROT2[:, :], QR2[j % 2][:, :], start=True, stop=True).then_inc(
                        *up(product_ready, ("2", l, a, j, "rot")))

            def recurrence(l):
                for name in ("bff", "bfb"):
                    for j in range(2):
                        gemm2(l, name, j, IN2[name] + j * P,
                              new=None if j or name != "bff" else lambda k: ("2", l, "h", 0, k))
                for j in range(2):
                    gemm2(l, "bq", j, IN2["bq"] + j * P)
                for j in range(2):
                    values2(l, f"bi{j}", IN2["bi"] + j * P, P)
                for j in range(2):
                    gemm2(l, "bg", j, IN2["bg"] + j * P)
                for t in range(2):
                    for d in range(2):
                        for i in range(len(LEVELS)):
                            pe.wait_ge(to_pe, at(to_pe, ("2", l, "qp", t, d, i)))
                            pe.wait_ge(pool_out, at(pool_out, ("2", l, "kp", t, d, i)))
                            qp, kp = QP[i % 2], KP[i % 2]
                            for h in range(2):
                                ps = open_group(("2", l, "lev", t, d, i, h))
                                hs = slice(64 * h, 64 * h + 64)
                                for c in range(NXB):
                                    ins = nc.tensor.matmul(ps[:, c * P:(c + 1) * P], kp[hs, c * P:(c + 1) * P],
                                                           qp[hs, c * P:(c + 1) * P], start=True, stop=True)
                                ins.then_inc(*up(product_ready, ("2", l, "lev", t, d, i, h)))
                        pe.wait_ge(to_pe, at(to_pe, ("2", l, "cross", t, d)))
                        for h in range(2):
                            hs = slice(64 * h, 64 * h + 64)
                            ps = open_group(("2", l, "cross", t, d, h))
                            for n, (q, k, _, _) in enumerate(cross_blocks(d)):
                                ins = nc.tensor.matmul(ps[:, n * P:(n + 1) * P], k[hs, :], q[hs, :],
                                                       start=True, stop=True)
                            ins.then_inc(*up(product_ready, ("2", l, "cross", t, d, h)))
                    for h in range(2):
                        for d in range(2):
                            for i in range(len(LEVELS)):
                                got(("2", l, "lev", t, d, i, h))
                            got(("2", l, "cross", t, d, h))
                        for b in range(4):
                            got(("2", l, "bi0" if t == 0 else "bi1", b))
                        ps = open_group(("2", l, "pv", t, h))
                        cols = slice((2 * t + h) * 64, (2 * t + h) * 64 + 64)
                        for tb in range(NXB):
                            parts = [(DIAG[h][:, d, tb * P:(tb + 1) * P], tb) for d in range(2)]
                            for d in range(2):
                                for n, (_, _, s_c, t_c) in enumerate(cross_blocks(d)):
                                    if t_c == tb:
                                        parts.append((OFF[h][:, d, n * P:(n + 1) * P], s_c))
                            for n, (lhs, s_c) in enumerate(parts):
                                ins = nc.tensor.matmul(ps[:, tb * 64:(tb + 1) * 64], lhs, VH[:, s_c, cols],
                                                       start=n == 0, stop=n == len(parts) - 1)
                        ins.then_inc(*up(product_ready, ("2", l, "pv", t, h)))
                pe.wait_ge(to_pe, at(to_pe, ("2", l, "otok")))
                for j in range(2):
                    ps = open_group(("2", l, "byT", j))
                    for tb in range(NXB):
                        ins = nc.tensor.transpose(ps[:, tb * P:(tb + 1) * P], OTOK[:, tb, j * P:(j + 1) * P], ident)
                    ins.then_inc(*up(product_ready, ("2", l, "byT", j)))

            def mixed_key(l, k):
                return ("2", l, "mix", "aaabbccc"[k], (0, 1, 2, 0, 1, 0, 1, 2)[k])

            def second_layer(l):
                norm_sum(("2", l, "n", 0), ACC2, SEQ)
                recurrence(l)
                heads2(l, "a")
                heads2(l, "c")
                for m in range(KD):
                    unit = take(("2", l, "wout", m), [("w_out_2", l * DM, KD, m * P, P, P)])
                    ps = open_group(("2", l, "out", m))
                    channels(ps, unit, KD, 0, P, XH2, XL2, SEQ, new=None if m else lambda k: mixed_key(l, k)).then_inc(
                        *up(product_ready, ("2", l, "out", m)))
                    given_back(("2", l, "wout", m))
                norm_sum(("2", l, "n", 1), ACC2, SEQ)
                for j in range(KF):
                    for s in range(2):
                        unit = take(("2", l, "up", j, s), [("w_up_2", l * DM, KD, s * DFF + j * P, P, P)])
                        ps = open_group(("2", l, "up", j, s))
                        channels(ps, unit, KD, 0, P, HH2, HL2, SEQ,
                                 new=None if j or s else lambda k: ("2", l, "h", 1, k)).then_inc(
                            *up(product_ready, ("2", l, "up", j, s)))
                        given_back(("2", l, "up", j, s))
                for m in range(KD):
                    ps = open_group(("2", l, "down", m))
                    for i, (k0, kt) in enumerate(((0, 8), (8, 8), (16, 6))):
                        unit = take(("2", l, "down", m, i), [("w_down_2", l * DFF + k0 * P, kt, m * P, P, P)])
                        ins = channels(ps, unit, kt, 0, P, FH, FL, SEQ, k0=k0, first=i == 0, last=i == 2,
                                       new=None if m else lambda k: ("2", l, "f", k))
                        ins.then_inc(*up(product_ready, ("2", l, "down", m, i)))
                        given_back(("2", l, "down", m, i))

            if stop is None or stop[0] == "second":
                for l in range(DEPTH):
                    second_layer(l)
                    if stop == ("second", l):
                        break
            if stop is None:
                for m in range(KD):
                    got(("2", DEPTH - 1, "down", m))
            elif stop[0] == "first":
                pe.wait_ge(dve_step, at(dve_step, (stop[1], "x", KD - 1)))
            else:
                for m in range(KD):
                    got(("2", stop[1], "down", m))
            for tb in range(NXB):
                ps = open_group(("outT", tb))
                for k in range(KD):
                    ins = nc.tensor.transpose(ps[:, k * P:(k + 1) * P], XT[:, k, tb * P:(tb + 1) * P], ident)
                ins.then_inc(*up(product_ready, ("outT", tb)))

        split_units = [i for i, u in enumerate(units) if u[2]]

        def w_index(key):
            n = led.events["unit", key]
            return sum(1 for i in split_units if i <= n) - 1

        @block.sync
        def _(sp):
            sp.dma_start(CONST[:, :], D["const1"][:, 0:800]).then_inc(const_in, 16)
            sp.dma_start(ROPE[:, :], D["const1"][:, 800:800 + 4 * SEQ]).then_inc(const_in, 16)
            sp.dma_start(SINK[:, :], D["sink"].to_broadcast([P, DEPTH * HEADS_A])).then_inc(const_in, 16)
            for s in range(0, NTB, 4):
                src = D["x"].rearrange("(b p) n -> p b n", p=P) if s == 0 else \
                    D["ctx"].rearrange("(b p) n -> p b n", p=P)
                n = src.shape[1]
                sp.dma_start(XIN[:, s:s + n, :], src).then_inc(x_in, 16)
            sp.wait_ge(pool_step, 1)
            for b, batch in enumerate(VECTOR_BATCHES):
                for used, source, start, n in batch:
                    dst = VROWS[used:used + n, b * P:(b + 1) * P]
                    if D[source].shape[1] == 64:
                        sp.dma_start(dst[:, 0:64], D[source][start:start + n, :]).then_inc(vec_in, 16)
                        sp.dma_start(dst[:, 64:P], D[source][start:start + n, :]).then_inc(vec_in, 16)
                    else:
                        sp.dma_start(dst, D[source][start:start + n, :]).then_inc(vec_in, 16)
            for n, (key, loads, split) in enumerate(units):
                if n >= NRAW:
                    if units[n - NRAW][2]:
                        sp.wait_ge(w_low, sum(1 for i in split_units if i <= n - NRAW))
                    else:
                        sp.wait_ge(mod_summed, n - NRAW + 1 - sum(1 for i in split_units if i <= n - NRAW))
                for load in loads:
                    source, row0, kt, col, width, stride = load[:6]
                    off = load[6] if len(load) > 6 else 0
                    dst = RAW[n % NRAW][:, off:off + (kt - 1) * stride + width] if width == stride else \
                        RAW[n % NRAW][:, 0:kt * stride]
                    if width == stride:
                        dst = dst.rearrange("p (k c) -> p k c", k=kt)
                    else:
                        dst = dst.rearrange("p (k c) -> p k c", k=kt)[:, :, off:off + width]
                    if source == "w_kvb_v":
                        for k in range(kt):
                            src = D["w_kvb"][row0 + k * P:row0 + (k + 1) * P, :]
                            src = src.rearrange("p (h c) -> p h c", c=P)[:, :, 64:P]
                            sp.dma_start(dst[:, k, :].rearrange("p (h c) -> p h c", c=64), src).then_inc(
                                loaded[n % NRAW], 16)
                    else:
                        src = D[source][row0:row0 + kt * P, :].rearrange("(k p) n -> p k n", p=P)
                        sp.dma_start(dst, src[:, :, col:col + width]).then_inc(loaded[n % NRAW], 16)
                if key == ("2", 0, "bff", 0):
                    sp.wait_ge(dve_step, at(dve_step, (1, "x", KD - 1)))
                    sp.dma_start(ROT2[:, :], D["const2"][:, 0:P]).then_inc(const2_in, 16)
                    sp.dma_start(ROPE[:, 0:2 * SEQ], D["const2"][:, P:P + 2 * SEQ]).then_inc(const2_in, 16)
                if key[0] == "2" and key[2:] == ("bff", 1):
                    l = key[1]
                    if l == 0:
                        sp.wait_ge(dve_step, at(dve_step, (1, "x", KD - 1)))
                    else:
                        sp.wait_ge(product_ready, led.events[product_ready.name, ("2", 0, "down", KD - 1, 2)])
                    sp.dma_start(HMASK[:, :], D["masks"][:, :]).then_inc(masks_in, 16)
                if key[0] == "2" and key[2:] == ("aq", 0):
                    l = key[1]
                    sp.wait_ge(product_ready, led.events[product_ready.name, ("2", l, "pv", 1, 1)])
                    sp.dma_start(CBIAS[:, :], D["bias"][:, :]).then_inc(bias_in, 16)
            for tb in range(NXB):
                sp.wait_ge(act_out, at(act_out, ("outT", tb)))
                sp.dma_start(out[tb * P:(tb + 1) * P, :], XOUT[:, tb, :]).then_inc(out_done, 16)
            sp.wait_ge(out_done, 16 * NXB)

        raw_count = {}
        for n, (key, loads, split) in enumerate(units):
            raw_count[n] = 16 * n_dmas(loads) + (raw_count[n - NRAW] if n >= NRAW else 0)

        def make_ahead(eng, emit):
            done = [0]

            def ahead(key, by=1):
                upto = min(w_index(key) + by, len(split_units) - 1)
                while done[0] <= upto:
                    emit(done[0])
                    done[0] += 1
            return ahead

        @block.scalar
        def _(act):
            A = nc.scalar.activation

            def split_weights(s):
                n = split_units[s]
                act.wait_ge(loaded[n % NRAW], raw_count[n])
                if s >= NWS:
                    act.wait_ge(product_ready, led.events["unit_used", units[split_units[s - NWS]][0]])
                w = units[n]
                used = used_columns(w)
                A(WH[s % NWS][:, 0:used], RAW[n % NRAW][:, 0:used], ACT.Copy).then_inc(*up(w_high))

            ahead = make_ahead(act, split_weights)

            def ready(key):
                act.wait_ge(product_ready, at(product_ready, key))
                return psum[led.slot(key)]

            def freed(key):
                return up(evacuated[led.slot(key)], key)

            def value_is_there(n_key, source=None):
                if source:
                    act.wait_ge(evacuated[led.slot(source)], at(evacuated[led.slot(source)], source))
                else:
                    act.wait_ge(split_value, at(split_value, n_key))

            def high(n_key, H, T, source=None):
                n = at_split(n_key)
                value_is_there(n_key, source)
                A(H, GV[n % 2][:, 0:T], ACT.Copy).then_inc(*up(split_high, n_key))

            def norm(key, tiles, sq, T, n, rstd_acc, wait=None):
                for i, x in enumerate(tiles):
                    if wait:
                        wait(i)
                    if i >= 2:
                        act.wait_ge(dve_step, at(dve_step, (key, "add", i - 2)))
                    A(sq[i % 2][:, 0:T], x, ACT.Square).then_inc(*up(act_out, (key, "sq", i)))
                root(key, T, n, rstd_acc)

            def root(key, T, n, rstd):
                ps = ready(key)
                A(rstd[:, 0:T], ps[:, 0:T], ACT.Sqrt, bias=epsb[:, 0:1], scale=1.0 / n).then_inc(*freed(key))

            for k in range(KD):
                ps = ready(("xT", k))
                A(XT[:, k, :], ps[:, 0:NT], ACT.Copy).then_inc(*freed(("xT", k)))
            act.wait_ge(dve_step, at(dve_step, "eps"))
            for b in range(len(VECTOR_BATCHES)):
                value_is_there(None, ("vec", b))
            A(CS[:, 0:16], VEC[:, COLUMN["c", 0]:COLUMN["c", 0] + 16], ACT.Silu).then_inc(*up(act_step, "cs"))
            A(CS[:, 16:24], VEC[:, COLUMN["c2", 0]:COLUMN["c2", 0] + 8], ACT.Silu).then_inc(*up(act_out, "silu_c"))
            act.wait_ge(dve_step, at(dve_step, "lb_max"))
            A(LB[:, 8:16], LB[:, 0:8], ACT.Exp).then_inc(*up(act_out, "lb_exp"))

            def head_part(l, h, part, width):
                T = tokens(l)
                if part == 0:
                    ahead((l, "wqk", h))
                    key = (l, "q", h)
                    ps = ready(key)
                    if h >= 2:
                        act.wait_ge(product_ready, at(product_ready, ("B", l, (h - 1) * width - 1, "s")))
                    A(QB[h % 2][0:96, 0:T], ps[0:96, 0:T], ACT.Copy, scale=SCALE_B).then_inc(*freed(key))
                elif part == 1:
                    key = (l, "k", h)
                    ps = ready(key)
                    A(KB[h % 2][0:64, :], ps[0:64, 0:NT], ACT.Copy).then_inc(*freed(key))

            def attention(kind, l, us, width, dve_turns):
                if kind == "B":
                    for part in range(2):
                        head_part(l, 0, part, width)
                N = len(us)
                for n in range(N + 1):
                    if n < N:
                        h, qb, k0, nloc, nctx = us[n]
                        keys = nloc + nctx + (1 if kind == "A" else 0)
                        act.wait_ge(to_act, at(to_act, (kind, l, n)))
                        if n >= 2:
                            act.wait_ge(product_ready, at(product_ready, (kind, l, n - 2, "t")))
                            act.wait_ge(dve_step, at(dve_step, (kind, l, n - 2, "inv")))
                        src = S2[n % 2][:, 0:keys] if kind == "c" else psum[led.slot((kind, l, n, "s"))][:, 0:keys]
                        ins = A(pr_of(kind, n)[:, 0:keys], src, ACT.Exp, bias=nmax[n % 2], accum_out=rowsum[n % 2])
                        ins.then_inc(*(up(probs_ready, (kind, l, n)) if kind == "c" else freed((kind, l, n, "s"))))
                    if kind == "B" and n // width + 1 < HEADS_B and n % width < 2:
                        head_part(l, n // width + 1, n % width, width)
                    if n and (n - 1) % dve_turns[1] >= dve_turns[0]:
                        evac_t(kind, l, us, n - 1)

            def evac_t(kind, l, us, n):
                h, qb, k0, nloc, nctx = us[n]
                keys = nloc + nctx
                key = (kind, l, n, "t")
                ps = ready(key)
                if n >= 2:
                    act.wait_ge(product_ready, at(product_ready, (kind, l, n - 2, "o")))
                A(pt_of(kind, n)[:, 0:keys], ps[:, 0:keys], ACT.Copy).then_inc(*freed(key))

            def merge(l, b, T):
                for j in range(4):
                    z_high(l, b, j, T)
                gates(l, b, T)

            def z_high(l, b, j, T):
                key = (l, Z1[b], j)
                ahead(key)
                ps = ready(key)
                if j >= 2:
                    value_is_there((l, "y", b, j - 2), (l, "yT", b, j - 2) if b < 2 else None)
                A(SZ[j % 2][:, 0:T], ps[:, 0:T], ACT.Silu).then_inc(*freed(key))
                if j < 3 or b == 2:
                    ahead(key, 2)
                high((l, "y", b, j), YH[:, j, 0:T], T, (l, "yT", b, j) if b < 2 else None)

            def gates(l, b, T):
                for m0 in range(0, KD, 2):
                    ahead((l, "wb", b, m0))
                    for m in (m0, m0 + 1):
                        key = (l, f"g{b}", m)
                        ahead(key)
                        ps = ready(key)
                        if m >= 2:
                            old = (l, "br", b, m - 2)
                            act.wait_ge(evacuated[led.slot(old)], at(evacuated[led.slot(old)], old))
                        A(SG[m % 2][:, 0:T], ps[:, 0:T], ACT.Sigmoid).then_inc(*freed(key))
                        ahead(key, 2)
                    if b == 2:
                        for m in (m0, m0 + 1):
                            high((l, "m", m), MH[:, m, 0:T], T)

            def first_layer(l):
                T = tokens(l)
                if l == 0:
                    wait = lambda k: act.wait_ge(evacuated[led.slot(("xT", k))], at(evacuated[led.slot(("xT", k))], ("xT", k)))
                else:
                    wait = lambda k: act.wait_ge(dve_step, at(dve_step, (0, "x", k)))
                norm((l, "pre"), [XT[:, k, :] for k in range(KD)], SQ, NT, DM, RSTD, wait)
                for k in range(KD):
                    high((l, "h", k), HH[:, k, :], NT)
                for j in range(6):
                    name, jj = (("qlb", j), ("kvlb", j - 3), ("krb", 0))[0 if j < 3 else 1 if j < 5 else 2]
                    key = (l, name, jj)
                    Tj = T if j < 3 else NT
                    ahead(key)
                    ps = ready(key)
                    if j < 5:
                        A(QLRAW[:, j, 0:Tj], ps[:, 0:Tj], ACT.Copy).then_inc(*freed(key))
                    else:
                        A(KR[64:96, :], ps[64:96, 0:NT], ACT.Copy).then_inc(*freed(key))
                ahead((l, "wv"), 0)
                own = lambda key: (lambda i: act.wait_ge(evacuated[led.slot((l, key, i))],
                                                         at(evacuated[led.slot((l, key, i))], (l, key, i))))
                norm((l, "qlb"), [QLRAW[:, j, 0:T] for j in range(3)], SQ, T, 384, RSTD, own("qlb"))
                for j in range(3):
                    high((l, "qn", j), QNH[:, j, 0:T], T)
                norm((l, "kvlb"), [QLRAW[:, 3 + j, :] for j in range(2)], SQ, NT, 256, RSTD, own("kvlb"))
                for j in range(2):
                    high((l, "kvn", j), KVNH[:, j, :], NT)
                for tb in range(NTB):
                    key = (l, "vb", tb)
                    if tb == 0:
                        ahead((l, "wv"))
                    ps = ready(key)
                    A(VB[:, tb, :], ps[:, 0:512], ACT.Copy).then_inc(*freed(key))
                attention("B", l, attention_units("B", l), T // P, (1, 2))
                merge(l, 1, T)
                for j in range(5):
                    Tj = T if j < 4 else NT
                    key = (l, "qa", j)
                    ahead(key)
                    ps = ready(key)
                    if j >= 2:
                        act.wait_ge(to_pe, at(to_pe, (l, "qa", j - 2)))
                    A(QRAW[j % 2][:, 0:Tj], ps[:, 0:Tj], ACT.Copy, scale=0.125 if j < 4 else 1.0).then_inc(*freed(key))
                for tb in range(NTB):
                    key = (l, "va", tb)
                    if tb == 0:
                        ahead((l, "va"))
                    ps = ready(key)
                    A(VA[:, tb, :], ps[:, 0:P], ACT.Copy).then_inc(*freed(key))
                attention("A", l, attention_units("A", l), 0, (0, 1))
                merge(l, 0, T)
                for j in range(4):
                    key = (l, "cc", j)
                    ahead(key)
                    ps = ready(key)
                    if j:
                        act.wait_ge(evacuated[led.slot((l, "uc", j - 1))],
                                    at(evacuated[led.slot((l, "uc", j - 1))], (l, "uc", j - 1)))
                    A(CU[:, 0:T], ps[:, 0:T], ACT.Copy).then_inc(*freed(key))
                    ahead((l, "uc", j))
                    ahead((l, "bc", j))
                    z_high(l, 2, j, T)
                gates(l, 2, T)
                for m in range(KD):
                    key = (l, "o", m)
                    ahead((l, "wo", m))
                    ps = ready(key)
                    A(OUT[:, m, 0:T], ps[:, 0:T], ACT.Copy).then_inc(*freed(key))
                norm((l, "post"), [OUT[:, m, 0:T] for m in range(KD)], SQ, T, DM, RSTD,
                     lambda m: act.wait_ge(evacuated[led.slot((l, "o", m))], at(evacuated[led.slot((l, "o", m))], (l, "o", m))))

            for l in range(DEPTH):
                first_layer(l)
                if stop == ("first", l):
                    break

            def norm2(l, i):
                if i == 0:
                    wait = (lambda k: act.wait_ge(dve_step, at(dve_step, (1, "x", k)))) if l == 0 else \
                        (lambda k: value_is_there(None, ("2", 0, "down", k)))
                else:
                    wait = lambda k: value_is_there(None, ("2", l, "out", k))
                norm(("2", l, "n", i), [XT[:, k, 0:SEQ] for k in range(KD)], SQ2, SEQ, DM, RSTD2, wait)
                for k in range(KD):
                    high(("2", l, "h", i, k), HH2[:, k, :], SEQ)

            def heads2(l, a):
                for j in range(4):
                    key = ("2", l, a + "q", j)
                    ahead(key)
                    ps = ready(key)
                    if j >= 2:
                        act.wait_ge(to_pe, at(to_pe, ("2", l, a, j - 2)))
                    A(QR2[j % 2][:, :], ps[:, 0:SEQ], ACT.Copy).then_inc(*freed(key))
                    act.wait_ge(evacuated[led.slot(key)], at(evacuated[led.slot(key)], key))
                    if j >= 2:
                        act.wait_ge(product_ready, at(product_ready, ("2", l, a, j - 2, "sum")))
                    A(SS2[j % 2][:, :], QR2[j % 2][:, :], ACT.Square).then_inc(*up(act_out, ("2", l, a, j, "sq")))
                    if j:
                        root2(l, a, j - 1)
                for tb in range(NXB):
                    key = ("2", l, a + "v", tb)
                    if tb == 0:
                        ahead(("2", l, a + "v"))
                    ps = ready(key)
                    A(V2[:, tb, :], ps[:, 0:P], ACT.Copy).then_inc(*freed(key))
                root2(l, a, 3)
                attention(a, l, [(h, qb, 0, SEQ, 0) for h in range(HEADS_2) for qb in range(NXB)], 0,
                          (0, 1) if a == "c" else (1, 2))
                for j in range(3):
                    high(("2", l, "mix", a, j), XH2[:, (0 if a == "a" else 5) + j, :], SEQ, ("2", l, a + "yT", j))

            def root2(l, a, j):
                key = ("2", l, a, j, "sum")
                if j >= 2:
                    act.wait_ge(to_pe, at(to_pe, ("2", l, a, j - 2)))
                ps = ready(key)
                A(RS2[j % 2][:, :], ps[:, 0:SEQ], ACT.Sqrt, bias=epsb[:, 0:1], scale=1.0 / 64).then_inc(*freed(key))

            def recurrence(l):
                for n in range(4):
                    name, j = (("bff", "bfb")[n // 2], n % 2)
                    key = ("2", l, name, j)
                    ahead(key)
                    ps = ready(key)
                    A(FS[:, n, :], ps[:, 0:SEQ], ACT.Sigmoid).then_inc(*freed(key))
                for j in range(2):
                    key = ("2", l, "bq", j)
                    ahead(key)
                    ps = ready(key)
                    A(QH[:, j, :], ps[:, 0:SEQ], ACT.Copy).then_inc(*freed(key))
                for j in range(2):
                    for tb in range(NXB):
                        key = ("2", l, f"bi{j}", tb)
                        if tb == 0:
                            ahead(("2", l, f"bi{j}"))
                        ps = ready(key)
                        A(VH[:, tb, j * P:(j + 1) * P], ps[:, 0:P], ACT.Copy).then_inc(*freed(key))
                for j in range(2):
                    key = ("2", l, "bg", j)
                    ahead(key)
                    ps = ready(key)
                    A(SZ2[j][:, :], ps[:, 0:SEQ], ACT.Silu).then_inc(*freed(key))
                for n in range(4):
                    act.wait_ge(to_act, at(to_act, ("2", l, "f", n)))
                    A(LF[:, n, :], FS[:, n, :], ACT.Ln).then_inc(*up(act_out, ("2", l, "lf", n)))
                for t in range(2):
                    for d in range(2):
                        n = 2 * d + t
                        for i in range(len(LEVELS)):
                            act.wait_ge(to_act, at(to_act, ("2", l, "dd", t, d, i)))
                            if i == 0:
                                sign = 1.0 if d == 0 else -1.0
                                A(EE[0][:, :], DD[0][:, :], ACT.Exp, scale=sign).then_inc(
                                    *up(act_out, ("2", l, "ee", t, d, "q")))
                                A(EE[1][:, :], DD[0][:, :], ACT.Exp, scale=-sign).then_inc(
                                    *up(act_out, ("2", l, "ee", t, d, 0)))
                            else:
                                e = (i + 1) % 2
                                if i != 2:
                                    act.wait_ge(to_pe, at(to_pe, ("2", l, "qp", t, d, max(i - 2, 0))))
                                if i >= 2:
                                    act.wait_ge(pool_out, at(pool_out, ("2", l, "kp", t, d, i - 2)))
                                A(EE[e][:, :], DD[i % 2][:, :], ACT.Exp, scale=-1.0).then_inc(
                                    *up(act_out, ("2", l, "ee", t, d, i)))
                        act.wait_ge(to_act, at(to_act, ("2", l, "dx", t, d)))
                        A(EE[0][:, :], PREF(n), ACT.Exp).then_inc(*up(act_out, ("2", l, "ex", t, d, 0)))
                        A(EE[1][:, :], DD[1][:, :], ACT.Exp, scale=-1.0).then_inc(*up(act_out, ("2", l, "ex", t, d, 1)))
                        A(EX[:, n, 0:4], SMALL[:, 16 + 4 * n:20 + 4 * n], ACT.Exp).then_inc(
                            *up(act_out, ("2", l, "ex", t, d, 2)))
                act.wait_ge(to_act, at(to_act, ("2", l, "oss")))
                A(smalls[:, 24:40], smalls[:, 24:40], ACT.Sqrt, bias=epsb[:, 0:1], scale=1.0 / 64).then_inc(
                    *up(act_out, ("2", l, "oss")))
                for j in range(2):
                    high(("2", l, "mix", "b", j), XH2[:, 3 + j, :], SEQ, ("2", l, "byT", j))

            def second_layer(l):
                norm2(l, 0)
                recurrence(l)
                heads2(l, "a")
                heads2(l, "c")
                for m in range(KD):
                    ahead(("2", l, "wout", m))
                norm2(l, 1)
                for j in range(KF):
                    for s in range(2):
                        key = ("2", l, "up", j, s)
                        ahead(key)
                        U = (UA, UB)[s]
                        ps = ready(key)
                        if j:
                            act.wait_ge(split_value, at(split_value, ("2", l, "f", j - 1)))
                        c = s * KF + j
                        A(U[:, :], ps[:, 0:SEQ], ACT.Identity, bias=vec("conv_b", l, c),
                          scale=vec("conv2", (l, 1), c)).then_inc(*up(act_out, ("2", l, "u", j, s)))
                    ahead(key, 2)
                    value_is_there(None, ("2", l, "up", j, 0))
                    A(UA[:, :], UA[:, :], ACT.Silu).then_inc(*up(act_out, ("2", l, "silu", j)))
                    high(("2", l, "f", j), FH[:, j, :], SEQ)
                for m in range(KD):
                    for i in range(3):
                        ahead(("2", l, "down", m, i))

            if stop is None or stop[0] == "second":
                for l in range(DEPTH):
                    second_layer(l)
                    if stop == ("second", l):
                        break
            for tb in range(NXB):
                key = ("outT", tb)
                ps = ready(key)
                A(XOUT[:, tb, :], ps[:, 0:DM], ACT.Copy).then_inc(*up(act_out, key))

        @block.gpsimd
        def _(pool):
            def split_weights(s):
                n = split_units[s]
                pool.wait_ge(w_high, s + 1)
                if s >= NWS:
                    pool.wait_ge(product_ready, led.events["unit_used", units[split_units[s - NWS]][0]])
                used = used_columns(units[n])
                nc.gpsimd.tensor_tensor(WL[s % NWS][:, 0:used], RAW[n % NRAW][:, 0:used],
                                        WH[s % NWS][:, 0:used].bitcast(F32), ALU.subtract).then_inc(*up(w_low))

            ahead = make_ahead(pool, split_weights)

            def low(key, L, H, T):
                n = at_split(key)
                pool.wait_ge(split_high, at(split_high, key))
                nc.gpsimd.tensor_tensor(L, GV[n % 2][:, 0:T], H.bitcast(F32), ALU.subtract).then_inc(
                    *up(split_low, key))

            nc.gpsimd.memset(VROWS[:, :], 0.0).then_inc(*up(pool_step))

            def gates(l, b, T):
                for m0 in range(0, KD, 2):
                    ahead((l, "wb", b, m0))
                    ahead((l, f"g{b}", m0))
                    ahead((l, f"g{b}", m0 + 1), 2 if b == 2 else 1)
                    if b == 2:
                        for m in (m0, m0 + 1):
                            low((l, "m", m), ML[:, m, 0:T], MH[:, m, 0:T], T)

            def first_layer(l):
                T = tokens(l)
                for k in range(KD):
                    low((l, "h", k), HL[:, k, :], HH[:, k, :], NT)
                for j in range(3):
                    ahead((l, "qlb", j))
                for j in range(2):
                    ahead((l, "kvlb", j))
                ahead((l, "krb", 0))
                for j in range(3):
                    low((l, "qn", j), QNL[:, j, 0:T], QNH[:, j, 0:T], T)
                for j in range(2):
                    low((l, "kvn", j), KVNL[:, j, :], KVNH[:, j, :], NT)
                ahead((l, "wv"))
                for h in range(HEADS_B):
                    ahead((l, "wqk", h))
                for b in (1, 0):
                    for j in range(4):
                        ahead((l, Z1[b], j), 2 if j < 3 else 1)
                        low((l, "y", b, j), YL[:, j, 0:T], YH[:, j, 0:T], T)
                    gates(l, b, T)
                    if b == 1:
                        for j in range(5):
                            ahead((l, "qa", j))
                        ahead((l, "va"))
                for j in range(4):
                    for name in ("cc", "uc", "bc", "zc"):
                        ahead((l, name, j), 2 if name == "zc" else 1)
                    low((l, "y", 2, j), YL[:, j, 0:T], YH[:, j, 0:T], T)
                gates(l, 2, T)
                for m in range(KD):
                    ahead((l, "wo", m))

            for l in range(DEPTH):
                first_layer(l)
                if stop == ("first", l):
                    break

            def heads2(l, a):
                for j in range(4):
                    ahead(("2", l, a + "q", j))
                ahead(("2", l, a + "v"))
                for j in range(3):
                    c = (0 if a == "a" else 5) + j
                    low(("2", l, "mix", a, j), XL2[:, c, :], XH2[:, c, :], SEQ)

            def recurrence(l):
                for name in ("bff", "bfb", "bq"):
                    for j in range(2):
                        ahead(("2", l, name, j))
                for j in range(2):
                    ahead(("2", l, f"bi{j}"))
                for j in range(2):
                    ahead(("2", l, "bg", j))
                for t in range(2):
                    for d in range(2):
                        n = 2 * d + t
                        for i in range(len(LEVELS)):
                            pool.wait_ge(act_out, at(act_out, ("2", l, "ee", t, d, i)))
                            pool.wait_ge(to_pool, at(to_pool, ("2", l, "kk", n)))
                            prev = (t, d, i - 2, 1) if i >= 2 else None
                            if prev:
                                pool.wait_ge(product_ready, at(product_ready, ("2", l, "lev") + prev))
                            elif (t, d) != (0, 0):
                                td = (t, d - 1) if d else (t - 1, 1)
                                pool.wait_ge(product_ready, at(product_ready, ("2", l, "lev") + td + (4, 1)))
                            nc.gpsimd.tensor_tensor(KP[i % 2][:, :], KK[:, n, :], EE[(i + 1) % 2][:, :],
                                                    ALU.mult).then_inc(*up(pool_out, ("2", l, "kp", t, d, i)))
                for j in range(2):
                    low(("2", l, "mix", "b", j), XL2[:, 3 + j, :], XH2[:, 3 + j, :], SEQ)

            def second_layer(l):
                for k in range(KD):
                    low(("2", l, "h", 0, k), HL2[:, k, :], HH2[:, k, :], SEQ)
                recurrence(l)
                heads2(l, "a")
                heads2(l, "c")
                for m in range(KD):
                    ahead(("2", l, "wout", m))
                for k in range(KD):
                    low(("2", l, "h", 1, k), HL2[:, k, :], HH2[:, k, :], SEQ)
                for j in range(KF):
                    for s in range(2):
                        ahead(("2", l, "up", j, s), 2 if s else 1)
                    low(("2", l, "f", j), FL[:, j, :], FH[:, j, :], SEQ)
                for m in range(KD):
                    for i in range(3):
                        ahead(("2", l, "down", m, i))

            if stop is None or stop[0] == "second":
                for l in range(DEPTH):
                    second_layer(l)
                    if stop == ("second", l):
                        break

        splits = [0]
        split_n = {}

        @block.vector
        def _(dve):
            V = nc.vector

            def ready(key):
                dve.wait_ge(product_ready, at(product_ready, key))
                return psum[led.slot(key)]

            def freed(key):
                return up(evacuated[led.slot(key)], key)

            def own(key):
                dve.wait_ge(evacuated[led.slot(key)], at(evacuated[led.slot(key)], key))

            def step(ins, key=None):
                s, _ = up(dve_step, key)
                ins.then_inc(s, 1)
                dve.wait_ge(s, led.count[s.name])

            def value(key):
                n = splits[0]
                splits[0] += 1
                led.events["split", key] = n
                split_n[n] = key
                if n >= 2:
                    dve.wait_ge(split_low, n - 1)
                return GV[n % 2]

            def valued(key):
                return up(split_value, key)

            def norm(key, tiles, sq, acc, rstd, T):
                for i in range(tiles):
                    dve.wait_ge(act_out, at(act_out, (key, "sq", i)))
                    if i == 0:
                        step(V.tensor_copy(acc[:, 0:T], sq[0][:, 0:T]), (key, "add", 0))
                    elif i < tiles - 1:
                        step(V.tensor_tensor(acc[:, 0:T], acc[:, 0:T], sq[i % 2][:, 0:T], ALU.add), (key, "add", i))
                    else:
                        V.tensor_tensor(acc[:, 0:T], acc[:, 0:T], sq[i % 2][:, 0:T], ALU.add).then_inc(
                            *up(to_pe, key))
                        dve.wait_ge(to_pe, led.count[to_pe.name])
                own(key)
                step(V.reciprocal(rstd[:, 0:T], rstd[:, 0:T]))

            step(V.memset(epsb[:, :], EPS), "eps")
            step(V.memset(SMALL[:, :], 0.0))
            for b in range(len(VECTOR_BATCHES)):
                key = ("vec", b)
                ps = ready(key)
                V.tensor_copy(VEC[:, b * P:(b + 1) * P], ps[:, 0:P]).then_inc(*freed(key))
                own(key)
            raw = VEC[:, COLUMN["b_lb", 0]:COLUMN["b_lb", 0] + 8].rearrange("p (d l t) -> p d l t", d=2, l=2)
            lb = LB[:, 0:8].rearrange("p (d l t) -> p d l t", d=2, l=2)
            ex = LB[:, 8:16].rearrange("p (d l t) -> p d l t", d=2, l=2)
            m4 = LB[:, 16:20].rearrange("p (d t) -> p d t", d=2)
            step(V.tensor_tensor(m4, raw[:, :, 0, :], raw[:, :, 1, :], ALU.max))
            step(V.tensor_tensor(lb[:, :, 0, :], raw[:, :, 0, :], m4, ALU.subtract))
            step(V.tensor_tensor(lb[:, :, 1, :], raw[:, :, 1, :], m4, ALU.subtract), "lb_max")
            dve.wait_ge(act_out, at(act_out, "lb_exp"))
            step(V.tensor_tensor(m4, ex[:, :, 0, :], ex[:, :, 1, :], ALU.add))
            step(V.reciprocal(LB[:, 20:24], LB[:, 16:20]))
            r4 = LB[:, 20:24].rearrange("p (d t) -> p d t", d=2)
            for i in range(2):
                step(V.tensor_tensor(ex[:, :, i, :], ex[:, :, i, :], r4, ALU.mult))
            l0 = LB[:, 24:28].rearrange("p (d t) -> p d t", d=2)
            l1 = LB[:, 28:32].rearrange("p (d t) -> p d t", d=2)
            step(V.tensor_tensor(l0, ex[:, :, 0, :], ex[:, :, 0, :], ALU.subtract))
            step(V.tensor_tensor(m4, ex[:, :, 0, :], ex[:, :, 1, :], ALU.add))
            step(V.tensor_tensor(l1, m4, ex[:, :, 0, :], ALU.subtract))
            dve.wait_ge(const_in, 48)

            def modulation_rows(chunk, rows, slot):
                for k in rows:
                    key = chunk + (k,)
                    n = led.events["unit", key]
                    dve.wait_ge(loaded[n % NRAW], raw_count[n])
                    for v, vector in enumerate(vectors_of(chunk)):
                        total = MSUM[slot + v][:, :]
                        row, c = RAW[n % NRAW][:, :], CS[:, KD * vector + k:KD * vector + k + 1]
                        done = up(mod_summed, key) if v == len(vectors_of(chunk)) - 1 else up(dve_step)
                        if k == 0:
                            V.tensor_scalar(total, row, c, None, ALU.mult).then_inc(*done)
                        else:
                            V.scalar_tensor_tensor(total, row, c, total, ALU.mult, ALU.add).then_inc(*done)
                    dve.wait_ge(dve_step, led.count[dve_step.name])
                    dve.wait_ge(mod_summed, led.count[mod_summed.name])

            def modulation_biases(chunk):
                name, l, c = chunk
                ps = ready(chunk)
                per = CHUNK // P
                for v in range(len(vectors_of(chunk))):
                    dst = MOD1[l][:, c * per:(c + 1) * per, v] if name == "mod1" else \
                        MOD2[l][:, c * per:(c + 1) * per]
                    col = COLUMN["b_mod" if name == "mod1" else "b_ada", l] + c * per
                    ins = V.tensor_tensor(dst, ps[:, v * per:(v + 1) * per], VEC[:, col:col + per], ALU.add)
                    if v == len(vectors_of(chunk)) - 1:
                        ins.then_inc(*freed(chunk))
                    else:
                        ins.then_inc(*up(dve_step))
                own(chunk)
                dve.wait_ge(dve_step, led.count[dve_step.name])

            dve.wait_ge(act_out, at(act_out, "silu_c"))
            for c in range(MOD1_CHUNKS):
                modulation_rows(("mod1", 0, c), range(KD), 2 * (c % 2))
                if c:
                    modulation_biases(("mod1", 0, c - 1))
            modulation_biases(("mod1", 0, MOD1_CHUNKS - 1))

            def attention(kind, l, us, width, dve_turns, y_of):
                if kind == "B":
                    rotate_q(l, 0)
                N = len(us)
                for n in range(N + 2):
                    if n < N:
                        h, qb, k0, nloc, nctx = us[n]
                        keys = nloc + nctx
                        ps = ready((kind, l, n, "s"))
                        if n >= 2:
                            exponentials(dve, kind, l, n - 2)
                        src = ps[:, 0:keys]
                        if kind == "A":
                            if qb < NXB and qb > 0:
                                step(V.tensor_tensor(ps[:, 0:P], ps[:, 0:P], mask_prev, ALU.add))
                            if qb < NXB - 1:
                                step(V.tensor_tensor(ps[:, nloc - P:nloc], ps[:, nloc - P:nloc], mask_next, ALU.add))
                            step(V.tensor_copy(ps[:, keys:keys + 1], SINK[:, l * HEADS_A + h:l * HEADS_A + h + 1]))
                            src = ps[:, 0:keys + 1]
                        elif kind == "c":
                            off = h * 896 + 384 - qb * P
                            V.tensor_tensor(S2[n % 2][:, :], ps[:, 0:SEQ], CBIAS[:, off:off + SEQ], ALU.add).then_inc(
                                *freed((kind, l, n, "s")))
                            own((kind, l, n, "s"))
                            src = S2[n % 2][:, :]
                        V.tensor_reduce(nmax[n % 2], src, AX.X, ALU.max, negate=True).then_inc(*up(to_act, (kind, l, n)))
                    if kind == "B" and n // width + 1 < HEADS_B and n % width == 2:
                        rotate_q(l, n // width + 1)
                    if n >= 4:
                        own((kind, l, n - 4, "o"))
                    if 1 <= n <= N:
                        exponentials(dve, kind, l, n - 1)
                        step(V.reciprocal(rowinv[(n - 1) % 3], rowsum[(n - 1) % 2]), (kind, l, n - 1, "inv"))
                    if n >= 2:
                        m = n - 2
                        key = (kind, l, m, "o")
                        ps = ready(key)
                        V.tensor_scalar(y_of(us[m]), ps[:, 0:64], rowinv[m % 3], None, ALU.mult).then_inc(*freed(key))
                    if 1 <= n <= N and (n - 1) % dve_turns[1] < dve_turns[0]:
                        m = n - 1
                        keys = us[m][3] + us[m][4]
                        key = (kind, l, m, "t")
                        ps = ready(key)
                        if m >= 2:
                            dve.wait_ge(product_ready, at(product_ready, (kind, l, m - 2, "o")))
                        V.tensor_copy(pt_of(kind, m)[:, 0:keys], ps[:, 0:keys]).then_inc(*freed(key))

            def rotate_q(l, h):
                key = (l, "q_rot", h)
                ps = ready(key)
                g = led.slot((l, "q", h))
                dve.wait_ge(evacuated[g], at(evacuated[g], (l, "q", h)))
                step(V.tensor_tensor(T1[64:96, :], ps[64:96, 0:SEQ], sin_b[64:96, :], ALU.mult))
                V.tensor_tensor(QB[h % 2][64:96, 0:SEQ], QB[h % 2][64:96, 0:SEQ], cos_b[64:96, :], ALU.mult).then_inc(
                    *freed(key))
                own(key)
                V.tensor_tensor(QB[h % 2][64:96, 0:SEQ], QB[h % 2][64:96, 0:SEQ], T1[64:96, :], ALU.add).then_inc(
                    *up(to_pe, (l, "qb", h)))
                dve.wait_ge(to_pe, led.count[to_pe.name])

            def rotate_a(l, j):
                T = tokens(l) if j < 4 else NT
                dst = QA[:, j, :] if j < 4 else KA[:, :]
                key = (l, "qa_rot", j)
                ps = ready(key)
                own((l, "qa", j))
                step(V.tensor_tensor(T1a[:, :], ps[:, 0:SEQ], sin_a, ALU.mult))
                V.tensor_tensor(T2a[:, :], QRAW[j % 2][:, 0:SEQ], cos_a, ALU.mult).then_inc(*freed(key))
                own(key)
                if T > SEQ:
                    step(V.tensor_copy(dst[:, SEQ:T], QRAW[j % 2][:, SEQ:T]))
                V.tensor_tensor(dst[:, 0:SEQ], T1a[:, :], T2a[:, :], ALU.add).then_inc(*up(to_pe, (l, "qa", j)))
                dve.wait_ge(to_pe, led.count[to_pe.name])

            def z_gate(l, b, j, T):
                if b < 2:
                    key = (l, "yT", b, j)
                    ps = ready(key)
                    own((l, Z1[b], j))
                    gv = value((l, "y", b, j))
                    V.tensor_tensor(gv[:, 0:T], ps[:, 0:T], SZ[j % 2][:, 0:T], ALU.mult).then_inc(*freed(key))
                    own(key)

            def gates(l, b, T):
                for m in range(KD):
                    chunk = chunk_beside(l, b, m - m % 2)
                    if chunk and m % 2 == 0:
                        modulation_rows(chunk, CHUNK_PARTS[0], 0)
                        modulation_rows(chunk, CHUNK_PARTS[1], 0)
                    elif chunk:
                        modulation_rows(chunk, CHUNK_PARTS[2], 0)
                    key = (l, "br", b, m)
                    ps = ready(key)
                    own((l, f"g{b}", m))
                    first = b == 1
                    if first:
                        V.tensor_tensor(MACC[:, m, 0:T], ps[:, 0:T], SG[m % 2][:, 0:T], ALU.mult).then_inc(*freed(key))
                        own(key)
                    else:
                        V.tensor_tensor(TM[m % 2][:, 0:T], ps[:, 0:T], SG[m % 2][:, 0:T], ALU.mult).then_inc(*freed(key))
                        own(key)
                        if b == 0:
                            step(V.tensor_tensor(MACC[:, m, 0:T], MACC[:, m, 0:T], TM[m % 2][:, 0:T], ALU.add))
                        else:
                            gv = value((l, "m", m))
                            V.tensor_tensor(gv[:, 0:T], MACC[:, m, 0:T], TM[m % 2][:, 0:T], ALU.add).then_inc(
                                *valued((l, "m", m)))
                    if chunk and m % 2:
                        modulation_biases(chunk)

            def first_layer(l):
                T = tokens(l)
                for k in range(KD):
                    V.tensor_scalar(SCG[:, k, :], MOD1[l][:, KD + k, :], 1.0, vec("g_pre", l, k), ALU.add,
                                    ALU.mult).then_inc(*up(dve_step))
                    step(V.tensor_scalar(GG[:, k, :], MOD1[l][:, 2 * KD + k, :], vec("g_post", l, k), None, ALU.mult))
                norm((l, "pre"), KD, SQ, ACC, RSTD, NT)
                if l == 0:
                    for k in range(KD):
                        own(("xT", k))
                for k in range(KD):
                    key = (l, "h", k)
                    gv = value(key)
                    step(V.tensor_tensor(gv[:, :], XT[:, k, :], RSTD[:, :], ALU.mult))
                    for s, (t0, tn) in enumerate(segs(NT)):
                        ins = V.tensor_scalar(gv[:, t0:t0 + tn], gv[:, t0:t0 + tn], SCG[:, k, s:s + 1],
                                              MOD1[l][:, k, s:s + 1], ALU.mult, ALU.add)
                        if s == 0:
                            step(ins)
                    ins.then_inc(*valued(key))
                norm((l, "qlb"), 3, SQ, ACC, RSTD, T)
                for j in range(3):
                    own((l, "qlb", j))
                    gv = value((l, "qn", j))
                    ins = V.scalar_tensor_tensor(gv[:, 0:T], QLRAW[:, j, 0:T], vec("g_qa", l, j), RSTD[:, 0:T],
                                                 ALU.mult, ALU.mult)
                    ins.then_inc(*valued((l, "qn", j)))
                dve.wait_ge(split_value, led.count[split_value.name])
                norm((l, "kvlb"), 2, SQ, ACC, RSTD, NT)
                for j in range(2):
                    own((l, "kvlb", j))
                    gv = value((l, "kvn", j))
                    ins = V.scalar_tensor_tensor(gv[:, :], QLRAW[:, 3 + j, :], vec("g_kva", l, j), RSTD[:, :],
                                                 ALU.mult, ALU.mult)
                    ins.then_inc(*valued((l, "kvn", j)))
                key = (l, "kr_rot")
                own((l, "krb", 0))
                ps = ready(key)
                step(V.tensor_tensor(T1[64:96, :], ps[64:96, 0:SEQ], sin_b[64:96, :], ALU.mult))
                V.tensor_tensor(KR[64:96, 0:SEQ], KR[64:96, 0:SEQ], cos_b[64:96, :], ALU.mult).then_inc(*freed(key))
                own(key)
                step(V.tensor_tensor(KR[64:96, 0:SEQ], KR[64:96, 0:SEQ], T1[64:96, :], ALU.add))
                step(V.tensor_copy(KB[0][64:96, :], KR[64:96, :]))
                V.tensor_copy(KB[1][64:96, :], KR[64:96, :]).then_inc(*up(to_pe, (l, "kr")))
                us = attention_units("B", l)
                attention("B", l, us, T // P, (1, 2), lambda u: YTOK[:, u[1], u[0] * 64:u[0] * 64 + 64])
                for j in range(4):
                    z_gate(l, 1, j, T)
                gates(l, 1, T)
                for j in range(5):
                    rotate_a(l, j)
                us = attention_units("A", l)
                attention("A", l, us, 0, (0, 1), lambda u: YTOK[:, u[1], u[0] * 64:u[0] * 64 + 64])
                for j in range(4):
                    z_gate(l, 0, j, T)
                gates(l, 0, T)
                for j in range(4):
                    ends = [0, SEQ + 1] + ([SEQ + 2, NT + 3] if T == NT else [])
                    for e in ends:
                        step(V.memset(ZP[:, e:e + 1], 0.0))
                    key = (l, "uc", j)
                    ps = ready(key)
                    own((l, "cc", j))
                    spans = [(0, SEQ, 1)] + ([(SEQ, CTX, SEQ + 3)] if T == NT else [])
                    for t0, tn, z0 in spans:
                        ins = V.tensor_tensor(ZP[:, z0:z0 + tn], CU[:, t0:t0 + tn], ps[:, t0:t0 + tn], ALU.mult)
                        if (t0, tn, z0) != spans[-1]:
                            step(ins)
                    ins.then_inc(*freed(key))
                    own(key)
                    for tap in range(3):
                        w = vec("conv1", l, 4 * tap + j)
                        for t0, tn, z0 in spans:
                            z = ZP[:, z0 + tap - 1:z0 + tap - 1 + tn]
                            c = CV[:, t0:t0 + tn]
                            step(V.tensor_scalar(c, z, w, None, ALU.mult) if tap == 0 else
                                 V.scalar_tensor_tensor(c, z, w, c, ALU.mult, ALU.add))
                    key = (l, "bc", j)
                    ps = ready(key)
                    V.tensor_tensor(CV[:, 0:T], CV[:, 0:T], ps[:, 0:T], ALU.mult).then_inc(*freed(key))
                    own(key)
                    own((l, "zc", j))
                    gv = value((l, "y", 2, j))
                    V.tensor_tensor(gv[:, 0:T], CV[:, 0:T], SZ[j % 2][:, 0:T], ALU.mult).then_inc(
                        *valued((l, "y", 2, j)))
                    dve.wait_ge(split_value, led.count[split_value.name])
                gates(l, 2, T)
                norm((l, "post"), KD, SQ, ACC, RSTD, T)
                for m in range(KD):
                    own((l, "o", m))
                    for s, (t0, tn) in enumerate(segs(T)):
                        o = OUT[:, m, t0:t0 + tn]
                        step(V.scalar_tensor_tensor(o, o, GG[:, m, s:s + 1], RSTD[:, t0:t0 + tn], ALU.mult, ALU.mult))
                        x = XT[:, m, t0:t0 + tn]
                        step(V.tensor_tensor(x, x, o, ALU.add), (l, "x", m) if t0 + tn == T else None)

            for l in range(DEPTH):
                first_layer(l)
                if stop == ("first", l):
                    break

            def norm2(l, i):
                norm(("2", l, "n", i), KD, SQ2, ACC2, RSTD2, SEQ)
                for k in range(KD):
                    step(V.tensor_scalar(SC[:, k:k + 1], MOD2[l][:, 24 * i + KD + k:24 * i + KD + k + 1], 1.0,
                                         vec("norm2", l, KD * i + k), ALU.add, ALU.mult))
                for k in range(KD):
                    key = ("2", l, "h", i, k)
                    gv = value(key)
                    step(V.tensor_tensor(gv[:, 0:SEQ], XT[:, k, 0:SEQ], RSTD2[:, :], ALU.mult))
                    V.tensor_scalar(gv[:, 0:SEQ], gv[:, 0:SEQ], SC[:, k:k + 1],
                                    MOD2[l][:, 24 * i + k:24 * i + k + 1], ALU.mult, ALU.add).then_inc(*valued(key))

            def heads2(l, a):
                for j in range(4):
                    dst = Q2[:, j, :] if j < 3 else K2[:, :]
                    gain = vec(f"{a}_q_norm_2" if j < 3 else f"{a}_k_norm_2", l)
                    key = ("2", l, a, j, "sum")
                    own(("2", l, a + "q", j))
                    own(key)
                    rs = RS2[j % 2]
                    step(V.reciprocal(rs[:, :], rs[:, :]))
                    if j < 3:
                        step(V.tensor_scalar(rs[:, :], rs[:, :], 0.125, None, ALU.mult))
                    if a == "a":
                        V.scalar_tensor_tensor(QR2[j % 2][:, :], QR2[j % 2][:, :], gain, rs[:, :], ALU.mult,
                                               ALU.mult).then_inc(*up(to_pe, ("2", l, a, j, "n")))
                        dve.wait_ge(to_pe, led.count[to_pe.name])
                        dve.wait_ge(const2_in, 32)
                        key = ("2", l, a, j, "rot")
                        ps = ready(key)
                        step(V.tensor_tensor(TA2[:, :], QR2[j % 2][:, :], ROPE[:, 0:SEQ], ALU.mult))
                        V.tensor_tensor(TB2[:, :], ps[:, 0:SEQ], ROPE[:, SEQ:2 * SEQ], ALU.mult).then_inc(*freed(key))
                        own(key)
                        V.tensor_tensor(dst, TA2[:, :], TB2[:, :], ALU.add).then_inc(*up(to_pe, ("2", l, a, j)))
                    else:
                        V.scalar_tensor_tensor(dst, QR2[j % 2][:, :], gain, rs[:, :], ALU.mult,
                                               ALU.mult).then_inc(*up(to_pe, ("2", l, a, j)))
                    dve.wait_ge(to_pe, led.count[to_pe.name])
                us = [(h, qb, 0, SEQ, 0) for h in range(HEADS_2) for qb in range(NXB)]
                if a == "c":
                    dve.wait_ge(bias_in, 16 * (l + 1))
                attention(a, l, us, 0, (0, 1) if a == "c" else (1, 2),
                          lambda u: Y2[:, u[1], u[0] * 64:u[0] * 64 + 64])
                for j in range(3):
                    key = ("2", l, a + "yT", j)
                    ps = ready(key)
                    gv = value(("2", l, "mix", a, j))
                    V.tensor_copy(gv[:, 0:SEQ], ps[:, 0:SEQ]).then_inc(*freed(key))
                    own(key)

            def distances(l, t, d, i):
                half = LEVELS[i]
                pref = PREF(2 * d + t).rearrange("p (b w) -> p b w", w=2 * half)
                dd = DD[i % 2][:, :].rearrange("p (b w) -> p b w", w=2 * half)
                r, blocks = half - 1 + d, SEQ // (2 * half)
                if i >= 2:
                    dve.wait_ge(act_out, at(act_out, ("2", l, "ee", t, d, i - 2)))
                if i == 0:
                    V.tensor_tensor(dd, pref, pref[:, :, r:r + 1].to_broadcast([P, blocks, 2 * half]),
                                    ALU.subtract).then_inc(*up(to_act, ("2", l, "dd", t, d, i)))
                else:
                    ref = pref[:, :, r:r + 1].to_broadcast([P, blocks, half])
                    V.tensor_tensor(dd[:, :, 0:half], pref[:, :, 0:half], ref, ALU.subtract).then_inc(*up(to_act))
                    V.tensor_tensor(dd[:, :, half:2 * half], ref, pref[:, :, half:2 * half],
                                    ALU.subtract).then_inc(*up(to_act, ("2", l, "dd", t, d, i)))

            def decayed_queries(l, t, d, i):
                if i == 0:
                    dve.wait_ge(act_out, at(act_out, ("2", l, "ee", t, d, "q")))
                    e = EE[0]
                else:
                    dve.wait_ge(act_out, at(act_out, ("2", l, "ee", t, d, i)))
                    e = EE[(i + 1) % 2]
                own(("2", l, "bq", t))
                if i >= 2:
                    dve.wait_ge(product_ready, at(product_ready, ("2", l, "lev", t, d, i - 2, 1)))
                elif (t, d) != (0, 0):
                    td = (t, d - 1) if d else (t - 1, 1)
                    dve.wait_ge(product_ready, at(product_ready, ("2", l, "lev") + td + (4, 1)))
                V.tensor_tensor(QP[i % 2][:, :], QH[:, t, :], e[:, :], ALU.mult).then_inc(
                    *up(to_pe, ("2", l, "qp", t, d, i)))

            def keep_level(l, t, d, i):
                for h in range(2):
                    key = ("2", l, "lev", t, d, i, h)
                    ps = ready(key)
                    mask = HMASK[:, (5 * d + i) * P:(5 * d + i + 1) * P]
                    mask = mask.rearrange("p (o t) -> p o t", o=1).to_broadcast([P, 4, P])
                    if i:
                        own(("2", l, "lev", t, d, i - 1, h))
                    V.copy_predicated(DIAG[h][:, d, :].rearrange("p (c t) -> p c t", t=P), mask,
                                      ps[:, 0:SEQ].rearrange("p (c t) -> p c t", t=P)).then_inc(*freed(key))

            def recurrence(l):
                step(V.memset(ONE_ROW[:, :], 1.0))
                lbv = LB[:, 24 + 4 * l:28 + 4 * l]
                step(V.tensor_scalar(SMALL[:, 8:12], lbv, -1.0, 1.0, ALU.mult, ALU.add))
                for n in range(4):
                    own(("2", l, ("bff", "bfb")[n // 2], n % 2))
                    f = FS[:, n, :]
                    step(V.tensor_scalar(f, f, SMALL[:, 8 + n:9 + n], lbv[:, n:n + 1], ALU.mult, ALU.add))
                    V.tensor_scalar(f, f, F_MIN, None, ALU.max).then_inc(*up(to_act, ("2", l, "f", n)))
                    dve.wait_ge(to_act, led.count[to_act.name])
                    V.tensor_scalar(KK[:, n, :], f, -1.0, 1.0, ALU.mult, ALU.add).then_inc(*up(to_pool, ("2", l, "kk", n)))
                    dve.wait_ge(to_pool, led.count[to_pool.name])
                for n in range(4):
                    dve.wait_ge(act_out, at(act_out, ("2", l, "lf", n)))
                    for c in range(NXB):
                        cs = slice(c * P, (c + 1) * P)
                        step(V.tensor_tensor_scan(FS[:, n, cs], ONE_ROW[:, :], LF[:, n, cs], 0.0, ALU.mult, ALU.add))
                    ends = FS[:, n, :].rearrange("p (c t) -> p c t", t=P)[:, :, P - 1:P]
                    step(V.tensor_copy(SMALL[:, 16 + 4 * n:20 + 4 * n].rearrange("p (c o) -> p c o", o=1), ends))
                    if n >= 2:
                        step(V.tensor_tensor(FS[:, n, :], FS[:, n, :], LF[:, n, :], ALU.subtract))
                dve.wait_ge(masks_in, 16 * (l + 1))
                for t in range(2):
                    if t:
                        dve.wait_ge(product_ready, at(product_ready, ("2", l, "pv", 0, 1)))
                    for h in range(2):
                        step(V.memset(DIAG[h][:, :, :], 0.0))
                    for d in range(2):
                        n = 2 * d + t
                        distances(l, t, d, 0)
                        for i in range(len(LEVELS)):
                            if i + 1 < len(LEVELS):
                                distances(l, t, d, i + 1)
                            decayed_queries(l, t, d, i)
                            if i:
                                keep_level(l, t, d, i - 1)
                        pref = PREF(n).rearrange("p (c t) -> p c t", t=P)
                        tot = SMALL[:, 16 + 4 * n:20 + 4 * n]
                        end = tot.rearrange("p (c o) -> p c o", o=1).to_broadcast([P, 4, P])
                        dve.wait_ge(pool_out, at(pool_out, ("2", l, "kp", t, d, 4)))
                        V.tensor_tensor(DD[1][:, :].rearrange("p (c t) -> p c t", t=P), pref, end, ALU.subtract).then_inc(
                            *up(to_act, ("2", l, "dx", t, d)))
                        keep_level(l, t, d, len(LEVELS) - 1)
                        dve.wait_ge(act_out, at(act_out, ("2", l, "ex", t, d, 2)))
                        q_e, k_e = (EE[0], EE[1]) if d == 0 else (EE[1], EE[0])
                        q, k = QPX[:, 2 * d, :], QPX[:, 2 * d + 1, :]
                        if (t, d) != (0, 0):
                            td = (t, d - 1) if d else (t - 1, 1)
                            dve.wait_ge(product_ready, at(product_ready, ("2", l, "cross") + td + (1,)))
                        step(V.tensor_tensor(q, QH[:, t, :], q_e[:, :], ALU.mult))
                        step(V.tensor_tensor(k, KK[:, n, :], k_e[:, :], ALU.mult))
                        qc, kc = (3, 0) if d == 0 else (0, 3)
                        q_tot, k_tot = (2, 1) if d == 0 else (1, 2)
                        step(V.tensor_scalar(QX[:, :], q[:, qc * P:(qc + 1) * P], EX[:, n, q_tot:q_tot + 1], None, ALU.mult))
                        V.tensor_scalar(KX[:, :], k[:, kc * P:(kc + 1) * P], EX[:, n, k_tot:k_tot + 1], None,
                                        ALU.mult).then_inc(*up(to_pe, ("2", l, "cross", t, d)))
                        dve.wait_ge(to_pe, led.count[to_pe.name])
                        for h in range(2):
                            key = ("2", l, "cross", t, d, h)
                            ps = ready(key)
                            V.tensor_copy(OFF[h][:, d, :], ps[:, 0:768]).then_inc(*freed(key))
                            own(key)
                    for h in range(2):
                        key = ("2", l, "pv", t, h)
                        ps = ready(key)
                        col = (2 * t + h) * 64
                        V.tensor_copy(OTOK[:, :, col:col + 64], ps[:, 0:256].rearrange("p (b v) -> p b v", v=64)).then_inc(
                            *freed(key))
                        own(key)
                step(V.tensor_tensor(OSQ[:, :], OTOK[:, :, :].rearrange("p b v -> p (b v)"),
                                     OTOK[:, :, :].rearrange("p b v -> p (b v)"), ALU.mult))
                V.tensor_reduce(smalls[:, 24:40], OSQ[:, :].rearrange("p (g v) -> p g v", v=64), AX.X, ALU.add).then_inc(
                    *up(to_act, ("2", l, "oss")))
                dve.wait_ge(act_out, at(act_out, ("2", l, "oss")))
                step(V.reciprocal(smalls[:, 24:40], smalls[:, 24:40]))
                o3 = OTOK[:, :, :].rearrange("p b (h v) -> p (b h) v", v=64)
                V.tensor_tensor(o3, o3, smalls[:, 24:40].rearrange("p (g o) -> p g o", o=1).to_broadcast([P, 16, 64]),
                                ALU.mult).then_inc(*up(to_pe, ("2", l, "otok")))
                for j in range(2):
                    key = ("2", l, "byT", j)
                    ps = ready(key)
                    own(("2", l, "bg", j))
                    gv = value(("2", l, "mix", "b", j))
                    V.scalar_tensor_tensor(gv[:, 0:SEQ], ps[:, 0:SEQ], vec("b_out_norm_2", l), SZ2[j][:, :],
                                           ALU.mult, ALU.mult).then_inc(*freed(key))
                    own(key)

            def second_layer(l):
                norm2(l, 0)
                recurrence(l)
                heads2(l, "a")
                heads2(l, "c")
                for m in range(KD):
                    key = ("2", l, "out", m)
                    ps = ready(key)
                    x = XT[:, m, 0:SEQ]
                    V.scalar_tensor_tensor(x, ps[:, 0:SEQ], MOD2[l][:, 16 + m:17 + m], x, ALU.mult, ALU.add).then_inc(
                        *freed(key))
                    own(key)
                norm2(l, 1)
                for j in range(KF):
                    for s in range(2):
                        key = ("2", l, "up", j, s)
                        U = (UA, UB)[s]
                        c = s * KF + j
                        dve.wait_ge(act_out, at(act_out, ("2", l, "u", j, s)))
                        ps = psum[led.slot(key)]
                        step(V.scalar_tensor_tensor(U[:, 1:SEQ], ps[:, 0:SEQ - 1], vec("conv2", (l, 0), c), U[:, 1:SEQ],
                                                    ALU.mult, ALU.add))
                        V.scalar_tensor_tensor(U[:, 0:SEQ - 1], ps[:, 1:SEQ], vec("conv2", (l, 2), c), U[:, 0:SEQ - 1],
                                               ALU.mult, ALU.add).then_inc(*freed(key))
                        own(key)
                    dve.wait_ge(act_out, at(act_out, ("2", l, "silu", j)))
                    gv = value(("2", l, "f", j))
                    V.tensor_tensor(gv[:, 0:SEQ], UA[:, :], UB[:, :], ALU.mult).then_inc(*valued(("2", l, "f", j)))
                    dve.wait_ge(split_value, led.count[split_value.name])
                for m in range(KD):
                    key = ("2", l, "down", m)
                    dve.wait_ge(product_ready, at(product_ready, ("2", l, "down", m, 2)))
                    ps = psum[led.slot(key)]
                    x = XT[:, m, 0:SEQ]
                    V.scalar_tensor_tensor(x, ps[:, 0:SEQ], MOD2[l][:, 40 + m:41 + m], x, ALU.mult, ALU.add).then_inc(
                        *freed(key))
                    own(key)

            if stop is None or stop[0] == "second":
                for l in range(DEPTH):
                    second_layer(l)
                    if stop == ("second", l):
                        break
    return led.events


LAYOUT = dict(
    x=(SEQ, DM), ctx=(CTX, DM), sink=(1, DEPTH * HEADS_A),
    c=(8, P), c_ctx=(8, P), c_2=(8, P), b_lb_2=(8, P),
    b_mod=(48, P), g_pre=(16, P), g_post=(16, P), g_qa=(6, P), g_kva=(4, P), conv_w=(24, P),
    b_ada_2=(96, P), norm_g_2=(32, P), conv_b_2=(88, P), conv_w_2=(264, P),
    a_q_norm_2=(2, 64), a_k_norm_2=(2, 64), b_out_norm_2=(2, 64), c_q_norm_2=(2, 64), c_k_norm_2=(2, 64),
    w_mod=(DEPTH * DM, 3 * DM), w_in=(DEPTH * DM, 7584), w_qb=(DEPTH * 384, 768), w_kvb=(DEPTH * 256, 1024),
    w_branch=(DEPTH * 3 * 512, DM), w_o=(DEPTH * DM, DM), w_ada_2=(DEPTH * DM, 6 * DM),
    w_in_2=(DEPTH * DM, 2560), w_out_2=(DEPTH * DM, DM), w_up_2=(DEPTH * DM, 2 * DFF), w_down_2=(DEPTH * DFF, DM),
)

STOP = None


def kernel(**inputs):
    import concourse.bacc as bacc
    from concourse.bass_utils import run_bass_kernel_spmd as run

    arrays = {f"in_{k}": np.ascontiguousarray(np.asarray(inputs[k]).reshape(shape)) for k, shape in LAYOUT.items()}
    for k, a in zip(("const1", "const2", "bias", "masks"), constants()):
        arrays[f"in_{k}"] = a

    def build(known):
        nc = bacc.Bacc("TRN2", target_bir_lowering=False, num_devices=1)
        D = {k[3:]: nc.dram_tensor(k, a.shape, mybir.dt.from_np(a.dtype), kind="ExternalInput").ap()
             for k, a in arrays.items()}
        out = nc.dram_tensor("out", (SEQ, DM), F32, kind="ExternalOutput").ap()
        return nc, program(nc, D, out, known, STOP)

    _, counts = build({})
    nc, _ = build(counts)
    r = run(nc, [arrays], core_ids=[0])
    return np.asarray(r.results[0]["out"]).reshape(1, SEQ, DM)
```
